# Optimizing a Trainium2 kernel written in Bass

```python
import math
import jax, jax.numpy as jnp
from jax import lax
import numpy as np

D_MODEL = 1024
BATCH = 1
SEQ = 512
DEPTH = 2
DEC_BATCH = 1
DEC_SEQ = 64
PAST_LEN = 1024

CHUNK = 64
N_RS_LAYERS = (DEPTH + 1) // 2
N_ML_LAYERS = DEPTH // 2
RET_HEADS = 4
RET_DK = 128
RET_DV = 128
RET_QK = RET_HEADS * RET_DK
RET_WIDTH = RET_HEADS * RET_DV
S5_WIDTH = D_MODEL - RET_WIDTH
S5_GROUP = 16
S5_GROUPS = S5_WIDTH // S5_GROUP
S5_STATE = 64
RS_IN = 2 * RET_QK + 2 * RET_WIDTH + S5_WIDTH
ML_HEADS = 4
ML_INNER = 2 * D_MODEL
ML_DH = ML_INNER // ML_HEADS
ML_CONV = 4
MEM_LEN = 256
X_HEADS = 4
X_DH = D_MODEL // X_HEADS
D_FF = 4 * D_MODEL
ROPE_BASE = 10000.0
EPS = 1e-6

kernel_name = 'hybrid_streaming_encoder_step'

def rmsnorm(x, g):
    xf = x.astype(jnp.float32)
    y = xf * lax.rsqrt(jnp.mean(xf * xf, axis=-1, keepdims=True) + EPS)
    return (y * g.astype(jnp.float32)).astype(x.dtype)

def head_layernorm(x, g):
    xf = x.astype(jnp.float32)
    mu = jnp.mean(xf, axis=-1, keepdims=True)
    var = jnp.mean(jnp.square(xf - mu), axis=-1, keepdims=True)
    y = (xf - mu) * lax.rsqrt(var + EPS)
    return y.reshape(*x.shape[:-2], -1) * g.astype(jnp.float32)

def rope(x, pos):
    half = x.shape[-1] // 2
    inv = ROPE_BASE ** (-jnp.arange(half, dtype=jnp.float32) / half)
    ang = pos.astype(jnp.float32)[:, None] * inv[None, :]
    cos = jnp.cos(ang)[None, :, None, :]
    sin = jnp.sin(ang)[None, :, None, :]
    xf = x.astype(jnp.float32)
    x1, x2 = xf[..., :half], xf[..., half:]
    return jnp.concatenate([x1 * cos - x2 * sin, x1 * sin + x2 * cos], axis=-1)

def retention(q, k, v, s0):
    bsz, L, H, _ = q.shape
    c = min(CHUNK, L)
    n = L // c
    log_g = jnp.log1p(-jnp.exp2(-5.0 - jnp.arange(H, dtype=jnp.float32)))
    idx = jnp.arange(c, dtype=jnp.float32)
    diff = idx[:, None] - idx[None, :]
    decay = jnp.where(diff[None] >= 0, jnp.exp(jnp.maximum(diff, 0.0)[None] * log_g[:, None, None]), 0.0)
    qc = q.reshape(bsz, n, c, H, -1)
    kc = k.reshape(bsz, n, c, H, -1)
    vc = v.reshape(bsz, n, c, H, -1)
    scores = jnp.einsum('bnihd,bnjhd->bnhij', qc, kc) * decay[None, None]
    inner = jnp.einsum('bnhij,bnjhe->bnihe', scores, vc)
    w_kv = jnp.exp((c - 1.0 - idx)[:, None] * log_g[None, :])
    kv = jnp.einsum('bnjhd,bnjhe->nbhde', kc * w_kv[None, None, :, :, None], vc)
    g_c = jnp.exp(c * log_g)[None, :, None, None]

    def step(s, kv_n):
        return g_c * s + kv_n, s

    s_final, s_prev = lax.scan(step, s0, kv)
    w_q = jnp.exp((idx + 1.0)[:, None] * log_g[None, :])
    cross = jnp.einsum('bnihd,nbhde->bnihe', qc, s_prev) * w_q[None, None, :, :, None]
    return (inner + cross).reshape(bsz, L, H, -1), s_final

def _complex_affine_combine(e1, e2):
    ar1, ai1, br1, bi1 = e1
    ar2, ai2, br2, bi2 = e2
    return (ar2 * ar1 - ai2 * ai1, ar2 * ai1 + ai2 * ar1,
            ar2 * br1 - ai2 * bi1 + br2, ar2 * bi1 + ai2 * br1 + bi2)

def s5_layer(u, h0_re, h0_im, a_re, a_im, log_dt, b_re, b_im, c_re, c_im, d_skip, w_glu, b_glu):
    to32 = lambda t: t.astype(jnp.float32)
    a_re, a_im, b_re, b_im, c_re, c_im = map(to32, (a_re, a_im, b_re, b_im, c_re, c_im))
    bsz, L, _ = u.shape
    dt = jnp.exp(to32(log_dt))[:, None]
    mag = jnp.exp(a_re * dt)
    ab_re = mag * jnp.cos(a_im * dt)
    ab_im = mag * jnp.sin(a_im * dt)
    den = a_re * a_re + a_im * a_im
    x_re = ab_re - 1.0
    f_re = (x_re * a_re + ab_im * a_im) / den
    f_im = (ab_im * a_re - x_re * a_im) / den
    bb_re = f_re[..., None] * b_re - f_im[..., None] * b_im
    bb_im = f_re[..., None] * b_im + f_im[..., None] * b_re
    ug = u.reshape(bsz, L, S5_GROUPS, S5_GROUP)
    bu_re = jnp.einsum('blgc,gpc->blgp', ug, bb_re)
    bu_im = jnp.einsum('blgc,gpc->blgp', ug, bb_im)
    h0_re = to32(h0_re)
    h0_im = to32(h0_im)
    bu_re = bu_re.at[:, 0].add(ab_re * h0_re - ab_im * h0_im)
    bu_im = bu_im.at[:, 0].add(ab_re * h0_im + ab_im * h0_re)
    shape = (1, L, S5_GROUPS, S5_STATE)
    _, _, h_re, h_im = lax.associative_scan(
        _complex_affine_combine,
        (jnp.broadcast_to(ab_re, shape), jnp.broadcast_to(ab_im, shape), bu_re, bu_im), axis=1)
    y = jnp.einsum('blgp,gcp->blgc', h_re, c_re) - jnp.einsum('blgp,gcp->blgc', h_im, c_im)
    y = y.reshape(bsz, L, S5_WIDTH) + to32(d_skip) * u
    y = jax.nn.gelu(y)
    y = y * jax.nn.sigmoid(y @ to32(w_glu) + to32(b_glu))
    return y, h_re[:, -1], h_im[:, -1]

def ret_s5_block(xn, pos, s_ret, h_re, h_im, w_in, w_out, ret_gn, a_re, a_im, log_dt,
                 b_re, b_im, c_re, c_im, d_skip, w_glu, b_glu):
    bsz, L, _ = xn.shape
    proj = xn @ w_in
    q, k, v, g, u = jnp.split(proj, [RET_QK, 2 * RET_QK, 2 * RET_QK + RET_WIDTH,
                                     2 * RET_QK + 2 * RET_WIDTH], axis=-1)
    q = rope(q.reshape(bsz, L, RET_HEADS, RET_DK), pos)
    k = rope(k.reshape(bsz, L, RET_HEADS, RET_DK), pos) * (RET_DK ** -0.5)
    v = v.reshape(bsz, L, RET_HEADS, RET_DV).astype(jnp.float32)
    o_ret, s_new = retention(q, k, v, s_ret.astype(jnp.float32))
    y_ret = jax.nn.silu(g.astype(jnp.float32)) * head_layernorm(o_ret, ret_gn)
    y_s5, hr, hi = s5_layer(u.astype(jnp.float32), h_re, h_im, a_re, a_im, log_dt,
                            b_re, b_im, c_re, c_im, d_skip, w_glu, b_glu)
    y = jnp.concatenate([y_ret, y_s5], axis=-1).astype(xn.dtype) @ w_out
    return y, s_new, hr, hi

def mlstm_cell(q, k, v, ig, lf, c0, n0, m0):
    bsz, L, H, d = q.shape
    c = min(CHUNK, L)
    n = L // c
    causal = jnp.tril(jnp.ones((c, c), dtype=bool))

    def to_chunks(t):
        return jnp.swapaxes(t.reshape(bsz, n, c, *t.shape[2:]), 0, 1)

    def step(carry, xs):
        cm, nv, m = carry
        qc, kc, vc, igc, lfc = xs
        b = jnp.cumsum(lfc, axis=1).transpose(0, 2, 1)
        i_h = igc.transpose(0, 2, 1)
        dlog = b[..., :, None] - b[..., None, :] + i_h[..., None, :]
        dlog = jnp.where(causal, dlog, -jnp.inf)
        inter = b + m[..., None]
        m_t = jnp.maximum(inter, jnp.max(dlog, axis=-1))
        w = jnp.exp(dlog - m_t[..., None])
        s_inter = jnp.exp(inter - m_t)
        qk = jnp.einsum('bthd,bshd->bhts', qc, kc) * w
        num = s_inter[..., None] * jnp.einsum('bthd,bhde->bhte', qc, cm) + jnp.einsum('bhts,bshe->bhte', qk, vc)
        den = s_inter * jnp.einsum('bthd,bhd->bht', qc, nv) + jnp.sum(qk, axis=-1)
        h = num / jnp.maximum(jnp.abs(den), jnp.exp(-m_t))[..., None]
        m_new = m_t[..., -1]
        w_s = jnp.exp(b[..., -1:] - b + i_h - m_new[..., None])
        dec = jnp.exp(b[..., -1] + m - m_new)
        kw = kc * w_s.transpose(0, 2, 1)[..., None]
        c_new = dec[..., None, None] * cm + jnp.einsum('bshd,bshe->bhde', kw, vc)
        n_new = dec[..., None] * nv + jnp.sum(kw, axis=1)
        return (c_new, n_new, m_new), h.transpose(0, 2, 1, 3)

    (cf, nf, mf), hs = lax.scan(step, (c0, n0, m0),
                                (to_chunks(q), to_chunks(k), to_chunks(v), to_chunks(ig), to_chunks(lf)))
    return jnp.swapaxes(hs, 0, 1).reshape(bsz, L, H, d), cf, nf, mf

def mlstm_block(xn, conv_state, c0, n0, m0, w_in, conv_w, conv_b, wq, wk, wv,
                w_gates, b_gates, gn, skip, w_out):
    bsz, L, _ = xn.shape
    proj = xn @ w_in
    xm, z = jnp.split(proj, 2, axis=-1)
    xp = jnp.concatenate([conv_state.astype(xm.dtype), xm], axis=1)
    xc = conv_b + sum(xp[:, j:j + L] * conv_w[j] for j in range(ML_CONV))
    xc = jax.nn.silu(xc)
    new_conv = xp[:, L:]
    xch = xc.reshape(bsz, L, ML_HEADS, ML_DH)
    xmh = xm.reshape(bsz, L, ML_HEADS, ML_DH)
    q = jnp.einsum('blhd,hde->blhe', xch, wq)
    k = jnp.einsum('blhd,hde->blhe', xch, wk)
    v = jnp.einsum('blhd,hde->blhe', xmh, wv)
    qkv = jnp.concatenate([q.reshape(bsz, L, -1), k.reshape(bsz, L, -1), v.reshape(bsz, L, -1)], axis=-1)
    gates = (qkv @ w_gates + b_gates).astype(jnp.float32)
    ig, fg = jnp.split(gates, 2, axis=-1)
    lf = jax.nn.log_sigmoid(fg)
    f32 = jnp.float32
    h, cf, nf, mf = mlstm_cell(q.astype(f32), k.astype(f32) * (ML_DH ** -0.5), v.astype(f32), ig, lf,
                               c0.astype(f32), n0.astype(f32), m0.astype(f32))
    o = jax.nn.sigmoid(z.astype(f32)).reshape(bsz, L, ML_HEADS, ML_DH)
    y = head_layernorm(o * h, gn) + skip.astype(f32) * xc.astype(f32)
    return y.astype(xn.dtype) @ w_out, cf, nf, mf, new_conv

def memory_kv(mem, g, wk, wv):
    mn = rmsnorm(mem, g)
    bsz, m_len, _ = mem.shape
    return ((mn @ wk).reshape(bsz, m_len, X_HEADS, X_DH),
            (mn @ wv).reshape(bsz, m_len, X_HEADS, X_DH))

def cross_attend(xn, k, v, wq, wo):
    bsz, L, _ = xn.shape
    q = (xn @ wq).reshape(bsz, L, X_HEADS, X_DH)
    s = jnp.einsum('blhd,bmhd->bhlm', q, k).astype(jnp.float32) * (X_DH ** -0.5)
    p = jax.nn.softmax(s, axis=-1).astype(v.dtype)
    o = jnp.einsum('bhlm,bmhd->blhd', p, v).reshape(bsz, L, D_MODEL)
    return o @ wo

def squared_relu_mlp(xn, w_up, w_down):
    h = jax.nn.relu(xn @ w_up)
    return (h * h) @ w_down

def trunk(x, pos0, st_ret, st_re, st_im, st_c, st_n, st_m, st_conv, mem_k, mem_v, p):
    L = x.shape[1]
    pos = pos0 + jnp.arange(L, dtype=jnp.int32)
    o_ret, o_re, o_im, o_c, o_n, o_m, o_conv = [], [], [], [], [], [], []
    for l in range(DEPTH):
        j = l // 2
        xn = rmsnorm(x, p['norm_mix'][l])
        if l % 2 == 0:
            y, s_new, hr, hi = ret_s5_block(
                xn, pos, st_ret[j], st_re[j], st_im[j], p['rs_w_in'][j], p['rs_w_out'][j], p['ret_gn'][j],
                p['s5_a_re'][j], p['s5_a_im'][j], p['s5_log_dt'][j], p['s5_b_re'][j], p['s5_b_im'][j],
                p['s5_c_re'][j], p['s5_c_im'][j], p['s5_d'][j], p['s5_w_glu'][j], p['s5_b_glu'][j])
            o_ret.append(s_new)
            o_re.append(hr)
            o_im.append(hi)
        else:
            y, cf, nf, mf, cv = mlstm_block(
                xn, st_conv[j], st_c[j], st_n[j], st_m[j], p['ml_w_in'][j], p['ml_conv_w'][j], p['ml_conv_b'][j],
                p['ml_wq'][j], p['ml_wk'][j], p['ml_wv'][j], p['ml_w_gates'][j], p['ml_b_gates'][j],
                p['ml_gn'][j], p['ml_skip'][j], p['ml_w_out'][j])
            o_c.append(cf)
            o_n.append(nf)
            o_m.append(mf)
            o_conv.append(cv)
        x = x + y.astype(x.dtype)
        x = x + cross_attend(rmsnorm(x, p['norm_cross'][l]), mem_k[l], mem_v[l], p['x_wq'][l], p['x_wo'][l])
        x = x + squared_relu_mlp(rmsnorm(x, p['norm_mlp'][l]), p['mlp_w_up'][l], p['mlp_w_down'][l])
    y = rmsnorm(x, p['norm_final'])
    stk = lambda t: jnp.stack(t).astype(x.dtype)
    return (y, stk(o_ret), stk(o_re), stk(o_im), stk(o_c), stk(o_n), stk(o_m), stk(o_conv))

def setup_inputs(seed: int = 0) -> dict:
    key = jax.random.key(seed)
    keys = iter(jax.random.split(key, 64))
    f32 = jnp.float32

    def nrm(shape, scale=1.0):
        return scale * jax.random.normal(next(keys), shape, f32)

    def gain(shape):
        return 1.0 + nrm(shape, 0.02)

    d = D_MODEL
    ne, no = N_RS_LAYERS, N_ML_LAYERS
    inp = {}
    inp['x_prompt'] = nrm((BATCH, SEQ, d))
    inp['x_sample'] = nrm((DEC_BATCH, DEC_SEQ, d))
    inp['mem_prompt'] = nrm((BATCH, MEM_LEN, d))
    inp['state_ret'] = nrm((ne, DEC_BATCH, RET_HEADS, RET_DK, RET_DV), 0.3)
    inp['state_s5_re'] = nrm((ne, DEC_BATCH, S5_GROUPS, S5_STATE), 0.3)
    inp['state_s5_im'] = nrm((ne, DEC_BATCH, S5_GROUPS, S5_STATE), 0.3)
    inp['state_mlstm_c'] = nrm((no, DEC_BATCH, ML_HEADS, ML_DH, ML_DH), 0.05)
    inp['state_mlstm_n'] = nrm((no, DEC_BATCH, ML_HEADS, ML_DH), 0.1)
    inp['state_mlstm_m'] = nrm((no, DEC_BATCH, ML_HEADS), 1.0)
    inp['cache_mlstm_conv'] = nrm((no, DEC_BATCH, ML_CONV - 1, ML_INNER))
    inp['cache_mem_k'] = nrm((DEPTH, DEC_BATCH, MEM_LEN, X_HEADS, X_DH))
    inp['cache_mem_v'] = nrm((DEPTH, DEC_BATCH, MEM_LEN, X_HEADS, X_DH))
    inp['norm_mix'] = gain((DEPTH, d))
    inp['norm_cross'] = gain((DEPTH, d))
    inp['norm_mem'] = gain((DEPTH, d))
    inp['norm_mlp'] = gain((DEPTH, d))
    inp['norm_final'] = gain((d,))
    inp['rs_w_in'] = nrm((ne, d, RS_IN), d ** -0.5)
    inp['rs_w_out'] = nrm((ne, RET_WIDTH + S5_WIDTH, d), 0.5 * (RET_WIDTH + S5_WIDTH) ** -0.5)
    inp['ret_gn'] = gain((ne, RET_WIDTH))
    inp['s5_a_re'] = -0.5 + nrm((ne, S5_GROUPS, S5_STATE), 0.01)
    inp['s5_a_im'] = jnp.pi * jnp.arange(S5_STATE, dtype=f32)[None, None, :] + nrm((ne, S5_GROUPS, S5_STATE), 0.01)
    inp['s5_log_dt'] = jax.random.uniform(next(keys), (ne, S5_GROUPS), f32, math.log(1e-3), math.log(1e-1))
    inp['s5_b_re'] = nrm((ne, S5_GROUPS, S5_STATE, S5_GROUP), (2.0 * S5_GROUP) ** -0.5)
    inp['s5_b_im'] = nrm((ne, S5_GROUPS, S5_STATE, S5_GROUP), (2.0 * S5_GROUP) ** -0.5)
    inp['s5_c_re'] = nrm((ne, S5_GROUPS, S5_GROUP, S5_STATE), (2.0 * S5_STATE) ** -0.5)
    inp['s5_c_im'] = nrm((ne, S5_GROUPS, S5_GROUP, S5_STATE), (2.0 * S5_STATE) ** -0.5)
    inp['s5_d'] = nrm((ne, S5_WIDTH), 1.0)
    inp['s5_w_glu'] = nrm((ne, S5_WIDTH, S5_WIDTH), S5_WIDTH ** -0.5)
    inp['s5_b_glu'] = nrm((ne, S5_WIDTH), 0.02)
    inp['ml_w_in'] = nrm((no, d, 2 * ML_INNER), d ** -0.5)
    inp['ml_conv_w'] = nrm((no, ML_CONV, ML_INNER), ML_CONV ** -0.5)
    inp['ml_conv_b'] = nrm((no, ML_INNER), 0.02)
    inp['ml_wq'] = nrm((no, ML_HEADS, ML_DH, ML_DH), ML_DH ** -0.5)
    inp['ml_wk'] = nrm((no, ML_HEADS, ML_DH, ML_DH), ML_DH ** -0.5)
    inp['ml_wv'] = nrm((no, ML_HEADS, ML_DH, ML_DH), ML_DH ** -0.5)
    inp['ml_w_gates'] = nrm((no, 3 * ML_INNER, 2 * ML_HEADS), 0.5 * (3 * ML_INNER) ** -0.5)
    f_bias = jnp.linspace(3.0, 6.0, ML_HEADS, dtype=f32)[None, :] + nrm((no, ML_HEADS), 0.01)
    inp['ml_b_gates'] = jnp.concatenate([nrm((no, ML_HEADS), 0.1), f_bias], axis=-1)
    inp['ml_gn'] = gain((no, ML_INNER))
    inp['ml_skip'] = gain((no, ML_INNER))
    inp['ml_w_out'] = nrm((no, ML_INNER, d), 0.5 * ML_INNER ** -0.5)
    inp['x_wq'] = nrm((DEPTH, d, d), d ** -0.5)
    inp['x_wk'] = nrm((DEPTH, d, d), d ** -0.5)
    inp['x_wv'] = nrm((DEPTH, d, d), d ** -0.5)
    inp['x_wo'] = nrm((DEPTH, d, d), 0.5 * d ** -0.5)
    inp['mlp_w_up'] = nrm((DEPTH, d, D_FF), d ** -0.5)
    inp['mlp_w_down'] = nrm((DEPTH, D_FF, d), 0.5 * D_FF ** -0.5)
    return inp

def reference(x_prompt, x_sample, mem_prompt, state_ret, state_s5_re, state_s5_im, state_mlstm_c,
              state_mlstm_n, state_mlstm_m, cache_mlstm_conv, cache_mem_k, cache_mem_v,
              norm_mix, norm_cross, norm_mem, norm_mlp, norm_final,
              rs_w_in, rs_w_out, ret_gn, s5_a_re, s5_a_im, s5_log_dt, s5_b_re, s5_b_im, s5_c_re, s5_c_im,
              s5_d, s5_w_glu, s5_b_glu,
              ml_w_in, ml_conv_w, ml_conv_b, ml_wq, ml_wk, ml_wv, ml_w_gates, ml_b_gates, ml_gn, ml_skip, ml_w_out,
              x_wq, x_wk, x_wv, x_wo, mlp_w_up, mlp_w_down):
    p = {'norm_mix': norm_mix, 'norm_cross': norm_cross, 'norm_mlp': norm_mlp, 'norm_final': norm_final,
         'rs_w_in': rs_w_in, 'rs_w_out': rs_w_out, 'ret_gn': ret_gn,
         's5_a_re': s5_a_re, 's5_a_im': s5_a_im, 's5_log_dt': s5_log_dt, 's5_b_re': s5_b_re, 's5_b_im': s5_b_im,
         's5_c_re': s5_c_re, 's5_c_im': s5_c_im, 's5_d': s5_d, 's5_w_glu': s5_w_glu, 's5_b_glu': s5_b_glu,
         'ml_w_in': ml_w_in, 'ml_conv_w': ml_conv_w, 'ml_conv_b': ml_conv_b, 'ml_wq': ml_wq, 'ml_wk': ml_wk,
         'ml_wv': ml_wv, 'ml_w_gates': ml_w_gates, 'ml_b_gates': ml_b_gates, 'ml_gn': ml_gn, 'ml_skip': ml_skip,
         'ml_w_out': ml_w_out, 'x_wq': x_wq, 'x_wo': x_wo, 'mlp_w_up': mlp_w_up, 'mlp_w_down': mlp_w_down}
    bp = x_prompt.shape[0]
    f32 = jnp.float32
    mk_rows, mv_rows = [], []
    for l in range(DEPTH):
        k_l, v_l = memory_kv(mem_prompt, norm_mem[l], x_wk[l], x_wv[l])
        mk_rows.append(k_l)
        mv_rows.append(v_l)
    mem_k_p = jnp.stack(mk_rows)
    mem_v_p = jnp.stack(mv_rows)
    y_prompt, ret_p, s5re_p, s5im_p, mc_p, mn_p, mm_p, conv_p = trunk(
        x_prompt, 0,
        jnp.zeros((N_RS_LAYERS, bp, RET_HEADS, RET_DK, RET_DV), f32),
        jnp.zeros((N_RS_LAYERS, bp, S5_GROUPS, S5_STATE), f32),
        jnp.zeros((N_RS_LAYERS, bp, S5_GROUPS, S5_STATE), f32),
        jnp.zeros((N_ML_LAYERS, bp, ML_HEADS, ML_DH, ML_DH), f32),
        jnp.zeros((N_ML_LAYERS, bp, ML_HEADS, ML_DH), f32),
        jnp.zeros((N_ML_LAYERS, bp, ML_HEADS), f32),
        jnp.zeros((N_ML_LAYERS, bp, ML_CONV - 1, ML_INNER), x_prompt.dtype),
        mem_k_p, mem_v_p, p)
    y_sample, ret_s, s5re_s, s5im_s, mc_s, mn_s, mm_s, conv_s = trunk(
        x_sample, PAST_LEN, state_ret, state_s5_re, state_s5_im, state_mlstm_c, state_mlstm_n,
        state_mlstm_m, cache_mlstm_conv, cache_mem_k, cache_mem_v, p)
    return (y_prompt, y_sample, ret_p, s5re_p, s5im_p, mc_p, mn_p, mm_p, conv_p, mem_k_p, mem_v_p,
            ret_s, s5re_s, s5im_s, mc_s, mn_s, mm_s, conv_s)


_drawn_inputs = setup_inputs


def setup_inputs(seed=0):
    import zlib

    import numpy as np

    out = dict(_drawn_inputs(seed))
    spreads = {}
    factors = {'norm_cross': 8.0,
     'norm_mem': 2.775,
     'norm_mlp': 3.215,
     'norm_final': 23.334,
     'ret_gn': 8.0,
     's5_a_re': 18.551,
     's5_b_glu': 22.342,
     'ml_gn': 134.24,
     'ml_skip': 200.0,
     's5_c_re': 3.955,
     's5_c_im': 3.506}
    for name, (base, spread) in spreads.items():
        noise = np.random.default_rng([zlib.crc32(name.encode()), seed]).standard_normal(out[name].shape)
        drawn = base * np.exp(spread * noise) if base else spread * noise
        out[name] = __import__('jax').numpy.asarray(drawn.astype(out[name].dtype))
    for name, factor in factors.items():
        out[name] = (out[name] * factor).astype(out[name].dtype)
    return out
```

```python
from contextlib import ExitStack

import numpy as np

import concourse.bass as bass
from concourse import mybir

F32 = mybir.dt.float32
F32R = mybir.dt.float32r
ALU = mybir.AluOpType
ACT = mybir.ActivationFunctionType
AX = mybir.AxisListType

P = 128
D = 1024
DT = D // P
TP, TS = 512, 64
T = TP + TS
HALF = T // 2
NTB = TP // P
PAST = 1024
RET_H = 4
S5_TILES = 16
NCH = NTB + 1
ML_H, ML_T = 4, 4
ML_DH = ML_T * P
CELL_ORDER = (3, 2, 1, 0)
OUT_BEFORE = ("den", "num", "mean", "var")
MEM = 256
XH = 4
SLAB = 2048
EPS = 1e-6
NEG = -1e30
TWO_PI = 2 * np.pi
ROUND = 1.5 * 2.0**23
PI_HI = float(np.float32(6.28125))
PI_MID = float(np.float32(TWO_PI - 6.28125))
PI_LO = float(np.float32(TWO_PI - 6.28125 - float(np.float32(TWO_PI - 6.28125))))
GAMMA = [1.0 - 2.0 ** (-5 - h) for h in range(RET_H)]

PARAMS = [("mix0", DT), ("cross0", DT), ("mlp0", DT), ("mix1", DT), ("cross1", DT), ("mlp1", DT), ("final", DT),
          ("mem0", DT), ("mem1", DT), ("ret_gn", 4), ("s5_d", 4), ("b_glu", 4), ("conv_w", 64), ("conv_b", 16),
          ("ml_gn", 16), ("ml_skip", 16), ("a_re", 16), ("a_im", 16), ("log_dt", 16), ("h0_re", 16), ("h0_im", 16),
          ("b_gates", 1), ("m0", 1), ("n0", 16), ("conv_cache", 48)]
PCOL = {}
_at = 0
for _n, _w in PARAMS:
    PCOL[_n] = (_at, _w)
    _at += _w
NPAR = _at


def blk(j):
    return sum(TP - P * i for i in range(j))


SCW = blk(NTB)
UNITS = [(c, hf) for c in range(NCH) for hf in range(2)]
MEM_SLABS = [(l, w, i) for l in range(2) for w in "kv" for i in range(4)]
MEM_AT = [MEM_SLABS[(n * 16) // 10:((n + 1) * 16) // 10] for n in range(10)]


def schedule():
    groups, slabs = {}, {}

    def g(*name):
        groups[name if len(name) > 1 else name[0]] = len(groups)

    def s(*name):
        slabs[name if len(name) > 1 else name[0]] = len(slabs)

    for part in ("u", "q", "k", "v", "g"):
        for i in range(2):
            s("rs", part, i)
            g("rs", part, i)
    g("s5B")
    for h in range(RET_H):
        for x in ("score", "aux", "out", "mean", "var"):
            g("ret", h, x)
    g("memnorm")
    for n, u in enumerate(UNITS):
        g("s5u", n)
        for m in MEM_AT[n]:
            s("mem", *m)
            g("mem", *m)
        if n:
            g("s5y", n - 1)
    g("s5y", len(UNITS) - 1)
    s("glu")
    g("glu", 0)
    g("glu", 1)
    for i in range(4):
        s("rs_out", i)
        g("rs_out", i)
    for l in range(2):
        if l == 1:
            for h in range(ML_H):
                for part in ("xm", "z"):
                    for i in range(2):
                        s("ml", h, part, i)
                        g("ml", h, part, i)
                for part in ("q", "k", "v"):
                    s("ml", h, part)
                    g("ml", h, part, 0)
                    g("ml", h, part, 1)
                g("gate", h)
            g("acol")
            for h in CELL_ORDER:
                for x in ("r", "aux", "score", "vT", "smp", "kT", "den", "num", "kv", "kvs", "n", "mean", "var"):
                    if h == 1 and x in OUT_BEFORE:
                        s("ml_out", 1, OUT_BEFORE.index(x))
                        g("ml_out", 1, OUT_BEFORE.index(x))
                    g("cell", h, x)
            for i in range(4):
                s("ml_out", 0, i)
                g("ml_out", 0, i)
        for i in range(4):
            s("xq", l, i)
            g("xq", l, i)
            if i == 1:
                g("att", l, "score", 0)
        for x in ("pT", 0), ("score", 1), ("pv", 0), ("score", 2), ("pT", 1), ("pT", 2), ("pv", 1), ("pv", 2):
            g("att", l, *x)
        for i in range(4):
            s("xo", l, i)
            g("xo", l, i)
        for a in range(4):
            for d in ("up", "down"):
                for i in range(4):
                    s("mlp", l, a, d, i)
                    g("mlp", l, a, d, i)
    g("final_norm")
    return groups, slabs


GROUPS, SLABS = schedule()
NSLAB = len(SLABS)
NORM_AT = [("rs", "u", 0), ("xq", 0, 0), ("mlp", 0, 0, "up", 0), ("ml", 0, "xm", 0), ("xq", 1, 0), ("mlp", 1, 0, "up", 0)]
XN_BEFORE = [None, ("rs_out", 3), ("xo", 0, 3), ("mlp", 0, 3, "up", 3), ("ml_out", 0, 3), ("xo", 1, 3)]
NW = T // 3


class Chain:

    def __init__(self, eng, sem):
        self.eng, self.sem, self.n = eng, sem, 0
        self.base = None

    def mark(self, ins, *signals):
        ins.then_inc(self.sem, 1)
        self.n += 1
        if signals:
            self.sync()
            for s in signals:
                self.eng.sem_inc(s, 1)

    def value(self):
        return self.n if self.base is None else self.base + self.n

    def sync(self):
        self.eng.wait_ge(self.sem, self.value())

    def loop(self, i, per):
        self.base, self.start, self.per = i * per + self.n, self.n, per
        self.n = 0

    def endloop(self, turns):
        assert self.n == self.per, (self.n, self.per)
        self.n = self.start + turns * self.per
        self.base = None


def program(nc, A):
    ctx = ExitStack()
    with ctx:
        def sb(name, shape, dt=F32, on=ctx):
            return on.enter_context(nc.sbuf_tensor(name, shape, dt))

        sems = {}

        def S(name):
            if name not in sems:
                sems[name] = ctx.enter_context(nc.semaphore(name))
            return sems[name]

        x = sb("x", [P, DT, T])
        xnh = sb("xnh", [P, DT, T], F32R)
        xnl = sb("xnl", [P, DT, T], F32R)
        raw = sb("raw", [P, 2, SLAB])
        whi = sb("whi", [P, 2, SLAB], F32R)
        wlo = sb("wlo", [P, 2, SLAB], F32R)
        par = sb("par", [P, NPAR])
        ones = sb("ones", [P, P])
        over = sb("over", [P, 3, P])
        ident = sb("ident", [P, P])
        epst = sb("epst", [P, 1])
        ss = sb("ss", [P, T])
        rs = sb("rs", [P, T])
        tm = sb("tm", [P, 2, T])
        rsc = sb("rsc", [P, NCH])
        psum = ctx.enter_context(nc.psum_tensor("psum", [P, 8, 512], F32))
        done = [S("group_done_even"), S("group_done_odd")]
        free = [S("group_free_even"), S("group_free_odd")]

        def col(name, i, n=1):
            a, w = PCOL[name]
            return par[:, a + i:a + i + n]

        def bank(g, b):
            return psum[:, 4 * (g % 2) + b, :]

        def group_ready(eng, g, turn=None):
            v = g // 2 + 1
            eng.wait_ge(done[g % 2], v if turn is None else turn + v)

        def group_freed(ins, g):
            ins.then_inc(free[g % 2], 1)

        def group_open(eng, g, turn=None):
            if g >= 2:
                v = g // 2
                eng.wait_ge(free[g % 2], v if turn is None else turn + v)

        def group_close(ins, g):
            ins.then_inc(done[g % 2], 1)

        l0 = ExitStack()
        u = sb("u", [P, 4, TP + P], on=l0)
        gt_ = sb("gsilu", [P, 4, T], on=l0)
        BT = sb("BT", [P, 2, 4, P], on=l0)
        Cm = sb("Cm", [P, 2, S5_TILES, 32], on=l0)
        sp = sb("sp", [P, 24, S5_TILES], on=l0)
        fin5 = sb("fin5", [P, 4, S5_TILES], on=l0)
        l0a = ExitStack()
        q = sb("q", [P, 4, T], on=l0a)
        k = sb("k", [P, 4, T], on=l0a)
        vt = sb("vt", [P, NCH, 512], on=l0a)
        dec = sb("dec", [P, RET_H, TP], on=l0a)
        rope = sb("rope", [P, 2, T], on=l0a)
        wq64 = sb("wq64", [P, RET_H, TS], on=l0a)
        Wm = sb("Wm", [P, SCW], on=l0a)
        Ws = sb("Ws", [TS, TS], on=l0a)
        kt = sb("kt", [P, NCH, P], on=l0a)
        qw = sb("qw", [P, TS], on=l0a)
        sw = sb("sw", [P, 4, HALF], on=l0a)
        S0 = sb("S0", [P, RET_H, P], on=l0a)
        retp = sb("retp", [P, RET_H, P], on=l0a)
        sq = sb("sq", [P, T], on=l0a)
        bz = gt_[:].rearrange("p a t -> p (a t)")[:, 0:2 * S5_TILES * 32].rearrange("p (c s n) -> p c s n", c=2, s=S5_TILES)
        bb = Wm[:, 0:2 * S5_TILES * 32].rearrange("p (c s n) -> p c s n", c=2, s=S5_TILES)
        l0a.close()
        l0b = ExitStack()
        rt = sb("rt", [P, S5_TILES, P], on=l0b)
        za = sb("za", [P, 8, P], on=l0b)
        zb = sb("zb", [P, 8, P], on=l0b)
        zc = sb("zc", [P, 8, P], on=l0b)
        he = sb("he", [P, 2, 8, P], on=l0b)
        hf_ = sb("hf", [P, 2, 8, P], on=l0b)
        memx = sb("memx", [P, DT, MEM], on=l0b)
        mkv = sb("mkv", [P, 2, 512], on=l0b)
        mrs = sb("mrs", [P, MEM], on=l0b)
        mss = sb("mss", [P, MEM], on=l0b)
        msq = sb("msq", [P, 2, MEM], on=l0b)
        l0b.close()
        l0c = ExitStack()
        gh = sb("gh", [P, 4, T], F32R, on=l0c)
        gl = sb("gl", [P, 4, T], F32R, on=l0c)
        sg = sb("sg", [P, 4, HALF], on=l0c)
        l0c.close()
        l0.close()
        xflat = x[:].rearrange("p a t -> p (a t)")
        ctab = xflat[:, 0:S5_TILES * P].rearrange("p (s t) -> p s t", s=S5_TILES)
        stab = xflat[:, S5_TILES * P:2 * S5_TILES * P].rearrange("p (s t) -> p s t", s=S5_TILES)
        mnh = xnh[:, 4:8, :].rearrange("p a t -> p (a t)")[:, 0:DT * MEM].rearrange("p (k t) -> p k t", k=DT)
        mnl = xnl[:, 4:8, :].rearrange("p a t -> p (a t)")[:, 0:DT * MEM].rearrange("p (k t) -> p k t", k=DT)
        la = ExitStack()
        xq = sb("xq", [P, DT, T], on=la)
        KT = sb("KT", [P, 2, DT, MEM], on=la)
        V = sb("V", [P, 2, 2, D], on=la)
        pr = sb("pr", [P, 2, 8, MEM], on=la)
        prs = sb("prs", [TS, XH, MEM], on=la)
        pT = sb("pT", [P, 2, 2, TP], on=la)
        pTs = sb("pTs", [P, 2 * XH, TS], on=la)
        mx = sb("mx", [P, 3, 8], on=la)
        nm = sb("nm", [P, 3, 8], on=la)
        sm = sb("sm", [P, 3, 8], on=la)
        la.close()
        lm = ExitStack()
        hh = sb("hh", [P, DT, T], F32R, on=lm)
        hl = sb("hl", [P, DT, T], F32R, on=lm)
        hr = sb("hr", [P, 4, HALF], on=lm)
        hs = sb("hs", [P, 4, HALF], on=lm)
        lm.close()
        ml = ExitStack()
        gtn = sb("gates_n0", [P, T], on=ml)
        gt = gtn[0:36, :]
        n0b = gtn[:, 0:ML_T * P].rearrange("p (d c) -> p d c", d=ML_T)
        cst = sb("conv_out", [P, 2, 16, 3], on=ml)
        mq = sb("mq", [P, ML_T, T], on=ml)
        mk = sb("mk", [P, ML_T, T], on=ml)
        mv = sb("mv", [P, ML_T, T], on=ml)
        xc = sb("xc", [P, ML_T, T], on=ml)
        mla = ExitStack()
        xm = sb("xm", [P, ML_T, T + 6], on=mla)
        xch = sb("xch", [P, ML_T, T], F32R, on=mla)
        xcl = sb("xcl", [P, ML_T, T], F32R, on=mla)
        xmh = sb("xmh", [P, ML_T, T], F32R, on=mla)
        xml = sb("xml", [P, ML_T, T], F32R, on=mla)
        gw = sb("gw", [P, 48, 36], on=mla)
        mla.close()
        mlb = ExitStack()
        rrow = sb("rrow", [4, SCW + TS], on=mlb)
        enrow = sb("enrow", [4, T], on=mlb)
        sirow = sb("sirow", [4, TS], on=mlb)
        acol = sb("acol", [P, 20], on=mlb)
        causal = sb("causal", [P, P], on=mlb)
        sel = sb("sel", [4, ML_H, P], on=mlb)
        mo = sb("mo", [4, 2], on=mlb)
        nout = sb("nout", [P, 2, 16], on=mlb)
        wcol = sb("wcol", [P, 5], on=mlb)
        siB = sb("siB", [P, TS], on=mlb)
        sz = sb("sz", [P, ML_T, T], on=mlb)
        mlr = ExitStack()
        zrow = sb("zrow", [4, TP], on=mlr)
        frow = sb("frow", [4, T], on=mlr)
        lrow = sb("lrow", [4, T], on=mlr)
        erow = sb("erow", [4, T], on=mlr)
        mrow = sb("mrow", [4, T], on=mlr)
        brow = sb("brow", [4, SCW + TS], on=mlr)
        arow = sb("arow", [4, 5, P], on=mlr)
        mlr.close()
        wt = sb("wt", [P, SCW], on=mlb)
        wts = sb("wts", [TS, TS], on=mlb)
        mvt = sb("mvt", [P, NTB, ML_DH], on=mlb)
        mkt = sb("mkt", [P, NTB, ML_DH], on=mlb)
        vt5 = sb("vt5", [TS, ML_DH], on=mlb)
        kt5 = sb("kt5", [TS, ML_DH], on=mlb)
        C0 = sb("C0", [P, ML_T, ML_DH], on=mlb)
        qs = sb("qs", [P, ML_T, TS], on=mlb)
        mlb.close()
        ml.close()
        kc = mk[:].rearrange("p d t -> p (d t)")[:, 0:ML_T * ML_DH].rearrange("p (d e) -> p d e", d=ML_T)

        GR, SL = GROUPS, SLABS
        block = ctx.enter_context(nc.Block())

        @block.sync
        def _(sp_):
            def load(s, n):
                sp_.dma_start(raw[:, s, :], n).then_inc(S(f"slab_loaded{s}"), 16)

            for s in range(2):
                load(s, A["w"][s])
            with sp_.Fori(1, NSLAB // 2) as i:
                for s in range(2):
                    sp_.wait_ge(S("slab_split"), i * 2 + (s - 1))
                    load(s, A["w"][bass.ds(i * 2 + s, 1)].rearrange("a p n -> p (a n)"))
            if NSLAB % 2:
                sp_.wait_ge(S("slab_split"), NSLAB - 2)
                load(0, A["w"][NSLAB - 1])

        @block.gpsimd
        def _(pool):
            def split(s, i, first=False):
                pool.wait_ge(S(f"slab_loaded{s}"), i * 16 + 16)
                if not first:
                    pool.wait_ge(S("slab_begun"), i * 2 + s)
                pool.sem_inc(S("split_begun"), 1)
                pool.tensor_scalar(whi[:, s, :], raw[:, s, :], 1.0, 1.0, ALU.mult, ALU.mult).then_inc(S("slab_hi"), 1)
                pool.wait_ge(S("slab_hi"), i * 2 + (s + 1))
                pool.tensor_tensor(wlo[:, s, :], raw[:, s, :], whi[:, s, :].bitcast(F32), ALU.subtract)\
                    .then_inc(S("slab_split"), 1)

            pool.memset(ones[:], 1.0)
            pool.memset(over[:, 0, :], 1.0 / D)
            pool.memset(over[:, 1, :], 1.0 / ML_DH)
            pool.memset(over[:, 2, :], 1.0 / P)
            pool.memset(epst[:], EPS).then_inc(S("consts"), 1)
            split(0, 0, True)
            split(1, 0, True)
            with pool.Fori(1, NSLAB // 2) as i:
                split(0, i)
                split(1, i)
            if NSLAB % 2:
                split(0, NSLAB // 2)

        @block.tensor
        def _(pe):
            def slab_start(n, turn=None):
                pe.wait_ge(S("slab_split"), n + 1 if turn is None else turn * 8 + (n + 1))

            def project(g, n, rh, rl, kts=DT, m0=0, ms=2, wait=None, turn=None, first=True, halves=((0, HALF), (HALF, T)),
                        order=None, close=True):
                s = n % 2
                slab_start(n, turn and turn[1])
                group_open(pe, g, turn and turn[0])
                W = [w[:, s, :].rearrange("p (k m c) -> p k m c", k=kts, m=ms) for w in (whi, wlo)]
                order = order or range(kts)
                for kk in order:
                    at_first, at_last = kk == order[0], kk == order[-1]
                    if wait:
                        wait(kk)
                    for m in range(2):
                        for wi, r in ((0, rh), (0, rl), (1, rh)):
                            for b, (t0, t1) in enumerate(halves):
                                ins = pe.matmul(bank(g, 2 * m + b)[:, 0:t1 - t0], W[wi][:, kk, m0 + m, :], r[:, kk, t0:t1],
                                                start=(at_first and wi == 0 and r is rh), stop=(at_last and wi == 1))
                            if at_first and m == 0 and wi == 0 and r is rh and first:
                                ins.then_inc(S("slab_begun"), 1)
                if close:
                    group_close(ins, g)

            def token_major(g, n, xh, xl, toks, rows):
                s = n % 2
                slab_start(n)
                group_open(pe, g)
                W = [w[:, s, :].rearrange("p (k c) -> p k c", k=DT) for w in (whi, wlo)]
                for (t0, t1), (b, c0) in zip(toks, rows):
                    for kk in range(DT):
                        for wi, r in ((0, xh), (0, xl), (1, xh)):
                            ins = pe.matmul(bank(g, b)[0:t1 - t0, c0:c0 + 256], r[:, kk, t0:t1], W[wi][:, kk, :],
                                            start=(kk == 0 and wi == 0 and r is xh), stop=(kk == DT - 1 and wi == 1))
                            if t0 == toks[0][0] and kk == 0 and wi == 0 and r is xh:
                                ins.then_inc(S("slab_begun"), 1)
                group_close(ins, g)

            def token_sum(g, which, src, width=T):
                group_open(pe, g)
                for b, (t0, t1) in enumerate(((0, HALF), (HALF, T)) if width == T else ((0, width),)):
                    ins = pe.matmul(bank(g, b)[:, 0:t1 - t0], over[:, which, :], src[:, t0:t1], start=True, stop=True)
                group_close(ins, g)

            def mm(out, lhsT, rhs, first=True, last=True):
                return pe.matmul(out, lhsT, rhs, start=first, stop=last)

            def project_first(i, g, n, turn=None):
                project(g, n, xnh, xnl, wait=lambda kk: pe.wait_ge(S("xn_ready"), 8 * i + kk + 1), close=False)
                pe.wait_ge(S("squares_ready"), i + 1)
                for b in range(3):
                    ins = mm(bank(g, b)[:, HALF:HALF + NW], over[:, 0, :], ss[:, NW * b:NW * b + NW])
                if i == 0:
                    for t in range(NCH):
                        w = P if t < NTB else TS
                        ins = mm(bank(g, 3)[0:w, HALF + t:HALF + t + 1], ss[:, P * t:P * t + w], over[:, 0, 0:1])
                group_close(ins, g)

            pe.wait_ge(S("consts"), 1)
            for part in ("u", "q", "k", "v", "g"):
                for i in range(2):
                    g, n = GR["rs", part, i], SL["rs", part, i]
                    if part == "v":
                        toks = [(P * t, min(P * t + P, T)) for t in range(NCH)]
                        token_major(g, n, xnh, xnl, toks, [(0, 0), (1, 0), (2, 0), (3, 0), (3, 256)])
                    elif (part, i) == ("u", 0):
                        project_first(0, g, n)
                    else:
                        project(g, n, xnh, xnl)
            pe.wait_ge(S("bb_ready"), 1)
            pe.wait_ge(S("const_loaded"), 16 * 9)
            g = GR["s5B"]
            group_open(pe, g)
            for c in range(2):
                for j in range(4):
                    ins = pe.transpose(bank(g, c)[:, P * j:P * j + P],
                                       bb[:, c, 4 * j:4 * j + 4, :].rearrange("p s c -> p (s c)"), ident[:])
            group_close(ins, g)

            pe.wait_ge(S("rope_done"), 2)
            for h in range(RET_H):
                g = GR["ret", h, "score"]
                group_open(pe, g)
                for j in range(NTB):
                    ins = mm(bank(g, j)[:, 0:TP - P * j], k[:, h, P * j:P * j + P], q[:, h, P * j:TP])
                group_close(ins, g)
                g = GR["ret", h, "aux"]
                group_open(pe, g)
                mm(bank(g, 0)[0:TS, 0:TS], k[:, h, TP:T], q[:, h, TP:T])
                for j in range(NTB):
                    pe.transpose(bank(g, 1)[:, P * j:P * j + P], k[:, h, P * j:P * j + P], ident[:])
                ins = pe.transpose(bank(g, 2)[0:TS, 0:P], k[:, h, TP:T], ident[:])
                group_close(ins, g)
                g = GR["ret", h, "out"]
                group_open(pe, g)
                hc = slice(h * P, h * P + P)
                pe.wait_ge(S("ret_w"), h + 1)
                for j in range(NTB):
                    mm(bank(g, 0)[:, P * j:TP], vt[:, j, hc], Wm[:, blk(j):blk(j) + TP - P * j], j == 0, j == NTB - 1)
                mm(bank(g, 1)[:, 0:TS], S0[:, h, :], qw[:], True, False)
                mm(bank(g, 1)[:, 0:TS], vt[0:TS, NTB, hc], Ws[:], False, True)
                for j in range(NTB):
                    mm(bank(g, 2)[:, 0:P], kt[:, j, :], vt[:, j, hc], j == 0, j == NTB - 1)
                ins = mm(bank(g, 3)[:, 0:P], kt[0:TS, NTB, :], vt[0:TS, NTB, hc])
                group_close(ins, g)
                pe.wait_ge(S("ret_o"), h + 1)
                token_sum(GR["ret", h, "mean"], 2, q[:, h, :])
                pe.wait_ge(S("ret_sq"), h + 1)
                token_sum(GR["ret", h, "var"], 2, sq[:])

            pe.wait_ge(S("mem_squares"), 1)
            token_sum(GR["memnorm"], 0, mss, MEM)

            def s5_y(n):
                c, hf = UNITS[n]
                g = GR["s5y", n]
                pe.wait_ge(S("s5_h"), n + 1)
                group_open(pe, g)
                for s in range(8):
                    o = bank(g, s // 4)[32 * (s % 4):32 * (s % 4) + 32, 0:P]
                    st = 8 * hf + s
                    mm(o, Cm[:, 0, st, :], he[:, n % 2, s, :], True, False)
                    ins = mm(o, Cm[:, 1, st, :], hf_[:, n % 2, s, :], False, True)
                group_close(ins, g)

            pe.wait_ge(S("s5_const"), 1)
            for n, (c, hf) in enumerate(UNITS):
                g = GR["s5u", n]
                group_open(pe, g)
                for i in range(4):
                    for c2 in range(2):
                        for a in range(2):
                            j = 2 * hf + a
                            r = slice(32 * i, 32 * i + 32)
                            ins = mm(bank(g, i)[:, P * (2 * c2 + a):P * (2 * c2 + a) + P], BT[r, c2, j, :], u[r, j, P * c:P * c + P])
                group_close(ins, g)
                for l, w, i in MEM_AT[n]:
                    gm, sn = GR["mem", l, w, i], SL["mem", l, w, i]
                    pe.wait_ge(S("mem_ready"), l + 1)
                    if w == "k":
                        project(gm, sn, mnh, mnl, halves=((0, MEM),))
                    else:
                        token_major(gm, sn, mnh, mnl, [(0, P), (P, 2 * P)], [(0, 0), (1, 0)])
                if n:
                    s5_y(n - 1)
            s5_y(len(UNITS) - 1)
            pe.wait_ge(S("glu_in"), 1)
            for a in range(2):
                project(GR["glu", a], SL["glu"], gh, gl, kts=4, m0=2 * a, ms=4, first=a == 0)
            pe.wait_ge(S("rs_y"), 1)
            for i in range(4):
                project(GR["rs_out", i], SL["rs_out", i], xnh, xnl)

            def attention(l):
                for i in range(4):
                    if i == 0:
                        project_first(3 * l + 1, GR["xq", l, i], SL["xq", l, i])
                    else:
                        project(GR["xq", l, i], SL["xq", l, i], xnh, xnl)
                    if i == 1:
                        pe.wait_ge(S("kv_loaded"), 64 * (l + 1))
                        scores(l, 0)
                transposed(l, 0)
                scores(l, 1)
                values(l, 0)
                g = GR["att", l, "score", 2]
                group_open(pe, g)
                for h in range(XH):
                    for e in range(2):
                        ins = mm(bank(g, h)[0:TS, 0:MEM], xq[:, 2 * h + e, TP:T], KT[:, 1, 2 * h + e, :], e == 0, e == 1)
                group_close(ins, g)
                transposed(l, 1)
                transposed(l, 2)
                values(l, 1)
                values(l, 2)
                pe.wait_ge(S("att_o"), 3 * (l + 1))
                for i in range(4):
                    project(GR["xo", l, i], SL["xo", l, i], xnh, xnl)

            def scores(l, x2):
                g = GR["att", l, "score", x2]
                pe.wait_ge(S("xq_ready"), 4 * l + 2 * x2 + 2)
                group_open(pe, g)
                for t in range(NTB):
                    for h in range(2):
                        for e in range(2):
                            f = 2 * (2 * x2 + h) + e
                            ins = mm(bank(g, t)[:, MEM * h:MEM * h + MEM], xq[:, f, P * t:P * t + P], KT[:, 0, f, :],
                                     e == 0, e == 1)
                group_close(ins, g)

            def transposed(l, x2):
                g = GR["att", l, "pT", x2]
                pe.wait_ge(S("prob"), 3 * l + x2 + 1)
                group_open(pe, g)
                if x2 < 2:
                    for h in range(2):
                        for m in range(2):
                            for t in range(NTB):
                                ins = pe.transpose(bank(g, 2 * h + m)[:, P * t:P * t + P],
                                                   pr[:, x2, 2 * t + h, P * m:P * m + P], ident[:])
                else:
                    for h in range(XH):
                        for m in range(2):
                            ins = pe.transpose(bank(g, 0)[:, TS * (2 * h + m):TS * (2 * h + m) + TS],
                                               prs[:, h, P * m:P * m + P], ident[0:TS, 0:TS])
                group_close(ins, g)

            def values(l, x2):
                g = GR["att", l, "pv", x2]
                pe.wait_ge(S("pT"), 3 * l + x2 + 1)
                group_open(pe, g)
                for h in range(2 if x2 < 2 else XH):
                    for e in range(2):
                        for m in range(2):
                            if x2 < 2:
                                hg = 2 * x2 + h
                                ins = mm(bank(g, 2 * h + e), V[:, 0, m, 2 * P * hg + P * e:2 * P * hg + P * e + P],
                                         pT[:, h, m, :], m == 0, m == 1)
                            else:
                                ins = mm(bank(g, 0)[:, TS * (2 * h + e):TS * (2 * h + e) + TS],
                                         V[:, 1, m, 2 * P * h + P * e:2 * P * h + P * e + P], pTs[:, 2 * h + m, :],
                                         m == 0, m == 1)
                group_close(ins, g)

            def mlp(l):
                g0, n0 = GR["mlp", l, 0, "up", 0], SL["mlp", l, 0, "up", 0]

                def quarter(first=False, tg=None, tn=None, base=0):
                    for i in range(4):
                        if first and i == 0:
                            project_first(3 * l + 2, g0, n0)
                        else:
                            project(g0 + i, n0 + i, xnh, xnl, turn=tn is not None and (tg, tn) or None)
                    for i in range(4):
                        def hid(kk):
                            pe.wait_ge(S("hidden_ready"), base + (16 * l + kk // 2 + 1))
                        project(g0 + 4 + i, n0 + 4 + i, hh, hl, turn=tn is not None and (tg, tn) or None,
                                wait=hid if i == 0 else None)

                quarter(first=True)
                with pe.Fori(1, 4) as a:
                    quarter(tg=a * 4, tn=a, base=a * 4)

            attention(0)
            mlp(0)
            for h in range(ML_H):
                for part in ("xm", "z"):
                    for i in range(2):
                        if (h, part, i) == (0, "xm", 0):
                            project_first(3, GR["ml", h, part, i], SL["ml", h, part, i])
                        else:
                            project(GR["ml", h, part, i], SL["ml", h, part, i], xnh, xnl)
                for w, part in enumerate(("q", "k", "v")):
                    if w == 0:
                        pe.wait_ge(S("xc_split"), 4 * (h + 1))
                    elif w == 2:
                        pe.wait_ge(S("xm_split"), h + 1)
                    for a in range(2):
                        project(GR["ml", h, part, a], SL["ml", h, part], *((xmh, xml) if w == 2 else (xch, xcl)), kts=4,
                                m0=2 * a, ms=4, first=a == 0)
                g = GR["gate", h]
                if h == 0:
                    pe.wait_ge(S("gw_loaded"), 16)
                group_open(pe, g)
                for w, buf in enumerate((mq, mk, mv)):
                    pe.wait_ge(S("qkv_ready"), 6 * h + 2 * w + 2)
                    for t in range(ML_T):
                        for b, (t0, t1) in enumerate(((0, HALF), (HALF, T))):
                            ins = mm(bank(g, b)[0:36, 0:t1 - t0], gw[:, 16 * w + 4 * h + t, :], buf[:, t, t0:t1],
                                     w == 0 and t == 0, w == 2 and t == ML_T - 1)
                group_close(ins, g)
            g = GR["acol"]
            pe.wait_ge(S("rows_ready"), 1)
            group_open(pe, g)
            for j in range(5):
                w = P if j < NTB else TS
                ins = pe.transpose(bank(g, 0)[0:w, 4 * j:4 * j + 4], arow[:, j, 0:w], ident[0:4, 0:4])
            group_close(ins, g)
            pe.wait_ge(S("cell_const"), 32)
            pe.wait_ge(S("rows_exp"), 1)

            def out_slab(pair, i):
                def tile_ready(kk):
                    pe.wait_ge(S("cell_y"), 8 * (1 - pair) + (kk - 3 if kk >= 4 else kk + 5))
                project(GR["ml_out", pair, i], SL["ml_out", pair, i], xnh, xnl, wait=None if i else tile_ready,
                        order=(4, 5, 6, 7, 0, 1, 2, 3))

            for n, h in enumerate(CELL_ORDER):
                def open_(x):
                    if h == 1 and x in ("den", "num"):
                        out_slab(1, OUT_BEFORE.index(x))
                    g = GR["cell", h, x]
                    group_open(pe, g)
                    return g, [bank(g, b) for b in range(4)]

                g, B = open_("r")
                for j in range(NTB):
                    w = TP - P * j
                    mm(B[j][:, 0:w], sel[:, h, :], rrow[:, blk(j):blk(j) + w], True, False)
                    ins = mm(B[j][:, 0:P], ident[:], causal[:], False, True)
                group_close(ins, g)
                g, B = open_("aux")
                mm(B[0][0:TS, 0:TS], sel[:, h, 0:TS], rrow[:, SCW:SCW + TS], True, False)
                mm(B[0][0:TS, 0:TS], ident[0:TS, 0:TS], causal[0:TS, 0:TS], False, True)
                mm(B[1][:, 0:TS], sel[:, h, :], sirow[:])
                for b in range(2):
                    ins = mm(B[2 + b][:, 0:HALF], sel[:, h, :], enrow[:, HALF * b:HALF * b + HALF])
                group_close(ins, g)
                pe.wait_ge(S("cell_q"), 16 * n + 1 if n else 1)
                pe.wait_ge(S("cell_k"), 16 * n + 1 if n else 1)
                g, B = open_("score")
                for j in range(NTB):
                    for d in range(ML_T):
                        ins = mm(B[j][:, 0:TP - P * j], mk[:, d, P * j:P * j + P], mq[:, d, P * j:TP], d == 0, d == ML_T - 1)
                group_close(ins, g)
                pe.wait_ge(S("cell_v"), 16 * n + 1 if n else 1)
                g, B = open_("vT")
                for j in range(NTB):
                    for d in range(ML_T):
                        ins = pe.transpose(B[j][:, P * d:P * d + P], mv[:, d, P * j:P * j + P], ident[:])
                group_close(ins, g)
                g, B = open_("smp")
                for d in range(ML_T):
                    mm(B[0][0:TS, 0:TS], mk[:, d, TP:T], mq[:, d, TP:T], d == 0, d == ML_T - 1)
                for b, src in ((1, mv), (2, mk)):
                    for d in range(ML_T):
                        ins = pe.transpose(B[b][0:TS, P * d:P * d + P], src[:, d, TP:T], ident[:])
                group_close(ins, g)
                g, B = open_("kT")
                for j in range(NTB):
                    for d in range(ML_T):
                        ins = pe.transpose(B[j][:, P * d:P * d + P], mk[:, d, P * j:P * j + P], ident[:])
                group_close(ins, g)
                g, B = open_("den")
                pe.wait_ge(S("cell_pt"), n + 1)
                pe.wait_ge(S("cell_qs"), n + 1)
                pe.wait_ge(S("cell_smp"), n + 1)
                pe.wait_ge(S("cell_c"), 16 * (n + 1))
                for j in range(NTB):
                    mm(B[0][:, P * j:TP], ones[:], wt[:, blk(j):blk(j) + TP - P * j], j == 0, j == NTB - 1)
                for d in range(ML_T):
                    mm(B[1][:, 0:TS], n0b[:, d, :], qs[:, d, :], d == 0, False)
                mm(B[1][:, 0:TS], ones[0:TS, :], wts[:], False, True)
                for e in range(ML_T):
                    o = B[2][:, TS * e:TS * e + TS]
                    for d in range(ML_T):
                        mm(o, C0[:, d, P * e:P * e + P], qs[:, d, :], d == 0, False)
                    ins = mm(o, vt5[:, P * e:P * e + P], wts[:], False, True)
                group_close(ins, g)
                g, B = open_("num")
                pe.wait_ge(S("cell_vt"), n + 1)
                for e in range(ML_T):
                    for j in range(NTB):
                        ins = mm(B[e][:, P * j:TP], mvt[:, j, P * e:P * e + P], wt[:, blk(j):blk(j) + TP - P * j],
                                 j == 0, j == NTB - 1)
                group_close(ins, g)
                pe.wait_ge(S("cell_kt"), n + 1)
                g, B = open_("kv")
                for d in range(ML_T):
                    for j in range(NTB):
                        ins = mm(B[d], mkt[:, j, P * d:P * d + P], mvt[:, j, :], j == 0, j == NTB - 1)
                group_close(ins, g)
                g, B = open_("kvs")
                for d in range(ML_T):
                    ins = mm(B[d], kt5[:, P * d:P * d + P], vt5[:])
                group_close(ins, g)
                g, B = open_("n")
                for d in range(ML_T):
                    for j in range(NTB):
                        mm(B[0][:, d:d + 1], mkt[:, j, P * d:P * d + P], ones[:, 0:1], j == 0, j == NTB - 1)
                for d in range(ML_T):
                    ins = mm(B[0][:, 4 + d:5 + d], kt5[:, P * d:P * d + P], ones[0:TS, 0:1])
                group_close(ins, g)
                if h == 1:
                    out_slab(1, 2)
                pe.wait_ge(S("cell_sum"), 2 * n + 1)
                token_sum(GR["cell", h, "mean"], 1, ss)
                if h == 1:
                    out_slab(1, 3)
                pe.wait_ge(S("cell_sum"), 2 * n + 2)
                token_sum(GR["cell", h, "var"], 1, ss)
            for i in range(4):
                out_slab(0, i)
            attention(1)
            mlp(1)
            pe.wait_ge(S("squares_ready"), 7)
            token_sum(GR["final_norm"], 0, ss)

        @block.scalar
        def _(act):
            ch = Chain(act, S("act_step"))

            def load(dst, src, sem):
                act.dma_start(dst, src).then_inc(S(sem), 16)

            load(par[:], A["par"], "par_loaded")
            for j in range(4):
                load(x[:, 2 * j:2 * j + 2, :], A["xT"][:, 2 * j:2 * j + 2, :], f"x_loaded{j}")
            load(rope[:], A["rope"], "const_loaded")
            load(dec[:], A["decay"], "const_loaded")
            load(wq64[:], A["wq64"], "const_loaded")
            load(ident[:], A["ident"], "const_loaded")
            load(S0[:], A["ret0"], "const_loaded")
            load(bz[:, 0], A["Bre"], "const_loaded")
            load(bz[:, 1], A["Bim"], "const_loaded")
            load(Cm[:, 0], A["Cre"], "const_loaded")
            load(Cm[:, 1], A["Cim"], "const_loaded")

            def rstd(g, out, width=T):
                group_ready(act, g)
                for b, (t0, t1) in enumerate(((0, HALF), (HALF, T)) if width == T else ((0, width),)):
                    ins = act.activation(out[:, t0:t1], bank(g, b)[:, 0:t1 - t0], ACT.Ln, bias=epst[:])
                    ch.mark(ins)
                ch.sync()
                act.sem_inc(free[g % 2], 1)
                act.activation(out[:, 0:width], out[:, 0:width], ACT.Exp, scale=-0.5).then_inc(S("rstd_ready"), 1)

            X_TILE = {1: ("x_tile", 0), 2: ("x_tile", 8), 3: ("x_mlp", 24), 4: ("x_tile", 24), 5: ("x_tile", 32),
                      6: ("x_mlp", 56)}

            def x_tile(i, kk):
                if i:
                    act.wait_ge(S(X_TILE[i][0]), X_TILE[i][1] + kk + 1)
                else:
                    act.wait_ge(S(f"x_loaded{kk // 2}"), 16)

            def squares(i, kks):
                for kk in kks:
                    x_tile(i, kk)
                    if 8 * i + kk >= 2:
                        act.wait_ge(S("sq_used"), 8 * i + kk - 1)
                    act.activation(tm[:, kk % 2, :], x[:, kk, :], ACT.Square).then_inc(S("sq_ready"), 1)

            def high(i, gain, kks):
                if i and kks[0] == 0:
                    group_ready(act, GR[XN_BEFORE[i]])
                for kk in kks:
                    x_tile(i, kk)
                    act.activation(xnh[:, kk, :], x[:, kk, :], ACT.Copy, scale=col(gain, kk)).then_inc(S("xn_hi"), 1)

            def norm_rstd(i, power=1):
                g = GR[NORM_AT[i]]
                group_ready(act, g)
                ch.mark(act.activation(rs[:].rearrange("p (b t) -> p b t", b=3),
                                       psum[:, 4 * (g % 2):4 * (g % 2) + 3, HALF:HALF + NW], ACT.Ln, bias=epst[:]))
                if i == 0:
                    ch.mark(act.activation(rsc[:, 0:NTB], bank(g, 3)[:, HALF:HALF + NTB], ACT.Ln, bias=epst[:]))
                    ch.mark(act.activation(rsc[0:TS, NTB:NCH], bank(g, 3)[0:TS, HALF + NTB:HALF + NCH], ACT.Ln,
                                           bias=epst[0:TS]))
                ch.sync()
                if i == 0:
                    act.activation(rsc[:, 0:NTB], rsc[:, 0:NTB], ACT.Exp, scale=-0.5)
                    act.activation(rsc[0:TS, NTB:NCH], rsc[0:TS, NTB:NCH], ACT.Exp, scale=-0.5)
                act.activation(rs[:], rs[:], ACT.Exp, scale=-0.5 * power).then_inc(S("rstd_ready"), 1)

            act.wait_ge(S("par_loaded"), 16)
            high(0, "mix0", range(DT))
            act.wait_ge(S("consts"), 1)
            squares(0, range(DT))
            norm_rstd(0)
            act.activation(sp[:, 0, :], col("log_dt", 0, 16), ACT.Exp).then_inc(S("s5_dt"), 1)
            act.wait_ge(S("s5_arg"), 1)
            act.activation(sp[:, 3, :], sp[:, 1, :], ACT.Exp)
            act.activation(sp[:, 4, :], sp[:, 2, :], ACT.Sin)
            act.activation(sp[:, 5, :], sp[:, 2, :], ACT.Sin, scale=0.5).then_inc(S("s5_trig"), 1)
            for w, part in enumerate(("q", "k")):
                for i in range(2):
                    g = GR["rs", part, i]
                    group_ready(act, g)
                    if 2 * w + i:
                        act.wait_ge(S("swap_used"), 2 * w + i)
                    for b in range(4):
                        act.activation(sw[0:64, b, :], bank(g, b)[64:128, 0:HALF], ACT.Copy)
                        ins = act.activation(sw[64:128, b, :], bank(g, b)[0:64, 0:HALF], ACT.Copy)
                    ins.then_inc(S("swap_ready"), 1)
            for i in range(2):
                act.wait_ge(S("g_scaled"), i + 1)
                act.activation(gt_[:, 2 * i:2 * i + 2, :], gt_[:, 2 * i:2 * i + 2, :], ACT.Silu).then_inc(S("g_silu"), 1)
            for h in range(RET_H):
                act.wait_ge(S("ret_c"), h + 1)
                act.activation(sq[:], q[:, h, :], ACT.Square).then_inc(S("ret_sq"), 1)
                rstd(GR["ret", h, "var"], rs)
                if h == RET_H - 1:
                    act.wait_ge(S("ret_state"), RET_H)
                    act.dma_start(A["o_retp"], retp[:]).then_inc(S("stored"), 16)
                    act.dma_start(A["o_rets"], S0[:]).then_inc(S("stored"), 16)
                    act.wait_ge(S("stored"), 32)
            act.wait_ge(S("ret_end"), 1)
            load(memx[:], A["memT"], "memx_loaded")
            act.wait_ge(S("memx_loaded"), 16)
            for kk in range(DT):
                if kk >= 2:
                    act.wait_ge(S("msq_used"), kk - 1)
                act.activation(msq[:, kk % 2, :], memx[:, kk, :], ACT.Square).then_inc(S("msq_ready"), 1)
            rstd(GR["memnorm"], mrs, MEM)
            for j, (l, w, i) in enumerate(MEM_SLABS):
                g = GR["mem", l, w, i]
                group_ready(act, g)
                if j >= 2:
                    act.wait_ge(S(f"mkv_stored{j % 2}"), 16 * (j // 2))
                if w == "k":
                    for m in range(2):
                        ins = act.activation(mkv[:, j % 2, MEM * m:MEM * m + MEM], bank(g, 2 * m)[:, 0:MEM], ACT.Copy)
                    dst = A["o_mkT"][l][:, 2 * i:2 * i + 2, :]
                else:
                    for t in range(2):
                        ins = act.activation(mkv[:, j % 2, 256 * t:256 * t + 256], bank(g, t)[:, 0:256], ACT.Copy)
                    dst = A["o_mv"][l][:, :, 256 * i:256 * i + 256]
                ch.mark(ins, free[g % 2])
                act.dma_start(dst, mkv[:, j % 2, :].rearrange("p (a b) -> p a b", a=2)).then_inc(S(f"mkv_stored{j % 2}"), 16)
            act.wait_ge(S("s5_y"), 10)
            for j in range(2):
                act.wait_ge(S(f"mkv_stored{j}"), 16 * 8)
            load(x[:], A["xT"], "x_again")
            for j in range(4):
                act.activation(u[:, j, 0:T], u[:, j, 0:T], ACT.Gelu_apprx_tanh).then_inc(S("gelu"), 1)
            for a in range(2):
                g = GR["glu", a]
                group_ready(act, g)
                if a:
                    act.wait_ge(S("sg_used"), 1)
                for m in range(2):
                    for b in range(2):
                        ins = act.activation(sg[:, 2 * m + b, :], bank(g, 2 * m + b)[:, 0:HALF], ACT.Sigmoid,
                                             bias=col("b_glu", 2 * a + m))
                ch.mark(ins, free[g % 2], S("sg_ready"))

            act.dma_start(A["o_s5"], fin5[:]).then_inc(S("stored"), 16)
            act.wait_ge(S("stored"), 48)

            def before_projection(i, gain):
                squares(i, range(6))
                high(i, gain, range(6))
                high(i, gain, range(6, 8))
                squares(i, range(6, 8))

            def attention(l):
                for j in range(2):
                    act.wait_ge(S(f"mkv_stored{j}"), 16 * 8)
                act.wait_ge(S("arena_free"), l + 1)
                load(KT[:, 0], A["o_mkT"][l], "kv_loaded")
                load(KT[:, 1], A["ckT"][l], "kv_loaded")
                load(V[:, 0], A["o_mv"][l], "kv_loaded")
                load(V[:, 1], A["cv"][l], "kv_loaded")
                before_projection(3 * l + 1, f"cross{l}")
                norm_rstd(3 * l + 1)
                for x2 in range(3):
                    g = GR["att", l, "score", x2]
                    act.wait_ge(S("row_max"), 3 * l + x2 + 1)
                    for t in range(NTB):
                        if x2 < 2:
                            for h in range(2):
                                ins = act.activation(pr[:, x2, 2 * t + h, :], bank(g, t)[:, MEM * h:MEM * h + MEM], ACT.Exp,
                                                     bias=nm[:, x2, 2 * t + h:2 * t + h + 1], scale=1.0 / 16,
                                                     accum_out=sm[:, x2, 2 * t + h:2 * t + h + 1])
                        else:
                            ins = act.activation(prs[:, t, :], bank(g, t)[0:TS, 0:MEM], ACT.Exp,
                                                 bias=nm[0:TS, x2, t:t + 1], scale=1.0 / 16, accum_out=sm[0:TS, x2, t:t + 1])
                    ch.mark(ins, free[g % 2], S("exp_done"))

            attention(0)
            before_projection(2, "mlp0")
            norm_rstd(2, power=2)
            high(3, "mix1", range(DT))
            squares(3, range(DT))
            load(gw[:], A["gw"], "gw_loaded")
            norm_rstd(3)

            def store(dst, src, name):
                act.dma_start(dst, src).then_inc(S(name), 16)

            for h in range(ML_H):
                act.wait_ge(S("xm_ready"), 2 * (h + 1))
                if h:
                    group_ready(act, GR["ml", h - 1, "v", 1])
                act.activation(xmh[:, :, 0:TP], xm[:, :, 3:3 + TP], ACT.Copy)
                act.activation(xmh[:, :, TP:T], xm[:, :, TP + 6:T + 6], ACT.Copy).then_inc(S("xm_hi"), 1)
                for t in range(ML_T):
                    act.wait_ge(S("conv_done"), 4 * h + t + 1)
                    ch.mark(act.activation(xc[:, t, :], xc[:, t, :], ACT.Silu))
                    ch.sync()
                    act.activation(xch[:, t, :], xc[:, t, :], ACT.Copy).then_inc(S("xc_hi"), 1)
                if h < ML_H - 1:
                    store(A["t_xc"][h], xc[:], "xc_spilled")
                for i in range(2):
                    act.wait_ge(S("z_scaled"), 2 * h + i + 1)
                    ch.mark(act.activation(mv[:, 2 * i:2 * i + 2, :], mv[:, 2 * i:2 * i + 2, :], ACT.Sigmoid))
                ch.sync()
                store(A["t_z"][h], mv[:], "z_spilled")
                if h < ML_H - 1:
                    for w, (nm_, buf) in enumerate((("q", mq), ("k", mk), ("v", mv))):
                        act.wait_ge(S("qkv_ready"), 6 * h + 2 * w + 2)
                        store(A["t_" + nm_][h], buf[:], nm_ + "_spilled")
            act.wait_ge(S("gates_done"), ML_H)
            load(causal[:], A["causal"], "cell_const")
            load(sel[:], A["sel"], "cell_const")
            act.wait_ge(S("z_spilled"), 16 * ML_H)
            load(sz[:], A["t_z"][CELL_ORDER[0]], "cell_z")
            ch.mark(act.activation(frow[:], gt[32:36, :], ACT.Copy))
            ch.sync()
            ch.mark(act.activation(erow[:], frow[:], ACT.Abs))
            ch.sync()
            ch.mark(act.activation(erow[:], erow[:], ACT.Exp, scale=-1.0))
            ch.sync()
            act.activation(erow[:], erow[:], ACT.Ln, bias=1.0).then_inc(S("log1p"), 1)
            act.wait_ge(S("rows_ready"), 1)
            act.activation(enrow[:], mrow[:], ACT.Exp, scale=-1.0)
            act.activation(sirow[:], rrow[:, SCW:SCW + TS], ACT.Exp, bias=par[0:4, PCOL["m0"][0]:PCOL["m0"][0] + 1])\
                .then_inc(S("rows_exp"), 1)
            group_ready(act, GR["acol"])
            act.wait_ge(S("rows_exp"), 1)
            act.wait_ge(S("acol_ready"), 1)
            load(C0[:], A["C0"][CELL_ORDER[0]], "cell_c")
            store(A["o_m"], mo[:], "stored")
            store(A["o_conv"], cst[:], "stored")
            for n, h in enumerate(CELL_ORDER):
                g = GR["cell", h, "r"]
                group_ready(act, g)
                if n:
                    group_ready(act, GR["cell", CELL_ORDER[n - 1], "num"])
                for j in range(NTB):
                    ins = act.activation(wt[:, blk(j):blk(j + 1)], bank(g, j)[:, 0:TP - P * j], ACT.Exp,
                                         bias=acol[:, 4 * j + h:4 * j + h + 1])
                group_freed(ins, g)
                g = GR["cell", h, "aux"]
                group_ready(act, g)
                if n:
                    act.wait_ge(S("cell_y"), 4 * n)
                act.activation(wts[:], bank(g, 0)[0:TS, 0:TS], ACT.Exp, bias=acol[0:TS, 16 + h:17 + h])
                act.activation(siB[:], bank(g, 1)[:, 0:TS], ACT.Copy)
                for b in range(2):
                    ins = act.activation(tm[:, 0, HALF * b:HALF * b + HALF], bank(g, 2 + b)[:, 0:HALF], ACT.Copy)
                ch.mark(ins, free[g % 2], S("cell_w"))
                g = GR["cell", h, "vT"]
                group_ready(act, g)
                for j in range(NTB):
                    ins = act.activation(mvt[:, j, :], bank(g, j), ACT.Copy)
                ch.mark(ins, free[g % 2], S("cell_vt"))
                g = GR["cell", h, "kT"]
                group_ready(act, g)
                act.wait_ge(S("cell_wcol"), n + 1)
                for j in range(NTB):
                    ins = act.activation(mkt[:, j, :], bank(g, j), ACT.Copy, scale=wcol[:, j:j + 1])
                ch.mark(ins, free[g % 2], S("cell_kt"))
                nxt = CELL_ORDER[n + 1] if n + 1 < ML_H else None
                if nxt is not None:
                    act.wait_ge(S("cell_qs"), n + 1)
                    load(mq[:], A["t_q"][nxt], "cell_q")
                    load(mv[:], A["t_v"][nxt], "cell_v")
                g = GR["cell", h, "den"]
                group_ready(act, g)
                act.activation(tm[:, 1, 0:TP], bank(g, 0), ACT.Abs)
                act.activation(tm[:, 1, TP:T], bank(g, 1)[:, 0:TS], ACT.Abs).then_inc(S("cell_abs"), 1)
                g = GR["cell", h, "kv"]
                group_ready(act, g)
                for d in range(ML_T):
                    ins = act.activation(kc[:, d, :], bank(g, d), ACT.Copy)
                ch.mark(ins, free[g % 2])
                store(A["o_cp"][h], kc, "cp_stored")
                act.wait_ge(S("cell_cs"), n + 1)
                store(A["o_cs"][h], C0[:], "cs_stored")
                act.wait_ge(S("cell_c0"), n + 1)
                for e in range(ML_T):
                    if 4 * n + e >= 2:
                        act.wait_ge(S("csq_used"), 4 * n + e - 1)
                    act.activation(tm[:, e % 2, :], sz[:, e, :], ACT.Square).then_inc(S("csq_ready"), 1)
                rstd(GR["cell", h, "var"], rs)
                act.wait_ge(S("cp_stored"), 16 * (n + 1))
                act.wait_ge(S("cs_stored"), 16 * (n + 1))
                if nxt is not None:
                    load(mk[:], A["t_k"][nxt], "cell_k")
                    load(C0[:], A["C0"][nxt], "cell_c")
                    act.wait_ge(S("cell_y"), 4 * (n + 1))
                    load(sz[:], A["t_z"][nxt], "cell_z")
                    load(xc[:], A["t_xc"][nxt], "cell_xc")
            store(A["o_n"], nout[:], "stored")
            act.wait_ge(S("stored"), 16 * 6)
            attention(1)
            before_projection(5, "mlp1")
            norm_rstd(5, power=2)
            squares(6, range(DT))
            rstd(GR["final_norm"], rs)
            for i in range(2):
                act.wait_ge(S("y_ready"), i + 1)
                store(A["o_y"][:, 4 * i:4 * i + 4, :], x[:, 4 * i:4 * i + 4, :], "stored")
            act.wait_ge(S("stored"), 16 * 8)

        @block.vector
        def _(v):
            ch = Chain(v, S("dve_step"))
            tt, stt, ts = v.tensor_tensor, v.scalar_tensor_tensor, v.tensor_scalar
            MUL, ADD, SUB = ALU.mult, ALU.add, ALU.subtract

            def add_squares(i, kks):
                for kk in kks:
                    v.wait_ge(S("sq_ready"), 8 * i + kk + 1)
                    if kk == 0:
                        if i:
                            group_ready(v, GR[NORM_AT[i - 1]])
                        ins = v.tensor_copy(ss[:], tm[:, 0, :])
                    else:
                        ch.sync()
                        ins = tt(ss[:], ss[:], tm[:, kk % 2, :], ADD)
                    ch.mark(ins, S("sq_used"))
                if kk == DT - 1:
                    v.sem_inc(S("squares_ready"), 1)

            rcount = [0]

            def rstd_ready():
                rcount[0] += 1
                v.wait_ge(S("rstd_ready"), rcount[0])

            def low(i, gain, kks):
                for kk in kks:
                    v.wait_ge(S("xn_hi"), 8 * i + kk + 1)
                    stt(xnl[:, kk, :], x[:, kk, :], col(gain, kk), xnh[:, kk, :].bitcast(F32), MUL, SUB)\
                        .then_inc(S("xn_ready"), 1)

            def halves(dst, j):
                return [dst[:, j, 0:HALF], dst[:, j, HALF:T]]

            v.wait_ge(S("consts"), 1)
            v.wait_ge(S("par_loaded"), 16)
            low(0, "mix0", range(DT))
            add_squares(0, range(DT))
            v.wait_ge(S("s5_dt"), 1)
            ch.mark(tt(sp[:, 1, :], col("a_re", 0, 16), sp[:, 0, :], MUL))
            ch.mark(tt(sp[:, 6, :], col("a_im", 0, 16), sp[:, 0, :], MUL))
            ch.sync()
            ch.mark(ts(sp[:, 7, :], sp[:, 6, :], 1.0 / TWO_PI, ROUND, MUL, ADD))
            ch.sync()
            ch.mark(ts(sp[:, 7, :], sp[:, 7, :], -ROUND, None, ADD))
            for c in (PI_HI, PI_MID, PI_LO):
                ch.sync()
                ch.mark(stt(sp[:, 6, :], sp[:, 7, :], -c, sp[:, 6, :], MUL, ADD))
            ch.sync()
            LIM = 3.1415925
            ts(sp[:, 2, :], sp[:, 6, :], LIM, -LIM, ALU.min, ALU.max).then_inc(S("s5_arg"), 1)

            RS = (rs[:, 0:HALF], rs[:, HALF:T])

            def evac_u(i):
                g = GR["rs", "u", i]
                group_ready(v, g)
                for m in range(2):
                    for b in range(2):
                        ins = tt(halves(u, 2 * i + m)[b], bank(g, 2 * m + b)[:, 0:HALF], RS[b], MUL)
                ch.mark(ins, free[g % 2])

            def evac_rope(w, i):
                part, dst = (("q", q), ("k", k))[w]
                g = GR["rs", part, i]
                v.wait_ge(S("swap_ready"), 2 * w + i + 1)
                v.wait_ge(S("const_loaded"), 16 * 9)
                for m in range(2):
                    for b in range(2):
                        hs_ = slice(HALF * b, HALF * b + HALF)
                        ch.mark(tt(halves(dst, 2 * i + m)[b], bank(g, 2 * m + b)[:, 0:HALF], rope[:, 0, hs_], MUL))
                        ch.mark(tt(sw[:, 2 * m + b, :], sw[:, 2 * m + b, :], rope[:, 1, hs_], MUL))
                ch.sync()
                v.sem_inc(free[g % 2], 1)
                for m in range(2):
                    for b in range(2):
                        ins = tt(halves(dst, 2 * i + m)[b], halves(dst, 2 * i + m)[b], sw[:, 2 * m + b, :], ADD)
                ch.mark(ins, S("swap_used"))
                if i:
                    v.sem_inc(S("rope_done"), 1)

            rstd_ready()
            evac_u(0)
            v.wait_ge(S("const_loaded"), 16 * 9)
            for w in range(2):
                ch.mark(tt(rope[:, w, :], rope[:, w, :], rs[:], MUL))
            evac_u(1)
            v.memset(u[:, :, T:TP + P], 0.0)
            v.wait_ge(S("s5_trig"), 1)
            R = lambda j: sp[:, j, :]
            are, aim = col("a_re", 0, 16), col("a_im", 0, 16)

            def step(*ops):
                for o in ops:
                    ch.mark(o())
                ch.sync()

            step(lambda: stt(R(6), R(5), -2.0, R(5), MUL, MUL), lambda: tt(R(7), are, are, MUL), lambda: tt(R(8), aim, aim, MUL))
            step(lambda: ts(R(6), R(6), 1.0, None, ADD), lambda: tt(R(7), R(7), R(8), ADD))
            step(lambda: tt(R(9), R(3), R(6), MUL), lambda: tt(R(10), R(3), R(4), MUL), lambda: v.reciprocal(R(7), R(7)))
            step(lambda: ts(R(8), R(9), -1.0, None, ADD))
            step(lambda: tt(R(11), R(8), are, MUL), lambda: tt(R(12), R(10), aim, MUL),
                 lambda: tt(R(13), R(10), are, MUL), lambda: tt(R(14), R(8), aim, MUL))
            step(lambda: tt(R(11), R(11), R(12), ADD), lambda: tt(R(13), R(13), R(14), SUB))
            step(lambda: tt(R(11), R(11), R(7), MUL), lambda: tt(R(13), R(13), R(7), MUL))
            v.wait_ge(S("const_loaded"), 16 * 9)
            fre = R(11).unsqueeze(2).to_broadcast([P, S5_TILES, 32])
            fim = R(13).unsqueeze(2).to_broadcast([P, S5_TILES, 32])
            zt = sq[:, 0:512].rearrange("p (s c) -> p s c", s=S5_TILES)
            step(lambda: tt(bb[:, 0], bz[:, 0], fre, MUL), lambda: tt(zt, bz[:, 1], fim, MUL))
            step(lambda: tt(bb[:, 0], bb[:, 0], zt, SUB))
            step(lambda: tt(bb[:, 1], bz[:, 1], fre, MUL), lambda: tt(zt, bz[:, 0], fim, MUL))
            step(lambda: tt(bb[:, 1], bb[:, 1], zt, ADD), lambda: ts(Cm[:, 1], Cm[:, 1], -1.0, None, MUL))
            v.sem_inc(S("bb_ready"), 1)
            evac_rope(0, 0)
            evac_rope(0, 1)
            step(lambda: v.memset(ctab[:, :, 0:1], 1.0), lambda: v.memset(stab[:, :, 0:1], 0.0),
                 lambda: v.tensor_copy(R(15), R(6)), lambda: v.tensor_copy(R(16), R(4)))

            def doubling(n):
                pc = R(15).unsqueeze(2).to_broadcast([P, S5_TILES, n])
                ps_ = R(16).unsqueeze(2).to_broadcast([P, S5_TILES, n])
                c0, s0, c1, s1 = ctab[:, :, 0:n], stab[:, :, 0:n], ctab[:, :, n:2 * n], stab[:, :, n:2 * n]
                t = sw[:].rearrange("p a t -> p (a t)")[:, 0:S5_TILES * n].rearrange("p (s t) -> p s t", s=S5_TILES)
                step(lambda: tt(c1, c0, pc, MUL), lambda: tt(t, s0, ps_, MUL))
                step(lambda: tt(c1, c1, t, SUB))
                step(lambda: tt(s1, c0, ps_, MUL), lambda: tt(t, s0, pc, MUL))
                step(lambda: tt(s1, s1, t, ADD), lambda: tt(R(17), R(15), R(15), MUL), lambda: tt(R(18), R(16), R(16), MUL),
                     lambda: stt(R(19), R(15), 2.0, R(16), MUL, MUL))
                step(lambda: tt(R(15), R(17), R(18), SUB), lambda: v.tensor_copy(R(16), R(19)))

            evac_rope(1, 0)
            evac_rope(1, 1)
            for i in range(2):
                g = GR["rs", "v", i]
                group_ready(v, g)
                for t, (b, c0) in enumerate([(0, 0), (1, 0), (2, 0), (3, 0), (3, 256)]):
                    r = P if t < NTB else TS
                    ins = ts(vt[0:r, t, 256 * i:256 * i + 256], bank(g, b)[0:r, c0:c0 + 256], rsc[0:r, t:t + 1], None, MUL)
                ch.mark(ins, free[g % 2])
                if i == 0:
                    for n in (1, 2, 4, 8, 16, 32, 64):
                        doubling(n)
            for i in range(2):
                g = GR["rs", "g", i]
                group_ready(v, g)
                for b in range(4):
                    ins = tt(halves(gt_, 2 * i + b // 2)[b % 2], bank(g, b)[:, 0:HALF], RS[b % 2], MUL)
                ch.mark(ins, free[g % 2], S("g_scaled"))
            g = GR["s5B"]
            group_ready(v, g)
            for c in range(2):
                ins = v.tensor_copy(BT[:, c].rearrange("p j s -> p (j s)"), bank(g, c))
            ch.mark(ins, free[g % 2], S("s5_const"))
            for h in range(RET_H):
                g = GR["ret", h, "score"]
                group_ready(v, g)
                if h:
                    group_ready(v, GR["ret", h - 1, "out"])
                for j in range(NTB):
                    w = TP - P * j
                    ins = tt(Wm[:, blk(j):blk(j) + w], bank(g, j)[:, 0:w], dec[:, h, 0:w], MUL)
                group_freed(ins, g)
                g = GR["ret", h, "aux"]
                group_ready(v, g)
                tt(Ws[:], bank(g, 0)[0:TS, 0:TS], dec[0:TS, h, 0:TS], MUL)
                tt(qw[:], q[:, h, TP:T], wq64[:, h, :], MUL)
                for j in range(NTB):
                    at = TP - 1 - P * j
                    ts(kt[:, j, :], bank(g, 1)[:, P * j:P * j + P], dec[:, h, at:at + 1], None, MUL)
                ins = ts(kt[0:TS, NTB, :], bank(g, 2)[0:TS, 0:P], dec[0:TS, h, TS - 1:TS], None, MUL)
                ch.mark(ins, free[g % 2], S("ret_w"))
                g = GR["ret", h, "out"]
                group_ready(v, g)
                ch.mark(v.tensor_copy(q[:, h, 0:TP], bank(g, 0)))
                ins = v.tensor_copy(q[:, h, TP:T], bank(g, 1)[:, 0:TS])
                ch.mark(ins, S("ret_o"))
                v.tensor_copy(retp[:, h, :], bank(g, 2)[:, 0:P])
                ins = stt(S0[:, h, :], S0[:, h, :], float(GAMMA[h] ** TS), bank(g, 3)[:, 0:P], MUL, ADD)
                ch.mark(ins, free[g % 2], S("ret_state"))
                g = GR["ret", h, "mean"]
                group_ready(v, g)
                for b in range(2):
                    ins = tt(halves(q, h)[b], halves(q, h)[b], bank(g, b)[:, 0:HALF], SUB)
                    ch.mark(ins)
                ch.sync()
                v.sem_inc(free[g % 2], 1)
                v.sem_inc(S("ret_c"), 1)
                if h == 0:
                    v.wait_ge(S("g_silu"), 2)
                    group_ready(v, GR["rs", "g", 1])
                rstd_ready()
                ch.sync()
                step(lambda: stt(tm[:, 0, :], q[:, h, :], col("ret_gn", h), rs[:], MUL, MUL))
                step(lambda: tt(tm[:, 1, :], tm[:, 0, :], gt_[:, h, :], MUL))
                step(lambda: v.tensor_copy(xnh[:, h, :], tm[:, 1, :]))
                step(lambda: tt(xnl[:, h, :], tm[:, 1, :], xnh[:, h, :].bitcast(F32), SUB))
            v.sem_inc(S("ret_end"), 1)

            for kk in range(DT):
                v.wait_ge(S("msq_ready"), kk + 1)
                if kk == 0:
                    ins = v.tensor_copy(mss[:], msq[:, 0, :])
                else:
                    ch.sync()
                    ins = tt(mss[:], mss[:], msq[:, kk % 2, :], ADD)
                ch.mark(ins, S("msq_used"))
            ch.sync()
            v.sem_inc(S("mem_squares"), 1)
            rstd_ready()

            def mem_split(l):
                if l:
                    group_ready(v, GR["mem", 0, "v", 3])
                for kk in range(DT):
                    step(lambda: stt(tm[:, kk % 2, 0:MEM], memx[:, kk, :], col(f"mem{l}", kk), mrs[:], MUL, MUL))
                    step(lambda: v.tensor_copy(mnh[:, kk, :], tm[:, kk % 2, 0:MEM]))
                    step(lambda: tt(mnl[:, kk, :], tm[:, kk % 2, 0:MEM], mnh[:, kk, :].bitcast(F32), SUB))
                v.sem_inc(S("mem_ready"), 1)

            mem_split(0)
            step(lambda: v.tensor_copy(rt[:], R(3).unsqueeze(2).to_broadcast([P, S5_TILES, P])))
            step(lambda: v.memset(rt[:, :, 0:1], 0.0))
            flat = lambda a: a.rearrange("p s t -> p (s t)")

            def s5_y(n):
                c, hf = UNITS[n]
                g = GR["s5y", n]
                group_ready(v, g)
                w = P if c < NTB else TS
                for a in range(2):
                    j = 2 * hf + a
                    ins = stt(u[:, j, P * c:P * c + w], u[:, j, P * c:P * c + w], col("s5_d", j), bank(g, a)[:, 0:w], MUL, ADD)
                ch.mark(ins, free[g % 2], S("s5_y"))

            for n, (c, hf) in enumerate(UNITS):
                g = GR["s5u", n]
                t8 = slice(8 * hf, 8 * hf + 8)
                cc, sc = ctab[:, t8, :], stab[:, t8, :]
                grp = psum[:, 4 * (g % 2):4 * (g % 2) + 4, :].rearrange("p i (c a t) -> p i c a t", c=2, a=2)
                re, im = grp[:, :, 0], grp[:, :, 1]
                ia = lambda z: z.rearrange("p (a i) t -> p i a t", i=4)
                group_ready(v, g)
                if c:
                    if c < NTB:
                        f = (n - 2) % 2
                        hr_, hi_ = he[:, f, :, P - 1:P].rearrange("p s o -> p (s o)"), hf_[:, f, :, P - 1:P].rearrange("p s o -> p (s o)")
                    else:
                        hr_, hi_ = col("h0_re", 8 * hf, 8), col("h0_im", 8 * hf, 8)
                    ar, ai = sp[:, 9, t8], sp[:, 10, t8]
                    step(lambda: tt(sp[:, 20, 0:8], ar, hr_, MUL), lambda: tt(sp[:, 21, 0:8], ai, hi_, MUL),
                         lambda: tt(sp[:, 22, 0:8], ar, hi_, MUL), lambda: tt(sp[:, 23, 0:8], ai, hr_, MUL))
                    step(lambda: tt(sp[:, 20, 8:16], sp[:, 20, 0:8], sp[:, 21, 0:8], SUB),
                         lambda: tt(sp[:, 22, 8:16], sp[:, 22, 0:8], sp[:, 23, 0:8], ADD))
                step(lambda: tt(ia(za[:]), re, ia(cc), MUL), lambda: tt(ia(zb[:]), im, ia(sc), MUL))
                step(lambda: tt(za[:], za[:], zb[:], ADD), lambda: tt(ia(zc[:]), im, ia(cc), MUL))
                step(lambda: tt(ia(zb[:]), re, ia(sc), MUL))
                v.sem_inc(free[g % 2], 1)
                step(lambda: tt(zc[:], zc[:], zb[:], SUB))
                if c:
                    step(lambda: tt(za[:, :, 0:1].rearrange("p s o -> p (s o)"), za[:, :, 0:1].rearrange("p s o -> p (s o)"),
                                    sp[:, 20, 8:16], ADD),
                         lambda: tt(zc[:, :, 0:1].rearrange("p s o -> p (s o)"), zc[:, :, 0:1].rearrange("p s o -> p (s o)"),
                                    sp[:, 22, 8:16], ADD))
                rt8 = flat(rt[:, t8, :])
                step(lambda: v.tensor_tensor_scan(flat(za[:]), rt8, flat(za[:]), 0.0, MUL, ADD),
                     lambda: v.tensor_tensor_scan(flat(zc[:]), rt8, flat(zc[:]), 0.0, MUL, ADD))
                E_, F_ = he[:, n % 2], hf_[:, n % 2]
                if n >= 2:
                    group_ready(v, GR["s5y", n - 2])
                step(lambda: tt(zb[:], za[:], cc, MUL), lambda: tt(E_, zc[:], sc, MUL))
                step(lambda: tt(E_, zb[:], E_, SUB))
                step(lambda: tt(zb[:], za[:], sc, MUL), lambda: tt(F_, zc[:], cc, MUL))
                step(lambda: tt(F_, zb[:], F_, ADD))
                v.sem_inc(S("s5_h"), 1)
                if c >= NTB - 1:
                    at = P - 1 if c < NTB else TS - 1
                    r = 2 * (c - NTB + 1)
                    for y in range(2):
                        v.tensor_copy(fin5[:, r + y, t8], (E_, F_)[y][:, :, at:at + 1].rearrange("p s o -> p (s o)"))
                if n:
                    s5_y(n - 1)
                if n == 4:
                    mem_split(1)
            s5_y(len(UNITS) - 1)
            for j in range(4):
                v.wait_ge(S("gelu"), j + 1)
                step(lambda: v.tensor_copy(gh[:, j, :], u[:, j, 0:T]))
                step(lambda: tt(gl[:, j, :], u[:, j, 0:T], gh[:, j, :].bitcast(F32), SUB))
            v.sem_inc(S("glu_in"), 1)
            group_ready(v, GR["mem", 1, "v", 3])
            for a in range(2):
                v.wait_ge(S("sg_ready"), a + 1)
                for m in range(2):
                    j = 2 * a + m
                    step(*[lambda b=b: tt(tm[:, m, HALF * b:HALF * b + HALF], halves(u, j)[b], sg[:, 2 * m + b, :], MUL)
                           for b in range(2)])
                    step(lambda: v.tensor_copy(xnh[:, 4 + j, :], tm[:, m, :]))
                    step(lambda: tt(xnl[:, 4 + j, :], tm[:, m, :], xnh[:, 4 + j, :].bitcast(F32), SUB))
                v.sem_inc(S("sg_used"), 1)
            v.sem_inc(S("rs_y"), 1)

            def add_residual(g, i):
                group_ready(v, g)
                for m in range(2):
                    for b in range(2):
                        ins = tt(halves(x, 2 * i + m)[b], halves(x, 2 * i + m)[b], bank(g, 2 * m + b)[:, 0:HALF], ADD)
                    ch.mark(ins)
                ch.sync()
                v.sem_inc(free[g % 2], 1)
                v.sem_inc(S("x_tile"), 2)

            def residual_and_norm(groups, i, gain):
                for j in range(4):
                    add_residual(groups[j], j)
                    if j in (1, 2):
                        add_squares(i, (2 * j - 2, 2 * j - 1))
                    if j == 2:
                        add_squares(i, (4, 5))
                        low(i, gain, (0, 1))
                low(i, gain, range(2, 8))
                add_squares(i, (6, 7))

            v.sem_inc(S("arena_free"), 1)
            v.wait_ge(S("x_again"), 16)
            residual_and_norm([GR["rs_out", i] for i in range(4)], 1, "cross0")

            def attention(l):
                rstd_ready()
                def copy_xq(i):
                    g = GR["xq", l, i]
                    group_ready(v, g)
                    for m in range(2):
                        for b in range(2):
                            ins = tt(halves(xq, 2 * i + m)[b], bank(g, 2 * m + b)[:, 0:HALF], RS[b], MUL)
                    ch.mark(ins, free[g % 2], S("xq_ready"))

                def row_max(x2):
                    g = GR["att", l, "score", x2]
                    group_ready(v, g)
                    r = P if x2 < 2 else TS
                    for t in range(4):
                        if x2 < 2:
                            ch.mark(v.tensor_reduce(mx[:, x2, 2 * t:2 * t + 2], bank(g, t).rearrange("p (h m) -> p h m", h=2),
                                                    AX.X, ALU.max))
                        else:
                            ch.mark(v.tensor_reduce(mx[0:r, x2, t:t + 1], bank(g, t)[0:r, 0:MEM], AX.X, ALU.max))
                    w = 8 if x2 < 2 else 4
                    ch.sync()
                    ins = ts(nm[0:r, x2, 0:w], mx[0:r, x2, 0:w], -1.0 / 16, None, MUL)
                    ch.mark(ins, S("row_max"))

                def prob(x2):
                    v.wait_ge(S("exp_done"), 3 * l + x2 + 1)
                    r, w = (P, 8) if x2 < 2 else (TS, 4)
                    step(lambda: v.reciprocal(sm[0:r, x2, 0:w], sm[0:r, x2, 0:w]))
                    dst = pr[:, x2] if x2 < 2 else prs
                    for j in range(w):
                        ins = ts(dst[0:r, j, :], dst[0:r, j, :], sm[0:r, x2, j:j + 1], None, MUL)
                    ch.mark(ins, S("prob"))

                def copy_pT(x2):
                    g = GR["att", l, "pT", x2]
                    group_ready(v, g)
                    if x2 < 2:
                        if x2 == 1:
                            group_ready(v, GR["att", l, "pv", 0])
                        for b in range(4):
                            ins = v.tensor_copy(pT[:, b // 2, b % 2, :], bank(g, b))
                    else:
                        ins = v.tensor_copy(pTs[:].rearrange("p h t -> p (h t)"), bank(g, 0))
                    ch.mark(ins, free[g % 2], S("pT"))

                def split_o(x2):
                    g = GR["att", l, "pv", x2]
                    group_ready(v, g)
                    if x2 < 2:
                        for b in range(4):
                            ch.mark(v.tensor_copy(xnh[:, 4 * x2 + b, 0:TP], bank(g, b)))
                        ch.sync()
                        for b in range(4):
                            ins = tt(xnl[:, 4 * x2 + b, 0:TP], bank(g, b), xnh[:, 4 * x2 + b, 0:TP].bitcast(F32), SUB)
                    else:
                        pb = bank(g, 0).rearrange("p (f t) -> p f t", f=DT)
                        ch.mark(v.tensor_copy(xnh[:, :, TP:T], pb))
                        ch.sync()
                        ins = tt(xnl[:, :, TP:T], pb, xnh[:, :, TP:T].bitcast(F32), SUB)
                    ch.mark(ins, free[g % 2], S("att_o"))

                copy_xq(0)
                copy_xq(1)
                row_max(0)
                copy_xq(2)
                prob(0)
                copy_xq(3)
                copy_pT(0)
                row_max(1)
                split_o(0)
                row_max(2)
                prob(1)
                copy_pT(1)
                prob(2)
                copy_pT(2)
                split_o(1)
                split_o(2)
                residual_and_norm([GR["xo", l, i] for i in range(4)], 3 * l + 2, f"mlp{l}")

            def mlp(l):
                rstd_ready()
                g0 = GR["mlp", l, 0, "up", 0]
                with v.Fori(0, 4) as a:
                    ch.loop(a, 4 * 12 + 4)
                    for i in range(4):
                        g = g0 + i
                        group_ready(v, g, a * 4)
                        B = [bank(g, b)[:, 0:HALF] for b in range(4)]
                        for b in range(4):
                            ch.mark(stt(hr[:, b, :], B[b], 0.0, RS[b % 2], ALU.max, MUL))
                        ch.sync()
                        for b in range(4):
                            ins = stt(hs[:, b, :], B[b], 0.0, hr[:, b, :], ALU.max, MUL)
                            ch.mark(ins)
                        ch.sync()
                        v.sem_inc(free[g % 2], 1)
                        for b in range(4):
                            ch.mark(v.tensor_copy(halves(hh, 2 * i + b // 2)[b % 2], hs[:, b, :]))
                        ch.sync()
                        for b in range(4):
                            h_ = halves(hh, 2 * i + b // 2)[b % 2]
                            ins = tt(halves(hl, 2 * i + b // 2)[b % 2], hs[:, b, :], h_.bitcast(F32), SUB)
                        ins.then_inc(S("hidden_ready"), 1)
                    for i in range(4):
                        g = g0 + 4 + i
                        group_ready(v, g, a * 4)
                        for m in range(2):
                            for b in range(2):
                                xx = halves(x, 2 * i + m)[b]
                                ins = tt(xx, xx, bank(g, 2 * m + b)[:, 0:HALF], ADD)
                        ch.mark(ins)
                        ch.sync()
                        v.sem_inc(free[g % 2], 1)
                        v.sem_inc(S("x_mlp"), 2)
                    ch.endloop(4)

            attention(0)
            mlp(0)
            low(3, "mix1", range(DT))
            add_squares(3, range(DT))
            rstd_ready()
            SEG = ((0, HALF, 0, 3, 0), (1, TP - HALF, 0, HALF + 3, HALF), (1, TS, TP - HALF, TP + 6, TP))
            v.memset(xm[:, :, 0:3], 0.0)
            for h in range(ML_H):
                for i in range(2):
                    g = GR["ml", h, "xm", i]
                    group_ready(v, g)
                    for m in range(2):
                        for b, w, c0, c1, t0 in SEG:
                            ins = tt(xm[:, 2 * i + m, c1:c1 + w], bank(g, 2 * m + b)[:, c0:c0 + w], rs[:, t0:t0 + w], MUL)
                    ch.mark(ins, free[g % 2], S("xm_ready"))

                def scale_z(i):
                    g = GR["ml", h, "z", i]
                    group_ready(v, g)
                    for b in range(4):
                        ins = tt(halves(mv, 2 * i + b // 2)[b % 2], bank(g, b)[:, 0:HALF], RS[b % 2], MUL)
                    ch.mark(ins, free[g % 2], S("z_scaled"))

                a, _ = PCOL["conv_cache"]
                cc = par[:, a + 12 * h:a + 12 * h + 12].rearrange("p (t k) -> p t k", k=3)
                ch.mark(v.tensor_copy(xm[:, :, TP + 3:TP + 6], cc))
                v.tensor_copy(cst[:, 0, 4 * h:4 * h + 4, :], xm[:, :, TP:TP + 3])
                v.tensor_copy(cst[:, 1, 4 * h:4 * h + 4, :], xm[:, :, T + 3:T + 6])
                ch.sync()
                if h:
                    v.wait_ge(S("xc_spilled"), 16 * h)
                    v.wait_ge(S("xc_split"), 4 * h)
                for t in range(ML_T):
                    for tap in range(4):
                        for d0, s0, w in ((0, 0, TP), (TP, TP + 3, TS)):
                            src, dst = xm[:, t, s0 + tap:s0 + tap + w], xc[:, t, d0:d0 + w]
                            wc = col("conv_w", 16 * h + 4 * t + tap)
                            if tap == 0:
                                ins = ts(dst, src, wc, col("conv_b", 4 * h + t), MUL, ADD)
                            else:
                                ins = stt(dst, src, wc, dst, MUL, ADD)
                            ch.mark(ins)
                        ch.sync()
                    v.sem_inc(S("conv_done"), 1)
                if h:
                    v.wait_ge(S("v_spilled"), 16 * h)
                scale_z(0)
                v.wait_ge(S("xm_hi"), h + 1)
                tt(xml[:, :, 0:TP], xm[:, :, 3:3 + TP], xmh[:, :, 0:TP].bitcast(F32), SUB)
                tt(xml[:, :, TP:T], xm[:, :, TP + 6:T + 6], xmh[:, :, TP:T].bitcast(F32), SUB).then_inc(S("xm_split"), 1)
                for t in range(ML_T):
                    v.wait_ge(S("xc_hi"), 4 * h + t + 1)
                    tt(xcl[:, t, :], xc[:, t, :], xch[:, t, :].bitcast(F32), SUB).then_inc(S("xc_split"), 1)
                scale_z(1)
                for w, (part, buf) in enumerate((("q", mq), ("k", mk), ("v", mv))):
                    if w == 2:
                        v.wait_ge(S("z_spilled"), 16 * (h + 1))
                    elif h:
                        v.wait_ge(S(part + "_spilled"), 16 * h)
                        group_ready(v, GR["gate", h - 1])
                    for i in range(2):
                        g = GR["ml", h, part, i]
                        group_ready(v, g)
                        for b in range(4):
                            ins = v.tensor_copy(halves(buf, 2 * i + b // 2)[b % 2], bank(g, b)[:, 0:HALF])
                        ch.mark(ins, free[g % 2], S("qkv_ready"))
                g = GR["gate", h]
                group_ready(v, g)
                for b in range(2):
                    c = slice(HALF * b, HALF * b + HALF)
                    if h == 0:
                        ins = ts(gt[:, c], bank(g, b)[0:36, 0:HALF], par[0:36, PCOL["b_gates"][0]:PCOL["b_gates"][0] + 1], None, ADD)
                    else:
                        ins = tt(gt[:, c], gt[:, c], bank(g, b)[0:36, 0:HALF], ADD)
                    ch.mark(ins)
                ch.sync()
                v.sem_inc(free[g % 2], 1)
                v.sem_inc(S("gates_done"), 1)
            ig = gt[0:4, :]
            step(lambda: v.memset(zrow[:], 0.0))
            v.wait_ge(S("log1p"), 1)
            step(lambda: stt(lrow[:], frow[:], 0.0, erow[:], ALU.min, SUB))
            scan = v.tensor_tensor_scan
            m0c = par[0:4, PCOL["m0"][0]:PCOL["m0"][0] + 1]
            step(lambda: scan(mrow[:, 0:TP], lrow[:, 0:TP], ig[:, 0:TP], 0.0, ADD, ALU.max),
                 lambda: scan(mrow[:, TP:T], lrow[:, TP:T], ig[:, TP:T], m0c, ADD, ALU.max),
                 *[lambda j=j: scan(brow[:, blk(j):blk(j + 1)], lrow[:, P * j:TP], zrow[:, P * j:TP], 0.0, ADD, ADD)
                   for j in range(NTB)],
                 lambda: scan(brow[:, SCW:SCW + TS], lrow[:, TP:T], zrow[:, 0:TS], 0.0, ADD, ADD))
            for j in range(NTB):
                ch.mark(tt(rrow[:, blk(j):blk(j + 1)], brow[:, blk(j):blk(j + 1)], mrow[:, P * j:TP], SUB))
                ch.mark(tt(arow[:, j, :], ig[:, P * j:P * j + P], brow[:, blk(j):blk(j) + P], SUB))
            ch.mark(tt(rrow[:, SCW:SCW + TS], brow[:, SCW:SCW + TS], mrow[:, TP:T], SUB))
            ch.mark(tt(arow[:, NTB, 0:TS], ig[:, TP:T], brow[:, SCW:SCW + TS], SUB))
            ch.mark(v.tensor_copy(mo[:, 0:1], mrow[:, TP - 1:TP]))
            ch.mark(v.tensor_copy(mo[:, 1:2], mrow[:, T - 1:T]))
            ch.sync()
            v.sem_inc(S("rows_ready"), 1)
            g = GR["acol"]
            group_ready(v, g)
            ch.mark(v.tensor_copy(acol[:, 0:16], bank(g, 0)[:, 0:16]))
            ch.mark(v.tensor_copy(acol[0:TS, 16:20], bank(g, 0)[0:TS, 16:20]))
            ch.sync()
            v.sem_inc(free[g % 2], 1)
            v.sem_inc(S("acol_ready"), 1)
            for x_ in ("cell_q", "cell_k", "cell_v", "cell_xc"):
                v.sem_inc(S(x_), 1)
            SC = float(ML_DH) ** -0.5
            for n, h in enumerate(CELL_ORDER):
                v.wait_ge(S("cell_w"), n + 1)
                if n:
                    group_ready(v, GR["cell", CELL_ORDER[n - 1], "n"])
                    v.wait_ge(S("cell_q"), 16 * n + 1)
                else:
                    v.wait_ge(S("rows_exp"), 1)
                for j in range(NTB):
                    at = blk(j + 1) - 1
                    ch.mark(ts(wcol[:, j:j + 1], wt[:, at:at + 1], SC, None, MUL))
                ch.mark(ts(wcol[0:TS, 4:5], wts[:, TS - 1:TS], SC, None, MUL))
                ch.sync()
                v.sem_inc(S("cell_wcol"), 1)
                g = GR["cell", h, "score"]
                group_ready(v, g)
                for j in range(NTB):
                    seg = wt[:, blk(j):blk(j + 1)]
                    ins = stt(seg, bank(g, j)[:, 0:TP - P * j], SC, seg, MUL, MUL)
                ch.mark(ins, free[g % 2], S("cell_pt"))
                for d in range(ML_T):
                    ts(n0b[:, d, :], ones[:], col("n0", 4 * h + d), None, MUL)
                g = GR["cell", h, "smp"]
                group_ready(v, g)
                ins = tt(qs[:], mq[:, :, TP:T], siB[:].unsqueeze(1).to_broadcast([P, ML_T, TS]), MUL)
                ch.mark(ins, S("cell_qs"))
                stt(wts[:], bank(g, 0)[0:TS, 0:TS], SC, wts[:], MUL, MUL)
                v.tensor_copy(vt5[:], bank(g, 1)[0:TS, :])
                ins = ts(kt5[:], bank(g, 2)[0:TS, :], wcol[0:TS, 4:5], None, MUL)
                ch.mark(ins, free[g % 2], S("cell_smp"))
                if h == 1:
                    add_residual(GR["ml_out", 1, 0], 0)
                v.wait_ge(S("cell_abs"), n + 1)
                step(lambda: tt(tm[:, 1, :], tm[:, 1, :], tm[:, 0, :], ALU.max))
                step(lambda: v.reciprocal(tm[:, 1, :], tm[:, 1, :]))
                v.wait_ge(S("cell_z"), 16 * (n + 1))
                step(lambda: tt(sz[:], sz[:], tm[:, 1, :].unsqueeze(1).to_broadcast([P, ML_T, T]), MUL))
                g = GR["cell", h, "den"]
                ins = tt(sz[:, :, TP:T], sz[:, :, TP:T], bank(g, 2)[:, 0:ML_T * TS].rearrange("p (e t) -> p e t", e=ML_T), MUL)
                ch.mark(ins, free[g % 2])
                if h == 1:
                    add_residual(GR["ml_out", 1, 1], 1)
                g = GR["cell", h, "num"]
                group_ready(v, g)
                for e in range(ML_T):
                    ins = tt(sz[:, e, 0:TP], sz[:, e, 0:TP], bank(g, e), MUL)
                ch.mark(ins, free[g % 2])
                step(lambda: tt(ss[:], sz[:, 0, :], sz[:, 1, :], ADD))
                step(lambda: tt(ss[:], ss[:], sz[:, 2, :], ADD))
                step(lambda: tt(ss[:], ss[:], sz[:, 3, :], ADD))
                v.sem_inc(S("cell_sum"), 1)
                g = GR["cell", h, "kvs"]
                group_ready(v, g)
                for d in range(ML_T):
                    ins = stt(C0[:, d, :], C0[:, d, :], siB[:, TS - 1:TS], bank(g, d), MUL, ADD)
                ch.mark(ins, free[g % 2], S("cell_cs"))
                g = GR["cell", h, "n"]
                group_ready(v, g)
                v.tensor_copy(nout[:, 0, 4 * h:4 * h + 4], bank(g, 0)[:, 0:4])
                ins = stt(nout[:, 1, 4 * h:4 * h + 4], col("n0", 4 * h, 4), siB[:, TS - 1:TS], bank(g, 0)[:, 4:8], MUL, ADD)
                ch.mark(ins, free[g % 2])
                if h == 1:
                    add_residual(GR["ml_out", 1, 2], 2)
                g = GR["cell", h, "mean"]
                group_ready(v, g)
                for b, (t0, t1) in enumerate(((0, HALF), (HALF, T))):
                    ins = tt(sz[:, :, t0:t1], sz[:, :, t0:t1], bank(g, b)[:, 0:HALF].unsqueeze(1).to_broadcast([P, ML_T, HALF]), SUB)
                    ch.mark(ins)
                ch.sync()
                v.sem_inc(free[g % 2], 1)
                v.sem_inc(S("cell_c0"), 1)
                for e in range(ML_T):
                    v.wait_ge(S("csq_ready"), 4 * n + e + 1)
                    if e == 0:
                        ins = v.tensor_copy(ss[:], tm[:, 0, :])
                    else:
                        ins = tt(ss[:], ss[:], tm[:, e % 2, :], ADD)
                    ch.mark(ins, S("csq_used"))
                v.sem_inc(S("cell_sum"), 1)
                if h == 1:
                    add_residual(GR["ml_out", 1, 3], 3)
                rstd_ready()
                if n == 2:
                    group_ready(v, GR["ml_out", 1, 3])
                v.wait_ge(S("cell_xc"), 16 * n + 1)
                for e in range(ML_T):
                    f, o = 4 * h + e, 4 * (h % 2) + e
                    step(lambda: stt(tm[:, 0, :], sz[:, e, :], col("ml_gn", f), rs[:], MUL, MUL))
                    step(lambda: stt(tm[:, 1, :], xc[:, e, :], col("ml_skip", f), tm[:, 0, :], MUL, ADD))
                    step(lambda: v.tensor_copy(xnh[:, o, :], tm[:, 1, :]))
                    step(lambda: tt(xnl[:, o, :], tm[:, 1, :], xnh[:, o, :].bitcast(F32), SUB))
                    v.sem_inc(S("cell_y"), 1)
            v.sem_inc(S("arena_free"), 1)
            residual_and_norm([GR["ml_out", 0, i] for i in range(4)], 4, "cross1")
            attention(1)
            mlp(1)
            add_squares(6, range(DT))
            rstd_ready()
            for kk in range(DT):
                ch.mark(stt(x[:, kk, :], x[:, kk, :], col("final", kk), rs[:], MUL, MUL))
                if kk % 4 == 3:
                    ch.sync()
                    v.sem_inc(S("y_ready"), 1)


INPUTS = {
    "w": [NSLAB, P, SLAB], "xT": [P, DT, T], "memT": [P, DT, MEM], "par": [P, NPAR], "rope": [P, 2, T],
    "decay": [P, RET_H, TP], "wq64": [P, RET_H, TS], "ident": [P, P], "ret0": [P, RET_H, P],
    "Bre": [P, S5_TILES, 32], "Bim": [P, S5_TILES, 32], "Cre": [P, S5_TILES, 32], "Cim": [P, S5_TILES, 32],
    "ckT": [2, P, DT, MEM], "cv": [2, P, 2, D],
    "gw": [P, 48, 36], "causal": [P, P], "sel": [4, ML_H, P], "C0": [ML_H, P, ML_T, ML_DH],
}
OUTPUTS = {
    "o_y": [P, DT, T], "o_retp": [P, RET_H, P], "o_rets": [P, RET_H, P], "o_s5": [P, 4, S5_TILES],
    "o_mkT": [2, P, DT, MEM], "o_mv": [2, P, 2, D],
    "o_cp": [ML_H, P, ML_T, ML_DH], "o_cs": [ML_H, P, ML_T, ML_DH], "o_n": [P, 2, 16], "o_m": [4, 2],
    "o_conv": [P, 2, 16, 3],
}
SCRATCH = {"t_q": [ML_H, P, ML_T, T], "t_k": [ML_H, P, ML_T, T], "t_v": [ML_H, P, ML_T, T], "t_xc": [ML_H, P, ML_T, T],
           "t_z": [ML_H, P, ML_T, T]}


def tiles(a):
    return np.ascontiguousarray(a.reshape(-1, P, a.shape[-1]).transpose(1, 0, 2))


def pack_weights(i):
    w = np.zeros((NSLAB, P, SLAB), np.float32)

    def slab(m, kg, cg, kts=DT, cols=256):
        b = m[kg * kts * P:(kg + 1) * kts * P, cg * cols:(cg + 1) * cols]
        return b.reshape(kts, P, cols).transpose(1, 0, 2).reshape(P, -1)

    at = {"q": 0, "k": 512, "v": 1024, "g": 1536, "u": 2048}
    for name, n in SLABS.items():
        if name[0] == "rs":
            m = i["rs_w_in"][0][:, at[name[1]]:at[name[1]] + 512]
            w[n] = slab(m, 0, name[2])
        elif name[0] == "mem":
            w[n] = slab(i["x_wk" if name[2] == "k" else "x_wv"][name[1]], 0, name[3])
        elif name == "glu":
            w[n] = slab(i["s5_w_glu"][0], 0, 0, 4, 512)
        elif name[0] == "rs_out":
            w[n] = slab(i["rs_w_out"][0], 0, name[1])
        elif name[0] in ("xq", "xo"):
            w[n] = slab(i["x_w" + name[0][1]][name[1]], 0, name[2])
        elif name[0] == "mlp":
            _, l, a, d, c = name
            w[n] = slab(i["mlp_w_up"][l], 0, 4 * a + c) if d == "up" else slab(i["mlp_w_down"][l], a, c)
        elif name[0] == "ml" and name[2] in ("xm", "z"):
            _, h, part, c = name
            w[n] = slab(i["ml_w_in"][0], 0, (8 if part == "z" else 0) + 2 * h + c)
        elif name[0] == "ml":
            w[n] = slab(i["ml_w" + name[2]][0][name[1]], 0, 0, 4, 512)
        elif name[0] == "ml_out":
            w[n] = slab(i["ml_w_out"][0], name[1], name[2])
    return w


def layout(i):
    i = {k: np.asarray(v) for k, v in i.items()}
    f = np.float32
    par = np.zeros((P, NPAR), f)

    def put(name, a):
        c, n = PCOL[name]
        par[:a.shape[0], c:c + n] = a.reshape(a.shape[0], n)

    vec = lambda a: a.reshape(-1, P).T
    for l in range(2):
        put(f"mix{l}", vec(i["norm_mix"][l]))
        put(f"cross{l}", vec(i["norm_cross"][l]))
        put(f"mlp{l}", vec(i["norm_mlp"][l]))
        put(f"mem{l}", vec(i["norm_mem"][l]))
    put("final", vec(i["norm_final"]))
    put("ret_gn", vec(i["ret_gn"][0]))
    put("s5_d", vec(i["s5_d"][0]))
    put("b_glu", vec(i["s5_b_glu"][0]))
    put("conv_w", i["ml_conv_w"][0].reshape(4, 16, P).transpose(2, 1, 0))
    put("conv_b", vec(i["ml_conv_b"][0]))
    put("ml_gn", vec(i["ml_gn"][0]))
    put("ml_skip", vec(i["ml_skip"][0]))
    put("a_re", i["s5_a_re"][0].reshape(16, P).T)
    put("a_im", i["s5_a_im"][0].reshape(16, P).T)
    put("log_dt", np.repeat(i["s5_log_dt"][0], 64).reshape(16, P).T)
    put("h0_re", i["state_s5_re"][0, 0].reshape(16, P).T)
    put("h0_im", i["state_s5_im"][0, 0].reshape(16, P).T)
    bg = np.zeros((36, 1), f)
    bg[0:4, 0], bg[32:36, 0] = i["ml_b_gates"][0][0:4], i["ml_b_gates"][0][4:8]
    put("b_gates", bg)
    put("m0", i["state_mlstm_m"][0, 0].reshape(4, 1))
    put("n0", i["state_mlstm_n"][0, 0].reshape(16, P).T)
    put("conv_cache", i["cache_mlstm_conv"][0, 0].reshape(3, 16, P).transpose(2, 1, 0))
    pos = np.concatenate([np.arange(TP), PAST + np.arange(TS)]).astype(f)
    inv = f(10000.0) ** (-np.arange(64, dtype=f) / f(64))
    ang = (pos[:, None] * inv[None, :]).astype(f).T
    cos, sin = np.cos(ang).astype(f), np.sin(ang).astype(f)
    rope = np.stack([np.concatenate([cos, cos]), np.concatenate([-sin, sin])], 1)
    lg = np.log1p(-np.exp2(-5.0 - np.arange(4)))
    d = np.arange(TP)[None, :] - np.arange(P)[:, None]
    decay = np.stack([np.where(d >= 0, np.exp(np.maximum(d, 0) * lg[h]) * P ** -0.5, 0) for h in range(4)], 1).astype(f)
    wq64 = np.broadcast_to(np.exp((np.arange(TS) + 1.0)[None, :] * lg[:, None]).astype(f), (P, 4, TS))

    def block_diag(a):
        z = np.zeros((16, 2, 64, 2, 16), f)
        a = a.reshape(16, 2, 64, 16)
        z[:, 0, :, 0], z[:, 1, :, 1] = a[:, 0], a[:, 1]
        return z.reshape(16, P, 32).transpose(1, 0, 2)

    gw = np.zeros((48, P, 36), f)
    g = i["ml_w_gates"][0].reshape(48, P, 8)
    gw[:, :, 0:4], gw[:, :, 32:36] = g[:, :, 0:4], g[:, :, 4:8]
    sel = np.zeros((4, 4, P), f)
    for h in range(4):
        sel[h, h] = 1
    out = {
        "w": pack_weights(i),
        "xT": tiles(np.concatenate([i["x_prompt"][0], i["x_sample"][0]]).T),
        "memT": tiles(i["mem_prompt"][0].T), "par": par, "rope": rope, "decay": decay, "wq64": wq64,
        "ident": np.eye(P, dtype=f), "ret0": i["state_ret"][0, 0].transpose(1, 0, 2),
        "Bre": block_diag(i["s5_b_re"][0]), "Bim": block_diag(i["s5_b_im"][0]),
        "Cre": block_diag(i["s5_c_re"][0].transpose(0, 2, 1)), "Cim": block_diag(i["s5_c_im"][0].transpose(0, 2, 1)),
        "ckT": np.stack([tiles(i["cache_mem_k"][l, 0].reshape(MEM, D).T) for l in range(2)]),
        "cv": np.stack([i["cache_mem_v"][l, 0].reshape(2, P, D).transpose(1, 0, 2) for l in range(2)]),
        "gw": gw.transpose(1, 0, 2), "causal": np.where(np.arange(P)[:, None] <= np.arange(P)[None, :], 0, NEG).astype(f),
        "sel": sel, "C0": i["state_mlstm_c"][0, 0].reshape(4, 4, P, 512).transpose(0, 2, 1, 3),
    }
    return {"in_" + k: np.ascontiguousarray(v) for k, v in out.items()}


def returned(r):
    y = r["o_y"].transpose(1, 0, 2).reshape(D, T).T
    s5 = r["o_s5"].transpose(1, 2, 0).reshape(4, 1, 1, 32, 64)
    ret = [r[n].transpose(1, 0, 2)[None, None] for n in ("o_retp", "o_rets")]
    mk = r["o_mkT"].transpose(0, 2, 1, 3).reshape(2, D, MEM).transpose(0, 2, 1).reshape(2, 1, MEM, 4, 256)
    mv = r["o_mv"].transpose(0, 2, 1, 3).reshape(2, 1, MEM, 4, 256)
    mc = [r[n].transpose(0, 2, 1, 3).reshape(1, 1, 4, 512, 512) for n in ("o_cp", "o_cs")]
    mn = r["o_n"].transpose(1, 2, 0).reshape(2, 1, 1, 4, 512)
    mm = r["o_m"].T.reshape(2, 1, 1, 4)
    cv = r["o_conv"].transpose(1, 3, 2, 0).reshape(2, 1, 1, 3, 2048)
    c = np.ascontiguousarray
    return tuple(c(a) for a in (y[None, :TP], y[None, TP:], ret[0], s5[0], s5[1], mc[0], mn[0], mm[0], cv[0], mk, mv,
                                ret[1], s5[2], s5[3], mc[1], mn[1], mm[1], cv[1]))


def kernel(**inputs):
    import concourse.bacc as bacc
    from concourse.bass_utils import run_bass_kernel_spmd as run

    nc = bacc.Bacc("TRN2", target_bir_lowering=False, num_devices=1)
    A = {}
    for n, sh in INPUTS.items():
        A[n] = nc.dram_tensor("in_" + n, sh, F32, kind="ExternalInput").ap()
    for n, sh in OUTPUTS.items():
        A[n] = nc.dram_tensor(n, sh, F32, kind="ExternalOutput").ap()
    for n, sh in SCRATCH.items():
        A[n] = nc.dram_tensor(n, sh, F32, kind="Internal").ap()
    program(nc, A)
    r = run(nc, [layout(inputs)], core_ids=[0])
    return returned(r.results[0])
```

```python
from contextlib import ExitStack

import numpy as np

import concourse.bass as bass
from concourse import mybir

F32 = mybir.dt.float32
F32R = mybir.dt.float32r
ALU = mybir.AluOpType
ACT = mybir.ActivationFunctionType
AX = mybir.AxisListType

P = 128
D = 1024
DT = D // P
TP, TS = 512, 64
T = TP + TS
HALF = T // 2
NTB = TP // P
PAST = 1024
RET_H = 4
S5_TILES = 16
NCH = NTB + 1
ML_H, ML_T = 4, 4
ML_DH = ML_T * P
LATE_Z = (3, "z", 1)
CELL_ORDER = (3, 2, 1, 0)
ATT_ORDER = (0, 2, 1)
OUT_BEFORE = ("den", "num", "n", "mean")
MEM = 256
XH = 4
SLAB = 2048
EPS = 1e-6
NEG = -1e30
TWO_PI = 2 * np.pi
ROUND = 1.5 * 2.0**23
PI_HI = float(np.float32(6.28125))
PI_MID = float(np.float32(TWO_PI - 6.28125))
PI_LO = float(np.float32(TWO_PI - 6.28125 - float(np.float32(TWO_PI - 6.28125))))
GAMMA = [1.0 - 2.0 ** (-5 - h) for h in range(RET_H)]

PARAMS = [("mix0", DT), ("cross0", DT), ("mlp0", DT), ("mix1", DT), ("cross1", DT), ("mlp1", DT), ("final", DT),
          ("mem0", DT), ("mem1", DT), ("ret_gn", 4), ("s5_d", 4), ("b_glu", 4), ("conv_w", 64), ("conv_b", 16),
          ("ml_gn", 16), ("ml_skip", 16), ("a_re", 16), ("a_im", 16), ("log_dt", 16), ("h0_re", 16), ("h0_im", 16),
          ("b_gates", 1), ("m0", 1), ("n0", 16), ("conv_cache", 48)]
PCOL = {}
_at = 0
for _n, _w in PARAMS:
    PCOL[_n] = (_at, _w)
    _at += _w
NPAR = _at


def blk(j):
    return sum(TP - P * i for i in range(j))


SCW = blk(NTB)
UNITS = [(c, hf) for c in range(NCH) for hf in range(2)]
NU = len(UNITS)
MEM_SLABS = [(l, w, i) for l in range(2) for w in "kv" for i in range(4)]
MEM_RET = [MEM_SLABS[2 * h:2 * h + 2] for h in range(RET_H)]
MEM_AT = [1, 2, 4, 5, 7, 8]
MEM_S5 = [[MEM_SLABS[8 + MEM_AT.index(n)]] if n in MEM_AT else [] for n in range(NU)] + [MEM_SLABS[14:]]


def unit_width(n):
    return P if UNITS[n][0] < NTB else TS


def schedule():
    groups, slabs = {}, {}

    def g(*name):
        groups[name if len(name) > 1 else name[0]] = len(groups)

    def s(*name):
        slabs[name if len(name) > 1 else name[0]] = len(slabs)

    for part in ("u", "q", "k", "v", "g"):
        for i in range(2):
            s("rs", part, i)
            g("rs", part, i)
        if part == "u":
            g("memnorm")
    g("s5B")
    for h in range(RET_H):
        g("ret", h, "score")
        if h:
            g("ret", h - 1, "var")
        g("ret", h, "aux")
        for x, m in zip(("out", "mean"), MEM_RET[h]):
            s("mem", *m)
            g("mem", *m)
            g("ret", h, x)
    g("ret", RET_H - 1, "var")
    g("s5u", 0)
    for n in range(NU):
        if n + 1 < NU:
            g("s5u", n + 1)
        for m in MEM_S5[n]:
            s("mem", *m)
            g("mem", *m)
        if n:
            g("s5y", n - 1)
    g("s5y", NU - 1)
    for m in MEM_S5[NU]:
        s("mem", *m)
        g("mem", *m)
    s("glu")
    g("glu", 0)
    g("glu", 1)
    for i in range(4):
        s("rs_out", i)
        g("rs_out", i)
    for l in range(2):
        if l == 1:
            for h in range(ML_H):
                for part in ("xm", "z"):
                    for i in range(2):
                        if (h, part, i) != LATE_Z:
                            s("ml", h, part, i)
                            g("ml", h, part, i)
                for part in ("q", "k", "v"):
                    s("ml", h, part)
                    g("ml", h, part, 0)
                    g("ml", h, part, 1)
                g("gate", h)
            s("ml", *LATE_Z)
            g("ml", *LATE_Z)
            g("acol")
            g("cell", CELL_ORDER[0], "r")
            for n, h in enumerate(CELL_ORDER):
                for x in ("aux", "score", "vT", "smp", "kT", "den", "num", "kv", "kvs", "n", "mean", "var"):
                    if h == 1 and x in OUT_BEFORE:
                        s("ml_out", 1, OUT_BEFORE.index(x))
                        g("ml_out", 1, OUT_BEFORE.index(x))
                    if x == "var" and n + 1 < ML_H:
                        g("cell", CELL_ORDER[n + 1], "r")
                    if x == "var" and n + 1 == ML_H:
                        s("ml_out", 0, 0)
                        g("ml_out", 0, 0)
                    g("cell", h, x)
            for i in range(1, 4):
                s("ml_out", 0, i)
                g("ml_out", 0, i)
        for i in range(4):
            s("xq", l, i)
            g("xq", l, i)
            if i == 1:
                g("att", l, "score", 0)
        for x in ("pT", 0), ("score", 2), ("score", 1), ("pv", 0), ("pT", 2), ("pT", 1), ("pv", 2), ("pv", 1):
            g("att", l, *x)
        for i in range(4):
            s("xo", l, i)
            g("xo", l, i)
        for a in range(4):
            for d in ("up", "down"):
                for i in range(4):
                    s("mlp", l, a, d, i)
                    g("mlp", l, a, d, i)
    g("final_norm")
    return groups, slabs


GROUPS, SLABS = schedule()
NSLAB = len(SLABS)
NORM_AT = [("rs", "u", 0), ("xq", 0, 0), ("mlp", 0, 0, "up", 0), ("ml", 0, "xm", 0), ("xq", 1, 0), ("mlp", 1, 0, "up", 0)]
XN_BEFORE = [None, ("rs_out", 3), ("xo", 0, 3), ("mlp", 0, 3, "up", 3), ("ml_out", 0, 3), ("xo", 1, 3)]
NW = T // 3


class Chain:

    def __init__(self, eng, sem):
        self.eng, self.sem, self.n = eng, sem, 0
        self.base = None

    def mark(self, ins, *signals):
        ins.then_inc(self.sem, 1)
        self.n += 1
        if signals:
            self.sync()
            for s in signals:
                self.eng.sem_inc(s, 1)

    def value(self):
        return self.n if self.base is None else self.base + self.n

    def sync(self):
        self.eng.wait_ge(self.sem, self.value())

    def loop(self, i, per):
        self.base, self.start, self.per = i * per + self.n, self.n, per
        self.n = 0

    def endloop(self, turns):
        assert self.n == self.per, (self.n, self.per)
        self.n = self.start + turns * self.per
        self.base = None


def program(nc, A):
    ctx = ExitStack()
    with ctx:
        def sb(name, shape, dt=F32, on=ctx):
            return on.enter_context(nc.sbuf_tensor(name, shape, dt))

        sems = {}

        def S(name):
            if name not in sems:
                sems[name] = ctx.enter_context(nc.semaphore(name))
            return sems[name]

        x = sb("x", [P, DT, T])
        xnh = sb("xnh", [P, DT, T], F32R)
        xnl = sb("xnl", [P, DT, T], F32R)
        raw = sb("raw", [P, 2, SLAB])
        whi = sb("whi", [P, 2, SLAB], F32R)
        wlo = sb("wlo", [P, 2, SLAB], F32R)
        par = sb("par", [P, NPAR])
        ones = sb("ones", [P, P])
        over = sb("over", [P, 3, P])
        ident = sb("ident", [P, P])
        epst = sb("epst", [P, 1])
        ss = sb("ss", [P, T])
        rs = sb("rs", [P, T])
        tm = sb("tm", [P, 2, T])
        rsc = sb("rsc", [P, NCH])
        psum = ctx.enter_context(nc.psum_tensor("psum", [P, 8, 512], F32))
        done = [S("group_done_even"), S("group_done_odd")]
        free = [S("group_free_even"), S("group_free_odd")]

        def col(name, i, n=1):
            a, w = PCOL[name]
            return par[:, a + i:a + i + n]

        def bank(g, b):
            return psum[:, 4 * (g % 2) + b, :]

        def unit(z, n):
            w = unit_width(n)
            e = n % 2 if z.shape[1] == 2 else 0
            return z[:, e, 0:8 * w].rearrange("p (s t) -> p s t", t=w)

        def group_ready(eng, g, turn=None):
            v = g // 2 + 1
            eng.wait_ge(done[g % 2], v if turn is None else turn + v)

        def group_freed(ins, g):
            ins.then_inc(free[g % 2], 1)

        def group_open(eng, g, turn=None):
            if g >= 2:
                v = g // 2
                eng.wait_ge(free[g % 2], v if turn is None else turn + v)

        def group_close(ins, g):
            ins.then_inc(done[g % 2], 1)

        l0 = ExitStack()
        u = sb("u", [P, 4, TP + P], on=l0)
        gt_ = sb("gsilu", [P, 4, T], on=l0)
        BT = sb("BT", [P, 2, 4, P], on=l0)
        Cm = sb("Cm", [P, 2, S5_TILES, 32], on=l0)
        sp = sb("sp", [P, 24, S5_TILES], on=l0)
        fin5 = sb("fin5", [P, 4, S5_TILES], on=l0)
        ropesw = sb("ropesw", [P, 4 * T], on=l0)
        rope = ropesw[:, 0:2 * T].rearrange("p (w t) -> p w t", w=2)
        sw = ropesw[:, 2 * T:4 * T].rearrange("p (a t) -> p a t", a=4)
        memx = ropesw[:, 0:DT * MEM].rearrange("p (k t) -> p k t", k=DT)
        mrs = ropesw[:, DT * MEM:DT * MEM + MEM]
        mrsc = sb("mrsc", [P, 2], on=l0)
        l0a = ExitStack()
        q = sb("q", [P, 4, T], on=l0a)
        k = sb("k", [P, 4, T], on=l0a)
        vt = sb("vt", [P, NCH, 512], on=l0a)
        dec = sb("dec", [P, RET_H, TP], on=l0a)
        wq64 = sb("wq64", [P, RET_H, TS], on=l0a)
        Wm = sb("Wm", [P, SCW], on=l0a)
        Ws = sb("Ws", [TS, TS], on=l0a)
        kt = sb("kt", [P, NCH, P], on=l0a)
        qw = sb("qw", [P, TS], on=l0a)
        S0 = sb("S0", [P, RET_H, P], on=l0a)
        retp = sb("retp", [P, RET_H, P], on=l0a)
        sq = sb("sq", [P, T], on=l0a)
        bz = gt_[:].rearrange("p a t -> p (a t)")[:, 0:2 * S5_TILES * 32].rearrange("p (c s n) -> p c s n", c=2, s=S5_TILES)
        bb = Wm[:, 0:2 * S5_TILES * 32].rearrange("p (c s n) -> p c s n", c=2, s=S5_TILES)
        l0a.close()
        l0b = ExitStack()
        rt = sb("rt", [P, S5_TILES * P], on=l0b)
        za = sb("za", [P, 2, 8 * P], on=l0b)
        zc = sb("zc", [P, 2, 8 * P], on=l0b)
        zb = sb("zb", [P, 1, 8 * P], on=l0b)
        zd = sb("zd", [P, 1, 8 * P], on=l0b)
        ze = sb("ze", [P, 1, 8 * P], on=l0b)
        he = sb("he", [P, 2, 8 * P], on=l0b)
        hf_ = sb("hf", [P, 2, 8 * P], on=l0b)
        l0b.close()
        l0c = ExitStack()
        gh = sb("gh", [P, 4, T], F32R, on=l0c)
        gl = sb("gl", [P, 4, T], F32R, on=l0c)
        sg = sb("sg", [P, 4, HALF], on=l0c)
        l0c.close()
        l0.close()
        xflat = x[:].rearrange("p a t -> p (a t)")
        ctab = xflat[:, 0:S5_TILES * P].rearrange("p (s t) -> p s t", s=S5_TILES)
        stab = xflat[:, S5_TILES * P:2 * S5_TILES * P].rearrange("p (s t) -> p s t", s=S5_TILES)
        memx0, msq = xflat[:, 0:DT * MEM], xflat[:, DT * MEM:2 * DT * MEM]
        mss, mrs0 = xflat[:, 2 * DT * MEM:2 * DT * MEM + MEM], xflat[:, 2 * DT * MEM + MEM:2 * DT * MEM + 2 * MEM]
        mkv = (ss[:, 0:512], xflat[:, 2 * DT * MEM:2 * DT * MEM + 512])
        mnh = xnh[:, 4:8, :].rearrange("p a t -> p (a t)")[:, 0:DT * MEM].rearrange("p (k t) -> p k t", k=DT)
        mnl = xnl[:, 4:8, :].rearrange("p a t -> p (a t)")[:, 0:DT * MEM].rearrange("p (k t) -> p k t", k=DT)
        la = ExitStack()
        xq = sb("xq", [P, DT, T], on=la)
        KT = sb("KT", [P, 2, DT, MEM], on=la)
        V = sb("V", [P, 2, 2, D], on=la)
        pr = sb("pr", [P, 2, 8, MEM], on=la)
        prs = sb("prs", [TS, XH, MEM], on=la)
        pT = sb("pT", [P, 2, 2, TP], on=la)
        pTs = sb("pTs", [P, 2 * XH, TS], on=la)
        mx = sb("mx", [P, 3, 8], on=la)
        nm = sb("nm", [P, 3, 8], on=la)
        sm = sb("sm", [P, 3, 8], on=la)
        la.close()
        lm = ExitStack()
        hh = sb("hh", [P, DT, T], F32R, on=lm)
        hl = sb("hl", [P, DT, T], F32R, on=lm)
        hr = sb("hr", [P, 4, HALF], on=lm)
        hs = sb("hs", [P, 4, HALF], on=lm)
        lm.close()
        ml = ExitStack()
        gtn = sb("gates_n0", [P, T], on=ml)
        gt = gtn[0:36, :]
        n0b = gtn[:, 0:ML_T * P].rearrange("p (d c) -> p d c", d=ML_T)
        cst = sb("conv_out", [P, 2, 16, 3], on=ml)
        mq = sb("mq", [P, ML_T, T], on=ml)
        mk = sb("mk", [P, ML_T, T], on=ml)
        mv = sb("mv", [P, ML_T, T], on=ml)
        xc = sb("xc", [P, ML_T, T], on=ml)
        mla = ExitStack()
        xm = sb("xm", [P, ML_T, T + 6], on=mla)
        xch = sb("xch", [P, ML_T, T], F32R, on=mla)
        xcl = sb("xcl", [P, ML_T, T], F32R, on=mla)
        xmh = sb("xmh", [P, ML_T, T], F32R, on=mla)
        xml = sb("xml", [P, ML_T, T], F32R, on=mla)
        gw = sb("gw", [P, 48, 36], on=mla)
        mla.close()
        mlb = ExitStack()
        rrow = sb("rrow", [4, SCW + TS], on=mlb)
        enrow = sb("enrow", [4, T], on=mlb)
        sirow = sb("sirow", [4, TS], on=mlb)
        acol = sb("acol", [P, 20], on=mlb)
        causal = sb("causal", [P, P], on=mlb)
        sel = sb("sel", [4, ML_H, P], on=mlb)
        mo = sb("mo", [4, 2], on=mlb)
        nout = sb("nout", [P, 2, 16], on=mlb)
        wcol = sb("wcol", [P, 5], on=mlb)
        siB = sb("siB", [P, TS], on=mlb)
        sz = sb("sz", [P, ML_T, T], on=mlb)
        mlr = ExitStack()
        zrow = sb("zrow", [4, TP], on=mlr)
        frow = sb("frow", [4, T], on=mlr)
        lrow = sb("lrow", [4, T], on=mlr)
        erow = sb("erow", [4, T], on=mlr)
        mrow = sb("mrow", [4, T], on=mlr)
        brow = sb("brow", [4, SCW + TS], on=mlr)
        arow = sb("arow", [4, 5, P], on=mlr)
        mlr.close()
        wt = sb("wt", [P, SCW], on=mlb)
        wts = sb("wts", [TS, TS], on=mlb)
        mvt = sb("mvt", [P, NTB, ML_DH], on=mlb)
        mkt = sb("mkt", [P, NTB, ML_DH], on=mlb)
        vt5 = sb("vt5", [TS, ML_DH], on=mlb)
        kt5 = sb("kt5", [TS, ML_DH], on=mlb)
        C0 = sb("C0", [P, ML_T, ML_DH], on=mlb)
        qs = sb("qs", [P, ML_T, TS], on=mlb)
        mlb.close()
        ml.close()

        GR, SL = GROUPS, SLABS
        block = ctx.enter_context(nc.Block())

        @block.sync
        def _(sp_):
            def load(s, n):
                sp_.dma_start(raw[:, s, :], n).then_inc(S(f"slab_loaded{s}"), 16)

            for j in range(4):
                c = slice(SLAB // 4 * j, SLAB // 4 * (j + 1))
                sp_.dma_start(raw[:, 0, c], A["w"][0][:, c]).then_inc(S(f"first_loaded{j}"), 16)
            sp_.wait_ge(S("x_loaded1"), 16)
            load(1, A["w"][1])
            with sp_.Fori(1, NSLAB // 2) as i:
                for s in range(2):
                    sp_.wait_ge(S("slab_split"), i * 2 + (s - 1))
                    load(s, A["w"][bass.ds(i * 2 + s, 1)].rearrange("a p n -> p (a n)"))
            if NSLAB % 2:
                sp_.wait_ge(S("slab_split"), NSLAB - 2)
                load(0, A["w"][NSLAB - 1])

        @block.gpsimd
        def _(pool):
            def split(s, i, first=False):
                pool.wait_ge(S(f"slab_loaded{s}"), i * 16 + (16 if s else 0))
                if not first:
                    pool.wait_ge(S("slab_begun"), i * 2 + s)
                pool.sem_inc(S("split_begun"), 1)
                pool.tensor_scalar(whi[:, s, :], raw[:, s, :], 1.0, 1.0, ALU.mult, ALU.mult).then_inc(S("slab_hi"), 1)
                pool.wait_ge(S("slab_hi"), i * 2 + (s + 1))
                pool.tensor_tensor(wlo[:, s, :], raw[:, s, :], whi[:, s, :].bitcast(F32), ALU.subtract)\
                    .then_inc(S("slab_split"), 1)

            pool.memset(ones[:], 1.0)
            pool.memset(over[:, 0, :], 1.0 / D)
            pool.memset(over[:, 1, :], 1.0 / ML_DH)
            pool.memset(over[:, 2, :], 1.0 / P)
            pool.memset(epst[:], EPS).then_inc(S("consts"), 1)
            for j in range(4):
                c = slice(SLAB // 4 * j, SLAB // 4 * (j + 1))
                pool.wait_ge(S(f"first_loaded{j}"), 16)
                pool.tensor_scalar(whi[:, 0, c], raw[:, 0, c], 1.0, 1.0, ALU.mult, ALU.mult).then_inc(S("first_hi"), 1)
                pool.wait_ge(S("first_hi"), j + 1)
                ins = pool.tensor_tensor(wlo[:, 0, c], raw[:, 0, c], whi[:, 0, c].bitcast(F32), ALU.subtract)
                ins.then_inc(S("first_split"), 1)
            pool.wait_ge(S("first_split"), 4)
            pool.sem_inc(S("slab_hi"), 1)
            pool.sem_inc(S("slab_split"), 1)
            split(1, 0, True)
            M = SLABS["mem", 1, "k", 0]
            assert M % 2 == 0
            with pool.Fori(1, M // 2) as i:
                split(0, i)
                split(1, i)
            split(0, M // 2)
            nxt, begun = M + 1, M
            ch = Chain(pool, S("pool_step"))

            def rotated_back(n):
                pool.wait_ge(S("s5_back"), n + 1)
                pool.tensor_tensor(unit(za, n), unit(za, n), unit(zb, n), ALU.add)
                ins = pool.tensor_tensor(unit(zc, n), unit(zc, n), unit(zd, n), ALU.subtract)
                c, hf = UNITS[n]
                if c == 0:
                    ins.then_inc(S("s5_in"), 1)
                    return
                ch.mark(ins)
                last = lambda z, i: z[:, :, i:i + 1].rearrange("p s o -> p (s o)")
                if c < NTB:
                    pool.wait_ge(S("s5_re"), n - 1)
                    pool.wait_ge(S("s5_im"), n - 1)
                    hr_, hi_ = last(unit(he, n - 2), P - 1), last(unit(hf_, n - 2), P - 1)
                else:
                    hr_, hi_ = col("h0_re", 8 * hf, 8), col("h0_im", 8 * hf, 8)
                ar, ai = sp[:, 9, 8 * hf:8 * hf + 8], sp[:, 10, 8 * hf:8 * hf + 8]
                for d, a_, h_ in ((20, ar, hr_), (21, ai, hi_), (22, ar, hi_), (23, ai, hr_)):
                    ch.mark(pool.tensor_tensor(sp[:, d, 0:8], a_, h_, ALU.mult))
                ch.sync()
                ch.mark(pool.tensor_tensor(sp[:, 20, 8:16], sp[:, 20, 0:8], sp[:, 21, 0:8], ALU.subtract))
                ch.mark(pool.tensor_tensor(sp[:, 22, 8:16], sp[:, 22, 0:8], sp[:, 23, 0:8], ALU.add))
                ch.sync()
                pool.tensor_tensor(last(unit(za, n), 0), last(unit(za, n), 0), sp[:, 20, 8:16], ALU.add)
                pool.tensor_tensor(last(unit(zc, n), 0), last(unit(zc, n), 0), sp[:, 22, 8:16], ALU.add)\
                    .then_inc(S("s5_in"), 1)

            rotated_back(0)
            for n in range(NU):
                if n + 1 < NU:
                    rotated_back(n + 1)
                begun += len(MEM_S5[n])
                while nxt <= begun:
                    split(nxt % 2, nxt // 2)
                    nxt += 1
                pool.wait_ge(S("s5_fwd"), n + 1)
                pool.tensor_tensor(unit(he, n), unit(he, n), unit(ze, n), ALU.subtract)\
                    .then_inc(S("s5_re"), 1)
            if nxt % 2:
                split(1, nxt // 2)
                nxt += 1
            with pool.Fori(nxt // 2, NSLAB // 2) as i:
                split(0, i)
                split(1, i)
            if NSLAB % 2:
                split(0, NSLAB // 2)

        @block.tensor
        def _(pe):
            def slab_start(n, turn=None):
                pe.wait_ge(S("slab_split"), n + 1 if turn is None else turn * 8 + (n + 1))

            def project(g, n, rh, rl, kts=DT, m0=0, ms=2, wait=None, turn=None, first=True, halves=((0, HALF), (HALF, T)),
                        order=None, start=True, stop=True, close=True):
                s = n % 2
                if start:
                    if n:
                        slab_start(n, turn and turn[1])
                    group_open(pe, g, turn and turn[0])
                W = [w[:, s, :].rearrange("p (k m c) -> p k m c", k=kts, m=ms) for w in (whi, wlo)]
                order = order or range(kts)
                for kk in order:
                    at_first, at_last = start and kk == order[0], stop and kk == order[-1]
                    if wait:
                        wait(kk)
                    for m in range(2):
                        for wi, r in ((0, rh), (0, rl), (1, rh)):
                            for b, (t0, t1) in enumerate(halves):
                                ins = pe.matmul(bank(g, 2 * m + b)[:, 0:t1 - t0], W[wi][:, kk, m0 + m, :], r[:, kk, t0:t1],
                                                start=(at_first and wi == 0 and r is rh), stop=(at_last and wi == 1))
                            if at_first and m == 0 and wi == 0 and r is rh and first:
                                ins.then_inc(S("slab_begun"), 1)
                if close:
                    group_close(ins, g)

            def token_major(g, n, xh, xl, toks, rows):
                s = n % 2
                slab_start(n)
                group_open(pe, g)
                W = [w[:, s, :].rearrange("p (k c) -> p k c", k=DT) for w in (whi, wlo)]
                for (t0, t1), (b, c0) in zip(toks, rows):
                    for kk in range(DT):
                        for wi, r in ((0, xh), (0, xl), (1, xh)):
                            ins = pe.matmul(bank(g, b)[0:t1 - t0, c0:c0 + 256], r[:, kk, t0:t1], W[wi][:, kk, :],
                                            start=(kk == 0 and wi == 0 and r is xh), stop=(kk == DT - 1 and wi == 1))
                            if t0 == toks[0][0] and kk == 0 and wi == 0 and r is xh:
                                ins.then_inc(S("slab_begun"), 1)
                group_close(ins, g)

            def token_sum(g, which, src, width=T):
                group_open(pe, g)
                for b, (t0, t1) in enumerate(((0, HALF), (HALF, T)) if width == T else ((0, width),)):
                    ins = pe.matmul(bank(g, b)[:, 0:t1 - t0], over[:, which, :], src[:, t0:t1], start=True, stop=True)
                group_close(ins, g)

            def mm(out, lhsT, rhs, first=True, last=True):
                return pe.matmul(out, lhsT, rhs, start=first, stop=last)

            def project_first(i, g, n, turn=None):
                def tile_ready(kk):
                    if n == 0:
                        pe.wait_ge(S("first_split"), kk // 2 + 1)
                    pe.wait_ge(S("xn_ready"), 8 * i + kk + 1)
                project(g, n, xnh, xnl, wait=tile_ready, close=False)
                pe.wait_ge(S("squares_ready"), i + 1)
                for b in range(3):
                    ins = mm(bank(g, b)[:, HALF:HALF + NW], over[:, 0, :], ss[:, NW * b:NW * b + NW])
                if i == 0:
                    for t in range(NCH):
                        w = P if t < NTB else TS
                        ins = mm(bank(g, 3)[0:w, HALF + t:HALF + t + 1], ss[:, P * t:P * t + w], over[:, 0, 0:1])
                group_close(ins, g)

            pe.wait_ge(S("consts"), 1)
            for part in ("u", "q", "k", "v", "g"):
                for i in range(2):
                    g, n = GR["rs", part, i], SL["rs", part, i]
                    if part == "v":
                        toks = [(P * t, min(P * t + P, T)) for t in range(NCH)]
                        token_major(g, n, xnh, xnl, toks, [(0, 0), (1, 0), (2, 0), (3, 0), (3, 256)])
                    elif (part, i) == ("u", 0):
                        project_first(0, g, n)
                    else:
                        project(g, n, xnh, xnl)
                if part == "u":
                    pe.wait_ge(S("mem_squares"), 1)
                    g = GR["memnorm"]
                    group_open(pe, g)
                    mm(bank(g, 0)[:, 0:MEM], over[:, 0, :], mss)
                    for t in range(2):
                        ins = mm(bank(g, 1)[:, t:t + 1], mss[:, P * t:P * t + P], over[:, 0, 0:1])
                    group_close(ins, g)
            pe.wait_ge(S("bb_ready"), 1)
            pe.wait_ge(S("const_loaded"), 16 * 8)
            g = GR["s5B"]
            group_open(pe, g)
            for c in range(2):
                for j in range(4):
                    ins = pe.transpose(bank(g, c)[:, P * j:P * j + P],
                                       bb[:, c, 4 * j:4 * j + 4, :].rearrange("p s c -> p (s c)"), ident[:])
            group_close(ins, g)

            def memory(m):
                gm, sn = GR[("mem",) + m], SL[("mem",) + m]
                pe.wait_ge(S("mem_ready"), 8 * (m[0] + 1))
                if m[1] == "k":
                    project(gm, sn, mnh, mnl, halves=((0, MEM),))
                else:
                    token_major(gm, sn, mnh, mnl, [(0, P), (P, 2 * P)], [(0, 0), (1, 0)])

            pe.wait_ge(S("rope_done"), 2)
            def ret_var(h):
                pe.wait_ge(S("ret_sq"), h + 1)
                token_sum(GR["ret", h, "var"], 2, sq[:])

            for h in range(RET_H):
                g = GR["ret", h, "score"]
                group_open(pe, g)
                for j in range(NTB):
                    ins = mm(bank(g, j)[:, 0:TP - P * j], k[:, h, P * j:P * j + P], q[:, h, P * j:TP])
                group_close(ins, g)
                if h:
                    ret_var(h - 1)
                g = GR["ret", h, "aux"]
                group_open(pe, g)
                mm(bank(g, 0)[0:TS, 0:TS], k[:, h, TP:T], q[:, h, TP:T])
                for j in range(NTB):
                    pe.transpose(bank(g, 1)[:, P * j:P * j + P], k[:, h, P * j:P * j + P], ident[:])
                ins = pe.transpose(bank(g, 2)[0:TS, 0:P], k[:, h, TP:T], ident[:])
                group_close(ins, g)
                memory(MEM_RET[h][0])
                g = GR["ret", h, "out"]
                group_open(pe, g)
                hc = slice(h * P, h * P + P)
                pe.wait_ge(S("ret_w"), h + 1)
                for j in range(NTB):
                    mm(bank(g, 0)[:, P * j:TP], vt[:, j, hc], Wm[:, blk(j):blk(j) + TP - P * j], j == 0, j == NTB - 1)
                mm(bank(g, 1)[:, 0:TS], S0[:, h, :], qw[:], True, False)
                mm(bank(g, 1)[:, 0:TS], vt[0:TS, NTB, hc], Ws[:], False, True)
                for j in range(NTB):
                    mm(bank(g, 2)[:, 0:P], kt[:, j, :], vt[:, j, hc], j == 0, j == NTB - 1)
                ins = mm(bank(g, 3)[:, 0:P], kt[0:TS, NTB, :], vt[0:TS, NTB, hc])
                group_close(ins, g)
                memory(MEM_RET[h][1])
                pe.wait_ge(S("ret_o"), h + 1)
                token_sum(GR["ret", h, "mean"], 2, q[:, h, :])
            ret_var(RET_H - 1)

            def s5_y(n):
                c, hf = UNITS[n]
                g = GR["s5y", n]
                w = unit_width(n)
                pe.wait_ge(S("s5_re"), n + 1)
                pe.wait_ge(S("s5_im"), n + 1)
                group_open(pe, g)
                for s in range(8):
                    o = bank(g, s // 4)[32 * (s % 4):32 * (s % 4) + 32, 0:w]
                    st = 8 * hf + s
                    mm(o, Cm[:, 0, st, :], unit(he, n)[:, s, :], True, False)
                    ins = mm(o, Cm[:, 1, st, :], unit(hf_, n)[:, s, :], False, True)
                group_close(ins, g)

            pe.wait_ge(S("s5_const"), 1)

            def s5_u(n):
                c, hf = UNITS[n]
                g = GR["s5u", n]
                group_open(pe, g)
                for i in range(4):
                    for c2 in range(2):
                        for a in range(2):
                            j = 2 * hf + a
                            r = slice(32 * i, 32 * i + 32)
                            ins = mm(bank(g, i)[:, P * (2 * c2 + a):P * (2 * c2 + a) + P], BT[r, c2, j, :], u[r, j, P * c:P * c + P])
                group_close(ins, g)

            s5_u(0)
            for n in range(NU):
                if n + 1 < NU:
                    s5_u(n + 1)
                for m in MEM_S5[n]:
                    memory(m)
                if n:
                    s5_y(n - 1)
            s5_y(NU - 1)
            for m in MEM_S5[NU]:
                memory(m)
            for a in range(2):
                project(GR["glu", a], SL["glu"], gh, gl, kts=4, m0=2 * a, ms=4, first=a == 0,
                        wait=None if a else lambda kk: pe.wait_ge(S("glu_in"), kk + 1))
            def s5_half(kk):
                if kk >= 4:
                    pe.wait_ge(S("rs_y"), kk - 3)
            for i in range(4):
                project(GR["rs_out", i], SL["rs_out", i], xnh, xnl, wait=None if i else s5_half)

            def attention(l):
                for i in range(4):
                    if i == 0:
                        project_first(3 * l + 1, GR["xq", l, i], SL["xq", l, i])
                    else:
                        project(GR["xq", l, i], SL["xq", l, i], xnh, xnl)
                    if i == 1:
                        pe.wait_ge(S("kv_loaded"), 64 * (l + 1))
                        scores(l, 0)
                transposed(l, 0)
                g = GR["att", l, "score", 2]
                pe.wait_ge(S("xq_ready"), 4 * l + 4)
                group_open(pe, g)
                for h in range(XH):
                    for e in range(2):
                        ins = mm(bank(g, h)[0:TS, 0:MEM], xq[:, 2 * h + e, TP:T], KT[:, 1, 2 * h + e, :], e == 0, e == 1)
                group_close(ins, g)
                scores(l, 1)
                values(l, 0)
                transposed(l, 2)
                transposed(l, 1)
                values(l, 2)
                values(l, 1)
                for i in range(4):
                    project(GR["xo", l, i], SL["xo", l, i], xnh, xnl,
                            wait=None if i else lambda kk: pe.wait_ge(S("att_o"), 3 * l + (2 if kk < 4 else 3)))

            def scores(l, x2):
                g = GR["att", l, "score", x2]
                pe.wait_ge(S("xq_ready"), 4 * l + 2 * x2 + 2)
                group_open(pe, g)
                for t in range(NTB):
                    for h in range(2):
                        for e in range(2):
                            f = 2 * (2 * x2 + h) + e
                            ins = mm(bank(g, t)[:, MEM * h:MEM * h + MEM], xq[:, f, P * t:P * t + P], KT[:, 0, f, :],
                                     e == 0, e == 1)
                group_close(ins, g)

            def transposed(l, x2):
                g = GR["att", l, "pT", x2]
                pe.wait_ge(S("prob"), 3 * l + ATT_ORDER.index(x2) + 1)
                group_open(pe, g)
                if x2 < 2:
                    for h in range(2):
                        for m in range(2):
                            for t in range(NTB):
                                ins = pe.transpose(bank(g, 2 * h + m)[:, P * t:P * t + P],
                                                   pr[:, x2, 2 * t + h, P * m:P * m + P], ident[:])
                else:
                    for h in range(XH):
                        for m in range(2):
                            ins = pe.transpose(bank(g, 0)[:, TS * (2 * h + m):TS * (2 * h + m) + TS],
                                               prs[:, h, P * m:P * m + P], ident[0:TS, 0:TS])
                group_close(ins, g)

            def values(l, x2):
                g = GR["att", l, "pv", x2]
                pe.wait_ge(S("pT"), 3 * l + ATT_ORDER.index(x2) + 1)
                group_open(pe, g)
                for h in range(2 if x2 < 2 else XH):
                    for e in range(2):
                        for m in range(2):
                            if x2 < 2:
                                hg = 2 * x2 + h
                                ins = mm(bank(g, 2 * h + e), V[:, 0, m, 2 * P * hg + P * e:2 * P * hg + P * e + P],
                                         pT[:, h, m, :], m == 0, m == 1)
                            else:
                                ins = mm(bank(g, 0)[:, TS * (2 * h + e):TS * (2 * h + e) + TS],
                                         V[:, 1, m, 2 * P * h + P * e:2 * P * h + P * e + P], pTs[:, 2 * h + m, :],
                                         m == 0, m == 1)
                group_close(ins, g)

            def mlp(l):
                g0, n0 = GR["mlp", l, 0, "up", 0], SL["mlp", l, 0, "up", 0]

                def quarter(first=False, tg=None, tn=None, base=0):
                    for i in range(4):
                        if first and i == 0:
                            project_first(3 * l + 2, g0, n0)
                        else:
                            project(g0 + i, n0 + i, xnh, xnl, turn=tn is not None and (tg, tn) or None)
                    for i in range(4):
                        def hid(kk):
                            pe.wait_ge(S("hidden_ready"), base + (16 * l + kk // 2 + 1))
                        project(g0 + 4 + i, n0 + 4 + i, hh, hl, turn=tn is not None and (tg, tn) or None,
                                wait=hid if i == 0 else None)

                quarter(first=True)
                with pe.Fori(1, 4) as a:
                    quarter(tg=a * 4, tn=a, base=a * 4)

            attention(0)
            mlp(0)
            for h in range(ML_H):
                for part in ("xm", "z"):
                    for i in range(2):
                        if (h, part, i) == (0, "xm", 0):
                            project_first(3, GR["ml", h, part, i], SL["ml", h, part, i])
                        elif (h, part, i) != LATE_Z:
                            project(GR["ml", h, part, i], SL["ml", h, part, i], xnh, xnl)
                for w, part in enumerate(("q", "k", "v")):
                    if w == 2:
                        pe.wait_ge(S("xm_split"), h + 1)
                    for a in range(2):
                        project(GR["ml", h, part, a], SL["ml", h, part], *((xmh, xml) if w == 2 else (xch, xcl)), kts=4,
                                m0=2 * a, ms=4, first=a == 0,
                                wait=None if w or a else lambda kk: pe.wait_ge(S("xc_split"), 4 * h + kk + 1))
                g = GR["gate", h]
                if h == 0:
                    pe.wait_ge(S("gw_loaded"), 16)
                group_open(pe, g)
                for w, buf in enumerate((mq, mk, mv)):
                    pe.wait_ge(S("qkv_ready"), 6 * h + 2 * w + 2)
                    for t in range(ML_T):
                        for b, (t0, t1) in enumerate(((0, HALF), (HALF, T))):
                            ins = mm(bank(g, b)[0:36, 0:t1 - t0], gw[:, 16 * w + 4 * h + t, :], buf[:, t, t0:t1],
                                     w == 0 and t == 0, w == 2 and t == ML_T - 1)
                group_close(ins, g)
            project(GR[("ml",) + LATE_Z], SL[("ml",) + LATE_Z], xnh, xnl)
            g = GR["acol"]
            pe.wait_ge(S("rows_ready"), 1)
            group_open(pe, g)
            for j in range(5):
                w = P if j < NTB else TS
                ins = pe.transpose(bank(g, 0)[0:w, 4 * j:4 * j + 4], arow[:, j, 0:w], ident[0:4, 0:4])
            group_close(ins, g)
            pe.wait_ge(S("cell_const"), 32)
            pe.wait_ge(S("rows_exp"), 1)

            def out_slab(pair, i, order=(4, 5, 6, 7, 0, 1, 2, 3), **parts):
                def tile_ready(kk):
                    pe.wait_ge(S("cell_y"), 8 * (1 - pair) + (kk - 3 if kk >= 4 else kk + 5))
                project(GR["ml_out", pair, i], SL["ml_out", pair, i], xnh, xnl, wait=None if i else tile_ready,
                        order=order, **parts)

            def rows(h):
                g = GR["cell", h, "r"]
                group_open(pe, g)
                for j in range(NTB):
                    w = TP - P * j
                    mm(bank(g, j)[:, 0:w], sel[:, h, :], rrow[:, blk(j):blk(j) + w], True, False)
                    ins = mm(bank(g, j)[:, 0:P], ident[:], causal[:], False, True)
                group_close(ins, g)

            rows(CELL_ORDER[0])
            for n, h in enumerate(CELL_ORDER):
                def open_(x):
                    if h == 1 and x in ("den", "num", "n"):
                        out_slab(1, OUT_BEFORE.index(x))
                    g = GR["cell", h, x]
                    group_open(pe, g)
                    return g, [bank(g, b) for b in range(4)]

                g, B = open_("aux")
                mm(B[0][0:TS, 0:TS], sel[:, h, 0:TS], rrow[:, SCW:SCW + TS], True, False)
                mm(B[0][0:TS, 0:TS], ident[0:TS, 0:TS], causal[0:TS, 0:TS], False, True)
                mm(B[1][:, 0:TS], sel[:, h, :], sirow[:])
                for b in range(2):
                    ins = mm(B[2 + b][:, 0:HALF], sel[:, h, :], enrow[:, HALF * b:HALF * b + HALF])
                group_close(ins, g)
                pe.wait_ge(S("cell_q"), 16 * n + 1 if n else 1)
                pe.wait_ge(S("cell_k"), 16 * n + 1 if n else 1)
                g, B = open_("score")
                for j in range(NTB):
                    for d in range(ML_T):
                        ins = mm(B[j][:, 0:TP - P * j], mk[:, d, P * j:P * j + P], mq[:, d, P * j:TP], d == 0, d == ML_T - 1)
                group_close(ins, g)
                pe.wait_ge(S("cell_v"), 16 * n + 1 if n else 1)
                g, B = open_("vT")
                for j in range(NTB):
                    for d in range(ML_T):
                        ins = pe.transpose(B[j][:, P * d:P * d + P], mv[:, d, P * j:P * j + P], ident[:])
                group_close(ins, g)
                g, B = open_("smp")
                for d in range(ML_T):
                    mm(B[0][0:TS, 0:TS], mk[:, d, TP:T], mq[:, d, TP:T], d == 0, d == ML_T - 1)
                for b, src in ((1, mv), (2, mk)):
                    for d in range(ML_T):
                        ins = pe.transpose(B[b][0:TS, P * d:P * d + P], src[:, d, TP:T], ident[:])
                group_close(ins, g)
                g, B = open_("kT")
                for j in range(NTB):
                    for d in range(ML_T):
                        ins = pe.transpose(B[j][:, P * d:P * d + P], mk[:, d, P * j:P * j + P], ident[:])
                group_close(ins, g)
                g, B = open_("den")
                pe.wait_ge(S("cell_pt"), n + 1)
                pe.wait_ge(S("cell_qs"), n + 1)
                pe.wait_ge(S("cell_smp"), n + 1)
                pe.wait_ge(S("cell_c"), 16 * (n + 1))
                for j in range(NTB):
                    mm(B[0][:, P * j:TP], ones[:], wt[:, blk(j):blk(j) + TP - P * j], j == 0, j == NTB - 1)
                for d in range(ML_T):
                    mm(B[1][:, 0:TS], n0b[:, d, :], qs[:, d, :], d == 0, False)
                mm(B[1][:, 0:TS], ones[0:TS, :], wts[:], False, True)
                for e in range(ML_T):
                    o = B[2][:, TS * e:TS * e + TS]
                    for d in range(ML_T):
                        mm(o, C0[:, d, P * e:P * e + P], qs[:, d, :], d == 0, False)
                    ins = mm(o, vt5[:, P * e:P * e + P], wts[:], False, True)
                group_close(ins, g)
                g, B = open_("num")
                pe.wait_ge(S("cell_vt"), n + 1)
                for e in range(ML_T):
                    for j in range(NTB):
                        ins = mm(B[e][:, P * j:TP], mvt[:, j, P * e:P * e + P], wt[:, blk(j):blk(j) + TP - P * j],
                                 j == 0, j == NTB - 1)
                group_close(ins, g)
                pe.wait_ge(S("cell_kt"), n + 1)
                g, B = open_("kv")
                for d in range(ML_T):
                    for j in range(NTB):
                        ins = mm(B[d], mkt[:, j, P * d:P * d + P], mvt[:, j, :], j == 0, j == NTB - 1)
                group_close(ins, g)
                g, B = open_("kvs")
                for d in range(ML_T):
                    ins = mm(B[d], kt5[:, P * d:P * d + P], vt5[:])
                group_close(ins, g)
                g, B = open_("n")
                for d in range(ML_T):
                    for j in range(NTB):
                        mm(B[0][:, d:d + 1], mkt[:, j, P * d:P * d + P], ones[:, 0:1], j == 0, j == NTB - 1)
                for d in range(ML_T):
                    ins = mm(B[0][:, 4 + d:5 + d], kt5[:, P * d:P * d + P], ones[0:TS, 0:1])
                group_close(ins, g)
                if h == 1:
                    out_slab(1, 3)
                pe.wait_ge(S("cell_sum"), 2 * n + 1)
                token_sum(GR["cell", h, "mean"], 1, ss)
                if n + 1 < ML_H:
                    rows(CELL_ORDER[n + 1])
                else:
                    out_slab(0, 0, order=(4, 5, 6, 7), stop=False, close=False)
                pe.wait_ge(S("cell_sum"), 2 * n + 2)
                token_sum(GR["cell", h, "var"], 1, ss)
            out_slab(0, 0, order=(0, 1, 2, 3), start=False)
            for i in range(1, 4):
                out_slab(0, i)
            attention(1)
            mlp(1)
            pe.wait_ge(S("squares_ready"), 7)
            token_sum(GR["final_norm"], 0, ss)

        @block.scalar
        def _(act):
            ch = Chain(act, S("act_step"))

            def load(dst, src, sem):
                act.dma_start(dst, src).then_inc(S(sem), 16)

            load(par[:], A["par"], "par_loaded")
            for j in range(4):
                load(x[:, 2 * j:2 * j + 2, :], A["xT"][:, 2 * j:2 * j + 2, :], f"x_loaded{j}")

            def rstd(g, out, width=T):
                group_ready(act, g)
                for b, (t0, t1) in enumerate(((0, HALF), (HALF, T)) if width == T else ((0, width),)):
                    ins = act.activation(out[:, t0:t1], bank(g, b)[:, 0:t1 - t0], ACT.Ln, bias=epst[:])
                    ch.mark(ins)
                ch.sync()
                act.sem_inc(free[g % 2], 1)
                act.activation(out[:, 0:width], out[:, 0:width], ACT.Exp, scale=-0.5).then_inc(S("rstd_ready"), 1)

            X_TILE = {1: ("x_tile", 0), 2: ("x_tile", 8), 3: ("x_mlp", 24), 4: ("x_tile", 24), 5: ("x_tile", 32),
                      6: ("x_mlp", 56)}

            def x_tile(i, kk):
                if i:
                    act.wait_ge(S(X_TILE[i][0]), X_TILE[i][1] + kk + 1)
                else:
                    act.wait_ge(S(f"x_loaded{kk // 2}"), 16)

            def squares(i, kks):
                for kk in kks:
                    x_tile(i, kk)
                    if 8 * i + kk >= 2:
                        act.wait_ge(S("sq_used"), 8 * i + kk - 1)
                    act.activation(tm[:, kk % 2, :], x[:, kk, :], ACT.Square).then_inc(S("sq_ready"), 1)

            def high(i, gain, kks):
                if i and kks[0] == 0:
                    group_ready(act, GR[XN_BEFORE[i]])
                for kk in kks:
                    x_tile(i, kk)
                    act.activation(xnh[:, kk, :], x[:, kk, :], ACT.Copy, scale=col(gain, kk)).then_inc(S("xn_hi"), 1)

            def norm_rstd(i, power=1):
                g = GR[NORM_AT[i]]
                group_ready(act, g)
                ch.mark(act.activation(rs[:].rearrange("p (b t) -> p b t", b=3),
                                       psum[:, 4 * (g % 2):4 * (g % 2) + 3, HALF:HALF + NW], ACT.Ln, bias=epst[:]))
                if i == 0:
                    ch.mark(act.activation(rsc[:, 0:NTB], bank(g, 3)[:, HALF:HALF + NTB], ACT.Ln, bias=epst[:]))
                    ch.mark(act.activation(rsc[0:TS, NTB:NCH], bank(g, 3)[0:TS, HALF + NTB:HALF + NCH], ACT.Ln,
                                           bias=epst[0:TS]))
                ch.sync()
                if i == 0:
                    act.activation(rsc[:, 0:NTB], rsc[:, 0:NTB], ACT.Exp, scale=-0.5)
                    act.activation(rsc[0:TS, NTB:NCH], rsc[0:TS, NTB:NCH], ACT.Exp, scale=-0.5)
                act.activation(rs[:], rs[:], ACT.Exp, scale=-0.5 * power).then_inc(S("rstd_ready"), 1)

            act.wait_ge(S("par_loaded"), 16)
            high(0, "mix0", range(DT))
            squares(0, range(DT))
            act.wait_ge(S("consts"), 1)
            load(rope[:], A["rope"], "rope_loaded")
            act.wait_ge(S("xn_ready"), 8)
            act.wait_ge(S("sq_ready"), 8)
            load(memx0, A["memT"].rearrange("p k t -> p (k t)"), "memx_loaded")
            load(dec[:], A["decay"], "const_loaded")
            load(wq64[:], A["wq64"], "const_loaded")
            load(ident[:], A["ident"], "const_loaded")
            load(S0[:], A["ret0"], "const_loaded")
            load(bz[:, 0], A["Bre"], "const_loaded")
            load(bz[:, 1], A["Bim"], "const_loaded")
            load(Cm[:, 0], A["Cre"], "const_loaded")
            load(Cm[:, 1], A["Cim"], "const_loaded")
            act.activation(sp[:, 0, :], col("log_dt", 0, 16), ACT.Exp).then_inc(S("s5_dt"), 1)
            norm_rstd(0)
            act.wait_ge(S("memx_loaded"), 16)
            act.activation(msq, memx0, ACT.Square).then_inc(S("msq_ready"), 1)
            act.wait_ge(S("s5_arg"), 1)
            act.activation(sp[:, 3, :], sp[:, 1, :], ACT.Exp)
            act.activation(sp[:, 4, :], sp[:, 2, :], ACT.Sin)
            act.activation(sp[:, 5, :], sp[:, 2, :], ACT.Sin, scale=0.5).then_inc(S("s5_trig"), 1)
            g = GR["memnorm"]
            group_ready(act, g)
            ch.mark(act.activation(mrs0, bank(g, 0)[:, 0:MEM], ACT.Ln, bias=epst[:]))
            ch.mark(act.activation(mrsc[:], bank(g, 1)[:, 0:2], ACT.Ln, bias=epst[:]), free[g % 2])
            act.activation(mrsc[:], mrsc[:], ACT.Exp, scale=-0.5)
            act.activation(mrs0, mrs0, ACT.Exp, scale=-0.5).then_inc(S("mrs_ready"), 1)
            for w, part in enumerate(("q", "k")):
                for i in range(2):
                    g = GR["rs", part, i]
                    group_ready(act, g)
                    if 2 * w + i:
                        act.wait_ge(S("swap_used"), 2 * w + i)
                    for b in range(4):
                        act.activation(sw[0:64, b, :], bank(g, b)[64:128, 0:HALF], ACT.Copy)
                        ins = act.activation(sw[64:128, b, :], bank(g, b)[0:64, 0:HALF], ACT.Copy)
                    ins.then_inc(S("swap_ready"), 1)
            act.wait_ge(S("rope_free"), 1)
            load(memx, A["memT"], "memx_loaded")

            def high_memory(l):
                for kk in range(DT):
                    act.activation(mnh[:, kk, :], memx[:, kk, :], ACT.Copy, scale=col(f"mem{l}", kk)).then_inc(S("mem_hi"), 1)

            def memory_out(m):
                l, w, i = m
                j, g = MEM_SLABS.index(m), GR[("mem",) + m]
                if w == "k":
                    act.wait_ge(S("mem_k"), 4 * l + i + 1)
                    dst = A["o_mkT"][l][:, 2 * i:2 * i + 2, :]
                else:
                    if j >= 2:
                        act.wait_ge(S(f"mkv_stored{j % 2}"), 16 * (j // 2))
                    group_ready(act, g)
                    for t in range(2):
                        ins = act.activation(mkv[j % 2][:, 256 * t:256 * t + 256], bank(g, t)[:, 0:256], ACT.Copy,
                                             scale=mrsc[:, t:t + 1])
                    ch.mark(ins, free[g % 2])
                    dst = A["o_mv"][l][:, :, 256 * i:256 * i + 256]
                act.dma_start(dst, mkv[j % 2].rearrange("p (a b) -> p a b", a=2)).then_inc(S(f"mkv_stored{j % 2}"), 16)

            for i in range(2):
                act.wait_ge(S("g_scaled"), i + 1)
                act.activation(gt_[:, 2 * i:2 * i + 2, :], gt_[:, 2 * i:2 * i + 2, :], ACT.Silu).then_inc(S("g_silu"), 1)
            group_ready(act, GR["rs", "g", 1])
            act.wait_ge(S("memx_loaded"), 32)
            high_memory(0)
            for h in range(RET_H):
                for m in MEM_RET[h]:
                    memory_out(m)
                if h == RET_H - 1:
                    act.wait_ge(S("ret_state"), RET_H)
                    act.dma_start(A["o_retp"], retp[:]).then_inc(S("stored"), 16)
                    act.dma_start(A["o_rets"], S0[:]).then_inc(S("stored"), 16)
                act.wait_ge(S("ret_c"), h + 1)
                act.activation(sq[:], q[:, h, :], ACT.Square).then_inc(S("ret_sq"), 1)
                rstd(GR["ret", h, "var"], rs)
            high_memory(1)
            for n in range(NU):
                for m in MEM_S5[n]:
                    memory_out(m)
            for j in range(4):
                act.wait_ge(S("s5_y"), NU - 1 + j // 2)
                act.activation(u[:, j, 0:T], u[:, j, 0:T], ACT.Gelu_apprx_tanh).then_inc(S("gelu"), 1)
            for m in MEM_S5[NU]:
                memory_out(m)
            for j in range(2):
                act.wait_ge(S(f"mkv_stored{j}"), 16 * 8)
            load(x[:], A["xT"], "x_again")
            for a in range(2):
                g = GR["glu", a]
                group_ready(act, g)
                if a:
                    act.wait_ge(S("sg_used"), 1)
                for m in range(2):
                    for b in range(2):
                        ins = act.activation(sg[:, 2 * m + b, :], bank(g, 2 * m + b)[:, 0:HALF], ACT.Sigmoid,
                                             bias=col("b_glu", 2 * a + m))
                ch.mark(ins, free[g % 2], S("sg_ready"))

            act.dma_start(A["o_s5"], fin5[:]).then_inc(S("stored"), 16)
            act.wait_ge(S("stored"), 48)

            def before_projection(i, gain):
                squares(i, range(6))
                high(i, gain, range(6))
                high(i, gain, range(6, 8))
                squares(i, range(6, 8))

            def attention(l):
                for j in range(2):
                    act.wait_ge(S(f"mkv_stored{j}"), 16 * 8)
                act.wait_ge(S("arena_free"), l + 1)
                load(KT[:, 0], A["o_mkT"][l], "kv_loaded")
                load(KT[:, 1], A["ckT"][l], "kv_loaded")
                load(V[:, 0], A["o_mv"][l], "kv_loaded")
                load(V[:, 1], A["cv"][l], "kv_loaded")
                before_projection(3 * l + 1, f"cross{l}")
                norm_rstd(3 * l + 1)
                def exps(x2):
                    g = GR["att", l, "score", x2]
                    act.wait_ge(S("row_max"), 3 * l + ATT_ORDER.index(x2) + 1)
                    for t in range(NTB):
                        if x2 < 2:
                            for h in range(2):
                                ins = act.activation(pr[:, x2, 2 * t + h, :], bank(g, t)[:, MEM * h:MEM * h + MEM], ACT.Exp,
                                                     bias=nm[:, x2, 2 * t + h:2 * t + h + 1], scale=1.0 / 16,
                                                     accum_out=sm[:, x2, 2 * t + h:2 * t + h + 1])
                        else:
                            ins = act.activation(prs[:, t, :], bank(g, t)[0:TS, 0:MEM], ACT.Exp,
                                                 bias=nm[0:TS, x2, t:t + 1], scale=1.0 / 16, accum_out=sm[0:TS, x2, t:t + 1])
                    ch.mark(ins, free[g % 2], S("exp_done"))

                def copy_pT(x2):
                    g = GR["att", l, "pT", x2]
                    group_ready(act, g)
                    if x2 < 2:
                        if x2 == 1:
                            group_ready(act, GR["att", l, "pv", 0])
                        for b in range(4):
                            ins = act.activation(pT[:, b // 2, b % 2, :], bank(g, b), ACT.Copy)
                    else:
                        ins = act.activation(pTs[:].rearrange("p h t -> p (h t)"), bank(g, 0), ACT.Copy)
                    ch.mark(ins, free[g % 2], S("pT"))

                def high_o(x2):
                    g = GR["att", l, "pv", x2]
                    group_ready(act, g)
                    if x2 < 2:
                        for b in range(4):
                            ins = act.activation(xnh[:, 4 * x2 + b, 0:TP], bank(g, b), ACT.Copy)
                    else:
                        ins = act.activation(xnh[:, :, TP:T], bank(g, 0).rearrange("p (f t) -> p f t", f=DT), ACT.Copy)
                    ins.then_inc(S("o_hi"), 1)

                exps(0)
                copy_pT(0)
                exps(2)
                exps(1)
                high_o(0)
                copy_pT(2)
                copy_pT(1)
                high_o(2)
                high_o(1)

            attention(0)
            before_projection(2, "mlp0")
            norm_rstd(2, power=2)
            for kk in range(0, DT, 2):
                high(3, "mix1", (kk, kk + 1))
                squares(3, (kk, kk + 1))
            load(gw[:], A["gw"], "gw_loaded")
            norm_rstd(3)

            def store(dst, src, name):
                act.dma_start(dst, src).then_inc(S(name), 16)

            for h in range(ML_H):
                act.wait_ge(S("xm_ready"), 2 * (h + 1))
                if h:
                    group_ready(act, GR["ml", h - 1, "v", 1])
                act.activation(xmh[:, :, 0:TP], xm[:, :, 3:3 + TP], ACT.Copy)
                act.activation(xmh[:, :, TP:T], xm[:, :, TP + 6:T + 6], ACT.Copy).then_inc(S("xm_hi"), 1)
                for t in range(ML_T):
                    act.wait_ge(S("conv_done"), 4 * h + t + 1)
                    ch.mark(act.activation(xc[:, t, :], xc[:, t, :], ACT.Silu))
                    ch.sync()
                    act.activation(xch[:, t, :], xc[:, t, :], ACT.Copy).then_inc(S("xc_hi"), 1)
                if h < ML_H - 1:
                    store(A["t_xc"][h], xc[:], "xc_spilled")
                zs = 1 if h == LATE_Z[0] else 2
                for i in range(zs):
                    act.wait_ge(S("z_scaled"), 2 * h + i + 1)
                    ch.mark(act.activation(mv[:, 2 * i:2 * i + 2, :], mv[:, 2 * i:2 * i + 2, :], ACT.Sigmoid))
                ch.sync()
                store(A["t_z"][h][:, 0:2 * zs, :], mv[:, 0:2 * zs, :], "z_spilled")
                if h < ML_H - 1:
                    for w, (nm_, buf) in enumerate((("q", mq), ("k", mk), ("v", mv))):
                        act.wait_ge(S("qkv_ready"), 6 * h + 2 * w + 2)
                        store(A["t_" + nm_][h], buf[:], nm_ + "_spilled")
            act.wait_ge(S("gates_done"), ML_H)
            load(causal[:], A["causal"], "cell_const")
            load(sel[:], A["sel"], "cell_const")
            act.wait_ge(S("z_spilled"), 16 * ML_H)
            load(sz[:, 0:2, :], A["t_z"][CELL_ORDER[0]][:, 0:2, :], "cell_z")
            ch.mark(act.activation(frow[:], gt[32:36, :], ACT.Copy))
            ch.sync()
            ch.mark(act.activation(erow[:], frow[:], ACT.Abs))
            ch.sync()
            ch.mark(act.activation(erow[:], erow[:], ACT.Exp, scale=-1.0))
            ch.sync()
            act.activation(erow[:], erow[:], ACT.Ln, bias=1.0).then_inc(S("log1p"), 1)
            act.wait_ge(S("rows_ready"), 1)
            act.activation(enrow[:], mrow[:], ACT.Exp, scale=-1.0)
            act.activation(sirow[:], rrow[:, SCW:SCW + TS], ACT.Exp, bias=par[0:4, PCOL["m0"][0]:PCOL["m0"][0] + 1])\
                .then_inc(S("rows_exp"), 1)
            group_ready(act, GR["acol"])
            act.wait_ge(S("rows_exp"), 1)
            act.wait_ge(S("acol_ready"), 1)
            load(C0[:], A["C0"][CELL_ORDER[0]], "cell_c")
            act.wait_ge(S("z_scaled"), 8)
            act.activation(sz[:, 2:4, :], sz[:, 2:4, :], ACT.Sigmoid).then_inc(S("late_z"), 1)
            store(A["o_m"], mo[:], "stored")
            store(A["o_conv"], cst[:], "stored")
            def gate_weights(h):
                g = GR["cell", h, "r"]
                group_ready(act, g)
                for j in range(NTB):
                    ins = act.activation(wt[:, blk(j):blk(j + 1)], bank(g, j)[:, 0:TP - P * j], ACT.Exp,
                                         bias=acol[:, 4 * j + h:4 * j + h + 1])
                group_freed(ins, g)

            gate_weights(CELL_ORDER[0])
            for n, h in enumerate(CELL_ORDER):
                g = GR["cell", h, "aux"]
                group_ready(act, g)
                act.activation(wts[:], bank(g, 0)[0:TS, 0:TS], ACT.Exp, bias=acol[0:TS, 16 + h:17 + h])
                act.activation(siB[:], bank(g, 1)[:, 0:TS], ACT.Copy)
                for b in range(2):
                    ins = act.activation(ss[:, HALF * b:HALF * b + HALF], bank(g, 2 + b)[:, 0:HALF], ACT.Copy)
                ch.mark(ins, free[g % 2], S("cell_w"))
                g = GR["cell", h, "vT"]
                group_ready(act, g)
                for j in range(NTB):
                    ins = act.activation(mvt[:, j, :], bank(g, j), ACT.Copy)
                ch.mark(ins, free[g % 2], S("cell_vt"))
                g = GR["cell", h, "kT"]
                group_ready(act, g)
                act.wait_ge(S("cell_wcol"), n + 1)
                for j in range(NTB):
                    ins = act.activation(mkt[:, j, :], bank(g, j), ACT.Copy, scale=wcol[:, j:j + 1])
                ch.mark(ins, free[g % 2], S("cell_kt"))
                if n:
                    act.wait_ge(S("cell_y"), 4 * n)
                    load(sz[:], A["t_z"][h], "cell_z")
                    load(xc[:], A["t_xc"][h], "cell_xc")
                nxt = CELL_ORDER[n + 1] if n + 1 < ML_H else None
                if nxt is not None:
                    act.wait_ge(S("cell_qs"), n + 1)
                    load(mq[:], A["t_q"][nxt], "cell_q")
                    load(mk[:], A["t_k"][nxt], "cell_k")
                    load(mv[:], A["t_v"][nxt], "cell_v")
                g = GR["cell", h, "den"]
                group_ready(act, g)
                act.activation(tm[:, 1, 0:TP], bank(g, 0), ACT.Abs)
                act.activation(tm[:, 1, TP:T], bank(g, 1)[:, 0:TS], ACT.Abs).then_inc(S("cell_abs"), 1)
                g = GR["cell", h, "kv"]
                group_ready(act, g)
                for d in range(ML_T):
                    ins = act.activation(mvt[:, d, :], bank(g, d), ACT.Copy)
                ch.mark(ins, free[g % 2])
                store(A["o_cp"][h], mvt[:], "cp_stored")
                act.wait_ge(S("cell_cs"), n + 1)
                store(A["o_cs"][h], C0[:], "cs_stored")
                act.wait_ge(S("cell_c0"), n + 1)
                for e in range(ML_T):
                    if 4 * n + e >= 2:
                        act.wait_ge(S("csq_used"), 4 * n + e - 1)
                    act.activation(tm[:, e % 2, :], sz[:, e, :], ACT.Square).then_inc(S("csq_ready"), 1)
                if nxt is not None:
                    gate_weights(nxt)
                rstd(GR["cell", h, "var"], rs)
                act.wait_ge(S("cp_stored"), 16 * (n + 1))
                act.wait_ge(S("cs_stored"), 16 * (n + 1))
                if nxt is not None:
                    load(C0[:], A["C0"][nxt], "cell_c")
            store(A["o_n"], nout[:], "stored")
            act.wait_ge(S("stored"), 16 * 6)
            attention(1)
            before_projection(5, "mlp1")
            norm_rstd(5, power=2)
            squares(6, range(DT))
            rstd(GR["final_norm"], rs)
            for i in range(4):
                act.wait_ge(S("y_ready"), i + 1)
                store(A["o_y"][:, 2 * i:2 * i + 2, :], x[:, 2 * i:2 * i + 2, :], "stored")
            act.wait_ge(S("stored"), 16 * 10)

        @block.vector
        def _(v):
            ch = Chain(v, S("dve_step"))
            tt, stt, ts = v.tensor_tensor, v.scalar_tensor_tensor, v.tensor_scalar
            MUL, ADD, SUB = ALU.mult, ALU.add, ALU.subtract

            def step(*ops):
                for o in ops:
                    ch.mark(o())
                ch.sync()

            def add_squares(i, kks):
                for kk in kks:
                    v.wait_ge(S("sq_ready"), 8 * i + kk + 1)
                    if kk == 0:
                        if i:
                            group_ready(v, GR[NORM_AT[i - 1]])
                        ins = v.tensor_copy(ss[:], tm[:, 0, :])
                    else:
                        ch.sync()
                        ins = tt(ss[:], ss[:], tm[:, kk % 2, :], ADD)
                    ch.mark(ins, S("sq_used"))
                if kk == DT - 1:
                    v.sem_inc(S("squares_ready"), 1)

            rcount = [0]

            def rstd_ready():
                rcount[0] += 1
                v.wait_ge(S("rstd_ready"), rcount[0])

            def low(i, gain, kks):
                for kk in kks:
                    v.wait_ge(S("xn_hi"), 8 * i + kk + 1)
                    stt(xnl[:, kk, :], x[:, kk, :], col(gain, kk), xnh[:, kk, :].bitcast(F32), MUL, SUB)\
                        .then_inc(S("xn_ready"), 1)

            def halves(dst, j):
                return [dst[:, j, 0:HALF], dst[:, j, HALF:T]]

            v.wait_ge(S("consts"), 1)
            v.wait_ge(S("par_loaded"), 16)
            low(0, "mix0", range(DT))
            add_squares(0, range(DT))
            v.wait_ge(S("s5_dt"), 1)
            ch.mark(tt(sp[:, 1, :], col("a_re", 0, 16), sp[:, 0, :], MUL))
            ch.mark(tt(sp[:, 6, :], col("a_im", 0, 16), sp[:, 0, :], MUL))
            ch.sync()
            ch.mark(ts(sp[:, 7, :], sp[:, 6, :], 1.0 / TWO_PI, ROUND, MUL, ADD))
            ch.sync()
            ch.mark(ts(sp[:, 7, :], sp[:, 7, :], -ROUND, None, ADD))
            for c in (PI_HI, PI_MID, PI_LO):
                ch.sync()
                ch.mark(stt(sp[:, 6, :], sp[:, 7, :], -c, sp[:, 6, :], MUL, ADD))
            ch.sync()
            LIM = 3.1415925
            ts(sp[:, 2, :], sp[:, 6, :], LIM, -LIM, ALU.min, ALU.max).then_inc(S("s5_arg"), 1)

            RS = (rs[:, 0:HALF], rs[:, HALF:T])

            def evac_u(i):
                g = GR["rs", "u", i]
                group_ready(v, g)
                for m in range(2):
                    for b in range(2):
                        ins = tt(halves(u, 2 * i + m)[b], bank(g, 2 * m + b)[:, 0:HALF], RS[b], MUL)
                ch.mark(ins, free[g % 2])

            def evac_rope(w, i):
                part, dst = (("q", q), ("k", k))[w]
                g = GR["rs", part, i]
                v.wait_ge(S("swap_ready"), 2 * w + i + 1)
                v.wait_ge(S("const_loaded"), 16 * 8)
                for m in range(2):
                    for b in range(2):
                        hs_ = slice(HALF * b, HALF * b + HALF)
                        ch.mark(tt(halves(dst, 2 * i + m)[b], bank(g, 2 * m + b)[:, 0:HALF], rope[:, 0, hs_], MUL))
                        ch.mark(tt(sw[:, 2 * m + b, :], sw[:, 2 * m + b, :], rope[:, 1, hs_], MUL))
                ch.sync()
                v.sem_inc(free[g % 2], 1)
                for m in range(2):
                    for b in range(2):
                        ins = tt(halves(dst, 2 * i + m)[b], halves(dst, 2 * i + m)[b], sw[:, 2 * m + b, :], ADD)
                ch.mark(ins, S("swap_used"))
                if i:
                    v.sem_inc(S("rope_done"), 1)

            rstd_ready()
            evac_u(0)
            v.wait_ge(S("rope_loaded"), 16)
            for w in range(2):
                ch.mark(tt(rope[:, w, :], rope[:, w, :], rs[:], MUL))
            v.wait_ge(S("msq_ready"), 1)
            for w in (4, 2):
                step(lambda: tt(msq[:, 0:w * MEM], msq[:, 0:w * MEM], msq[:, w * MEM:2 * w * MEM], ADD))
            step(lambda: tt(mss, msq[:, 0:MEM], msq[:, MEM:2 * MEM], ADD))
            v.sem_inc(S("mem_squares"), 1)
            evac_u(1)
            v.memset(u[:, :, T:TP + P], 0.0)
            v.wait_ge(S("s5_trig"), 1)
            R = lambda j: sp[:, j, :]
            are, aim = col("a_re", 0, 16), col("a_im", 0, 16)

            step(lambda: stt(R(6), R(5), -2.0, R(5), MUL, MUL), lambda: tt(R(7), are, are, MUL), lambda: tt(R(8), aim, aim, MUL))
            step(lambda: ts(R(6), R(6), 1.0, None, ADD), lambda: tt(R(7), R(7), R(8), ADD))
            step(lambda: tt(R(9), R(3), R(6), MUL), lambda: tt(R(10), R(3), R(4), MUL), lambda: v.reciprocal(R(7), R(7)))
            step(lambda: ts(R(8), R(9), -1.0, None, ADD))
            step(lambda: tt(R(11), R(8), are, MUL), lambda: tt(R(12), R(10), aim, MUL),
                 lambda: tt(R(13), R(10), are, MUL), lambda: tt(R(14), R(8), aim, MUL))
            step(lambda: tt(R(11), R(11), R(12), ADD), lambda: tt(R(13), R(13), R(14), SUB))
            step(lambda: tt(R(11), R(11), R(7), MUL), lambda: tt(R(13), R(13), R(7), MUL))
            v.wait_ge(S("const_loaded"), 16 * 8)
            fre = R(11).unsqueeze(2).to_broadcast([P, S5_TILES, 32])
            fim = R(13).unsqueeze(2).to_broadcast([P, S5_TILES, 32])
            zt = sq[:, 0:512].rearrange("p (s c) -> p s c", s=S5_TILES)
            step(lambda: tt(bb[:, 0], bz[:, 0], fre, MUL), lambda: tt(zt, bz[:, 1], fim, MUL))
            step(lambda: tt(bb[:, 0], bb[:, 0], zt, SUB))
            step(lambda: tt(bb[:, 1], bz[:, 1], fre, MUL), lambda: tt(zt, bz[:, 0], fim, MUL))
            step(lambda: tt(bb[:, 1], bb[:, 1], zt, ADD), lambda: ts(Cm[:, 1], Cm[:, 1], -1.0, None, MUL))
            v.sem_inc(S("bb_ready"), 1)
            evac_rope(0, 0)
            evac_rope(0, 1)
            v.wait_ge(S("mrs_ready"), 1)
            step(lambda: v.memset(ctab[:, :, 0:1], 1.0), lambda: v.memset(stab[:, :, 0:1], 0.0),
                 lambda: v.tensor_copy(R(15), R(6)), lambda: v.tensor_copy(R(16), R(4)))

            def doubling(n):
                pc = R(15).unsqueeze(2).to_broadcast([P, S5_TILES, n])
                ps_ = R(16).unsqueeze(2).to_broadcast([P, S5_TILES, n])
                c0, s0, c1, s1 = ctab[:, :, 0:n], stab[:, :, 0:n], ctab[:, :, n:2 * n], stab[:, :, n:2 * n]
                t = sw[:].rearrange("p a t -> p (a t)")[:, 0:S5_TILES * n].rearrange("p (s t) -> p s t", s=S5_TILES)
                step(lambda: tt(c1, c0, pc, MUL), lambda: tt(t, s0, ps_, MUL))
                step(lambda: tt(c1, c1, t, SUB))
                step(lambda: tt(s1, c0, ps_, MUL), lambda: tt(t, s0, pc, MUL))
                step(lambda: tt(s1, s1, t, ADD), lambda: tt(R(17), R(15), R(15), MUL), lambda: tt(R(18), R(16), R(16), MUL),
                     lambda: stt(R(19), R(15), 2.0, R(16), MUL, MUL))
                step(lambda: tt(R(15), R(17), R(18), SUB), lambda: v.tensor_copy(R(16), R(19)))

            evac_rope(1, 0)
            evac_rope(1, 1)
            for i in range(2):
                g = GR["rs", "v", i]
                group_ready(v, g)
                for t, (b, c0) in enumerate([(0, 0), (1, 0), (2, 0), (3, 0), (3, 256)]):
                    r = P if t < NTB else TS
                    ins = ts(vt[0:r, t, 256 * i:256 * i + 256], bank(g, b)[0:r, c0:c0 + 256], rsc[0:r, t:t + 1], None, MUL)
                ch.mark(ins, free[g % 2])
                if i == 0:
                    for n in (1, 2, 4, 8, 16, 32, 64):
                        doubling(n)
                    step(lambda: v.tensor_copy(mrs, mrs0))
                    v.sem_inc(S("rope_free"), 1)
            for i in range(2):
                g = GR["rs", "g", i]
                group_ready(v, g)
                for b in range(4):
                    ins = tt(halves(gt_, 2 * i + b // 2)[b % 2], bank(g, b)[:, 0:HALF], RS[b % 2], MUL)
                ch.mark(ins, free[g % 2], S("g_scaled"))
            g = GR["s5B"]
            group_ready(v, g)
            for c in range(2):
                ins = v.tensor_copy(BT[:, c].rearrange("p j s -> p (j s)"), bank(g, c))
            ch.mark(ins, free[g % 2], S("s5_const"))
            def low_memory(l):
                for kk in range(DT):
                    v.wait_ge(S("mem_hi"), 8 * l + kk + 1)
                    stt(mnl[:, kk, :], memx[:, kk, :], col(f"mem{l}", kk), mnh[:, kk, :].bitcast(F32), MUL, SUB)\
                        .then_inc(S("mem_ready"), 1)

            def memory_keys(m):
                l, w, i = m
                if w != "k":
                    return
                j, g = MEM_SLABS.index(m), GR[("mem",) + m]
                if j >= 2:
                    v.wait_ge(S(f"mkv_stored{j % 2}"), 16 * (j // 2))
                group_ready(v, g)
                for a in range(2):
                    ins = tt(mkv[j % 2][:, MEM * a:MEM * a + MEM], bank(g, 2 * a)[:, 0:MEM], mrs, MUL)
                ch.mark(ins, free[g % 2], S("mem_k"))

            low_memory(0)
            def ret_y(h):
                if h == 0:
                    v.wait_ge(S("g_silu"), 2)
                    group_ready(v, GR["rs", "g", 1])
                rstd_ready()
                step(lambda: stt(tm[:, 0, :], q[:, h, :], col("ret_gn", h), rs[:], MUL, MUL))
                step(lambda: tt(tm[:, 1, :], tm[:, 0, :], gt_[:, h, :], MUL))
                step(lambda: v.tensor_copy(xnh[:, h, :], tm[:, 1, :]))
                ch.mark(tt(xnl[:, h, :], tm[:, 1, :], xnh[:, h, :].bitcast(F32), SUB))

            for h in range(RET_H):
                g = GR["ret", h, "score"]
                group_ready(v, g)
                if h:
                    group_ready(v, GR["ret", h - 1, "out"])
                for j in range(NTB):
                    w = TP - P * j
                    ins = tt(Wm[:, blk(j):blk(j) + w], bank(g, j)[:, 0:w], dec[:, h, 0:w], MUL)
                group_freed(ins, g)
                g = GR["ret", h, "aux"]
                group_ready(v, g)
                tt(Ws[:], bank(g, 0)[0:TS, 0:TS], dec[0:TS, h, 0:TS], MUL)
                tt(qw[:], q[:, h, TP:T], wq64[:, h, :], MUL)
                for j in range(NTB):
                    at = TP - 1 - P * j
                    ts(kt[:, j, :], bank(g, 1)[:, P * j:P * j + P], dec[:, h, at:at + 1], None, MUL)
                ins = ts(kt[0:TS, NTB, :], bank(g, 2)[0:TS, 0:P], dec[0:TS, h, TS - 1:TS], None, MUL)
                ch.mark(ins, free[g % 2], S("ret_w"))
                if h:
                    ret_y(h - 1)
                memory_keys(MEM_RET[h][0])
                g = GR["ret", h, "out"]
                group_ready(v, g)
                ch.mark(v.tensor_copy(q[:, h, 0:TP], bank(g, 0)))
                ins = v.tensor_copy(q[:, h, TP:T], bank(g, 1)[:, 0:TS])
                ch.mark(ins, S("ret_o"))
                v.tensor_copy(retp[:, h, :], bank(g, 2)[:, 0:P])
                ins = stt(S0[:, h, :], S0[:, h, :], float(GAMMA[h] ** TS), bank(g, 3)[:, 0:P], MUL, ADD)
                ch.mark(ins, free[g % 2], S("ret_state"))
                memory_keys(MEM_RET[h][1])
                g = GR["ret", h, "mean"]
                group_ready(v, g)
                for b in range(2):
                    ins = tt(halves(q, h)[b], halves(q, h)[b], bank(g, b)[:, 0:HALF], SUB)
                    ch.mark(ins)
                ch.sync()
                v.sem_inc(free[g % 2], 1)
                v.sem_inc(S("ret_c"), 1)
            ret_y(RET_H - 1)
            def decay_table(w):
                z3 = rt[:, 0:S5_TILES * w].rearrange("p (s t) -> p s t", t=w)
                step(lambda: v.tensor_copy(z3, R(3).unsqueeze(2).to_broadcast([P, S5_TILES, w])))
                step(lambda: v.memset(z3[:, :, 0:1], 0.0))

            def s5_y(n):
                c, hf = UNITS[n]
                g = GR["s5y", n]
                group_ready(v, g)
                w = P if c < NTB else TS
                for a in range(2):
                    j = 2 * hf + a
                    ins = stt(u[:, j, P * c:P * c + w], u[:, j, P * c:P * c + w], col("s5_d", j), bank(g, a)[:, 0:w], MUL, ADD)
                ch.mark(ins, free[g % 2], S("s5_y"))

            def rotate_back(n):
                c, hf = UNITS[n]
                w, g = unit_width(n), GR["s5u", n]
                t8 = slice(8 * hf, 8 * hf + 8)
                cc, sc = ctab[:, t8, 0:w], stab[:, t8, 0:w]
                grp = psum[:, 4 * (g % 2):4 * (g % 2) + 4, :].rearrange("p i (c a t) -> p i c a t", c=2, a=2)
                re, im = grp[:, :, 0, :, 0:w], grp[:, :, 1, :, 0:w]
                ia = lambda z: z.rearrange("p (a i) t -> p i a t", i=4)
                group_ready(v, g)
                if n:
                    v.wait_ge(S("s5_in"), n)
                tt(ia(unit(za, n)), re, ia(cc), MUL)
                tt(ia(unit(zb, n)), im, ia(sc), MUL)
                tt(ia(unit(zc, n)), im, ia(cc), MUL)
                ins = tt(ia(unit(zd, n)), re, ia(sc), MUL)
                ch.mark(ins, free[g % 2], S("s5_back"))

            def scan_unit(n):
                c, hf = UNITS[n]
                w = unit_width(n)
                t8 = slice(8 * hf, 8 * hf + 8)
                if n == NU - 2:
                    decay_table(TS)
                v.wait_ge(S("s5_in"), n + 1)
                step(*[lambda z=z: v.tensor_tensor_scan(z[:, n % 2, 0:8 * w], rt[:, 8 * hf * w:8 * (hf + 1) * w],
                                                        z[:, n % 2, 0:8 * w], 0.0, MUL, ADD) for z in (za, zc)])

            def rotate_forward(n):
                c, hf = UNITS[n]
                w = unit_width(n)
                t8 = slice(8 * hf, 8 * hf + 8)
                cc, sc = ctab[:, t8, 0:w], stab[:, t8, 0:w]
                A_, C_, E_, F_ = (unit(z, n) for z in (za, zc, he, hf_))
                if n >= 2:
                    group_ready(v, GR["s5y", n - 2])
                if n:
                    v.wait_ge(S("s5_re"), n)
                tt(E_, A_, cc, MUL)
                ch.mark(tt(unit(ze, n), C_, sc, MUL), S("s5_fwd"))
                step(lambda: tt(F_, A_, sc, MUL), lambda: tt(C_, C_, cc, MUL))
                step(lambda: tt(F_, F_, C_, ADD))
                v.sem_inc(S("s5_im"), 1)

            def final_state(n):
                c, hf = UNITS[n]
                if c >= NTB - 1:
                    v.wait_ge(S("s5_re"), n + 1)
                    at, y = unit_width(n) - 1, 2 * (c - NTB + 1)
                    for r, z in enumerate((he, hf_)):
                        v.tensor_copy(fin5[:, y + r, 8 * hf:8 * hf + 8], unit(z, n)[:, :, at:at + 1].rearrange("p s o -> p (s o)"))

            v.wait_ge(S("stored"), 32)
            rotate_back(0)
            low_memory(1)
            decay_table(P)
            for n in range(NU):
                if n + 1 < NU:
                    rotate_back(n + 1)
                scan_unit(n)
                for m in MEM_S5[n]:
                    memory_keys(m)
                rotate_forward(n)
                if n:
                    final_state(n - 1)
                    s5_y(n - 1)
            final_state(NU - 1)
            s5_y(NU - 1)
            for j in range(4):
                v.wait_ge(S("gelu"), j + 1)
                step(lambda: v.tensor_copy(gh[:, j, :], u[:, j, 0:T]))
                tt(gl[:, j, :], u[:, j, 0:T], gh[:, j, :].bitcast(F32), SUB).then_inc(S("glu_in"), 1)
            group_ready(v, GR["mem", 1, "v", 3])
            for a in range(2):
                v.wait_ge(S("sg_ready"), a + 1)
                for m in range(2):
                    j = 2 * a + m
                    step(*[lambda b=b: tt(tm[:, m, HALF * b:HALF * b + HALF], halves(u, j)[b], sg[:, 2 * m + b, :], MUL)
                           for b in range(2)])
                    step(lambda: v.tensor_copy(xnh[:, 4 + j, :], tm[:, m, :]))
                    tt(xnl[:, 4 + j, :], tm[:, m, :], xnh[:, 4 + j, :].bitcast(F32), SUB).then_inc(S("rs_y"), 1)
                v.sem_inc(S("sg_used"), 1)

            def add_residual(g, i):
                group_ready(v, g)
                for m in range(2):
                    for b in range(2):
                        ins = tt(halves(x, 2 * i + m)[b], halves(x, 2 * i + m)[b], bank(g, 2 * m + b)[:, 0:HALF], ADD)
                    ch.mark(ins)
                ch.sync()
                v.sem_inc(free[g % 2], 1)
                v.sem_inc(S("x_tile"), 2)

            def residual_and_norm(groups, i, gain):
                for j in range(4):
                    add_residual(groups[j], j)
                    if j in (1, 2):
                        add_squares(i, (2 * j - 2, 2 * j - 1))
                    if j == 2:
                        add_squares(i, (4, 5))
                        low(i, gain, (0, 1))
                low(i, gain, range(2, 8))
                add_squares(i, (6, 7))

            v.sem_inc(S("arena_free"), 1)
            v.wait_ge(S("x_again"), 16)
            residual_and_norm([GR["rs_out", i] for i in range(4)], 1, "cross0")

            def attention(l):
                rstd_ready()
                def copy_xq(i):
                    g = GR["xq", l, i]
                    group_ready(v, g)
                    for m in range(2):
                        for b in range(2):
                            ins = tt(halves(xq, 2 * i + m)[b], bank(g, 2 * m + b)[:, 0:HALF], RS[b], MUL)
                    ch.mark(ins, free[g % 2], S("xq_ready"))

                def row_max(x2):
                    g = GR["att", l, "score", x2]
                    group_ready(v, g)
                    r = P if x2 < 2 else TS
                    for t in range(4):
                        if x2 < 2:
                            ch.mark(v.tensor_reduce(mx[:, x2, 2 * t:2 * t + 2], bank(g, t).rearrange("p (h m) -> p h m", h=2),
                                                    AX.X, ALU.max))
                        else:
                            ch.mark(v.tensor_reduce(mx[0:r, x2, t:t + 1], bank(g, t)[0:r, 0:MEM], AX.X, ALU.max))
                    w = 8 if x2 < 2 else 4
                    ch.sync()
                    ins = ts(nm[0:r, x2, 0:w], mx[0:r, x2, 0:w], -1.0 / 16, None, MUL)
                    ch.mark(ins, S("row_max"))

                def prob(x2):
                    v.wait_ge(S("exp_done"), 3 * l + ATT_ORDER.index(x2) + 1)
                    r, w = (P, 8) if x2 < 2 else (TS, 4)
                    step(lambda: v.reciprocal(sm[0:r, x2, 0:w], sm[0:r, x2, 0:w]))
                    dst = pr[:, x2] if x2 < 2 else prs
                    for j in range(w):
                        ins = ts(dst[0:r, j, :], dst[0:r, j, :], sm[0:r, x2, j:j + 1], None, MUL)
                    ch.mark(ins, S("prob"))

                def low_o(x2):
                    g = GR["att", l, "pv", x2]
                    v.wait_ge(S("o_hi"), 3 * l + ATT_ORDER.index(x2) + 1)
                    if x2 < 2:
                        for b in range(4):
                            ins = tt(xnl[:, 4 * x2 + b, 0:TP], bank(g, b), xnh[:, 4 * x2 + b, 0:TP].bitcast(F32), SUB)
                    else:
                        pb = bank(g, 0).rearrange("p (f t) -> p f t", f=DT)
                        ins = tt(xnl[:, :, TP:T], pb, xnh[:, :, TP:T].bitcast(F32), SUB)
                    ch.mark(ins, free[g % 2], S("att_o"))

                copy_xq(0)
                copy_xq(1)
                row_max(0)
                copy_xq(2)
                prob(0)
                copy_xq(3)
                row_max(2)
                row_max(1)
                prob(2)
                prob(1)
                low_o(0)
                low_o(2)
                low_o(1)
                residual_and_norm([GR["xo", l, i] for i in range(4)], 3 * l + 2, f"mlp{l}")

            def mlp(l):
                rstd_ready()
                g0 = GR["mlp", l, 0, "up", 0]

                def hidden(g, i, turn=None):
                    group_ready(v, g, turn)
                    B = [bank(g, b)[:, 0:HALF] for b in range(4)]
                    for b in range(4):
                        ch.mark(stt(hr[:, b, :], B[b], 0.0, RS[b % 2], ALU.max, MUL))
                    ch.sync()
                    for b in range(4):
                        ch.mark(stt(hs[:, b, :], B[b], 0.0, hr[:, b, :], ALU.max, MUL))
                    ch.sync()
                    v.sem_inc(free[g % 2], 1)
                    for b in range(4):
                        ch.mark(v.tensor_copy(halves(hh, 2 * i + b // 2)[b % 2], hs[:, b, :]))
                    ch.sync()
                    for b in range(4):
                        h_ = halves(hh, 2 * i + b // 2)[b % 2]
                        ins = tt(halves(hl, 2 * i + b // 2)[b % 2], hs[:, b, :], h_.bitcast(F32), SUB)
                    ins.then_inc(S("hidden_ready"), 1)

                def onto_x(g, i, turn=None):
                    group_ready(v, g, turn)
                    for m in range(2):
                        for b in range(2):
                            xx = halves(x, 2 * i + m)[b]
                            ins = tt(xx, xx, bank(g, 2 * m + b)[:, 0:HALF], ADD)
                    ch.mark(ins)
                    ch.sync()
                    v.sem_inc(free[g % 2], 1)
                    v.sem_inc(S("x_mlp"), 2)

                with v.Fori(0, 3) as a:
                    ch.loop(a, 4 * 12 + 4)
                    for i in range(4):
                        hidden(g0 + i, i, a * 4)
                    for i in range(4):
                        onto_x(g0 + 4 + i, i, a * 4)
                    ch.endloop(3)
                for i in range(4):
                    hidden(g0 + 24 + i, i)
                for i in range(4):
                    onto_x(g0 + 28 + i, i)
                    if l == 0:
                        low(3, "mix1", (2 * i, 2 * i + 1))
                    add_squares(3 * l + 3, (2 * i, 2 * i + 1))

            attention(0)
            mlp(0)
            rstd_ready()
            SEG = ((0, HALF, 0, 3, 0), (1, TP - HALF, 0, HALF + 3, HALF), (1, TS, TP - HALF, TP + 6, TP))
            v.memset(xm[:, :, 0:3], 0.0)
            for h in range(ML_H):
                for i in range(2):
                    g = GR["ml", h, "xm", i]
                    group_ready(v, g)
                    for m in range(2):
                        for b, w, c0, c1, t0 in SEG:
                            ins = tt(xm[:, 2 * i + m, c1:c1 + w], bank(g, 2 * m + b)[:, c0:c0 + w], rs[:, t0:t0 + w], MUL)
                    ch.mark(ins, free[g % 2], S("xm_ready"))

                def low_xc(t):
                    v.wait_ge(S("xc_hi"), 4 * h + t + 1)
                    tt(xcl[:, t, :], xc[:, t, :], xch[:, t, :].bitcast(F32), SUB).then_inc(S("xc_split"), 1)

                def scale_z(i):
                    g = GR["ml", h, "z", i]
                    group_ready(v, g)
                    for b in range(4):
                        dst = sz if (h, "z", i) == LATE_Z else mv
                        ins = tt(halves(dst, 2 * i + b // 2)[b % 2], bank(g, b)[:, 0:HALF], RS[b % 2], MUL)
                    ch.mark(ins, free[g % 2], S("z_scaled"))

                a, _ = PCOL["conv_cache"]
                cc = par[:, a + 12 * h:a + 12 * h + 12].rearrange("p (t k) -> p t k", k=3)
                ch.mark(v.tensor_copy(xm[:, :, TP + 3:TP + 6], cc))
                v.tensor_copy(cst[:, 0, 4 * h:4 * h + 4, :], xm[:, :, TP:TP + 3])
                v.tensor_copy(cst[:, 1, 4 * h:4 * h + 4, :], xm[:, :, T + 3:T + 6])
                ch.sync()
                if h:
                    v.wait_ge(S("xc_spilled"), 16 * h)
                    v.wait_ge(S("xc_split"), 4 * h)
                for t in range(ML_T):
                    for tap in range(4):
                        for d0, s0, w in ((0, 0, TP), (TP, TP + 3, TS)):
                            src, dst = xm[:, t, s0 + tap:s0 + tap + w], xc[:, t, d0:d0 + w]
                            wc = col("conv_w", 16 * h + 4 * t + tap)
                            if tap == 0:
                                ins = ts(dst, src, wc, col("conv_b", 4 * h + t), MUL, ADD)
                            else:
                                ins = stt(dst, src, wc, dst, MUL, ADD)
                            ch.mark(ins)
                        ch.sync()
                    v.sem_inc(S("conv_done"), 1)
                    if t:
                        low_xc(t - 1)
                low_xc(ML_T - 1)
                if h:
                    v.wait_ge(S("v_spilled"), 16 * h)
                scale_z(0)
                v.wait_ge(S("xm_hi"), h + 1)
                tt(xml[:, :, 0:TP], xm[:, :, 3:3 + TP], xmh[:, :, 0:TP].bitcast(F32), SUB)
                tt(xml[:, :, TP:T], xm[:, :, TP + 6:T + 6], xmh[:, :, TP:T].bitcast(F32), SUB).then_inc(S("xm_split"), 1)
                if (h, "z", 1) != LATE_Z:
                    scale_z(1)
                for w, (part, buf) in enumerate((("q", mq), ("k", mk), ("v", mv))):
                    if w == 2:
                        v.wait_ge(S("z_spilled"), 16 * (h + 1))
                    elif h:
                        v.wait_ge(S(part + "_spilled"), 16 * h)
                        group_ready(v, GR["gate", h - 1])
                    for i in range(2):
                        g = GR["ml", h, part, i]
                        group_ready(v, g)
                        for b in range(4):
                            ins = v.tensor_copy(halves(buf, 2 * i + b // 2)[b % 2], bank(g, b)[:, 0:HALF])
                        ch.mark(ins, free[g % 2], S("qkv_ready"))
                g = GR["gate", h]
                group_ready(v, g)
                for b in range(2):
                    c = slice(HALF * b, HALF * b + HALF)
                    if h == 0:
                        ins = ts(gt[:, c], bank(g, b)[0:36, 0:HALF], par[0:36, PCOL["b_gates"][0]:PCOL["b_gates"][0] + 1], None, ADD)
                    else:
                        ins = tt(gt[:, c], gt[:, c], bank(g, b)[0:36, 0:HALF], ADD)
                    ch.mark(ins)
                ch.sync()
                v.sem_inc(free[g % 2], 1)
                v.sem_inc(S("gates_done"), 1)
            ig = gt[0:4, :]
            step(lambda: v.memset(zrow[:], 0.0))
            v.wait_ge(S("log1p"), 1)
            step(lambda: stt(lrow[:], frow[:], 0.0, erow[:], ALU.min, SUB))
            scan = v.tensor_tensor_scan
            m0c = par[0:4, PCOL["m0"][0]:PCOL["m0"][0] + 1]
            step(lambda: scan(mrow[:, 0:TP], lrow[:, 0:TP], ig[:, 0:TP], 0.0, ADD, ALU.max),
                 lambda: scan(mrow[:, TP:T], lrow[:, TP:T], ig[:, TP:T], m0c, ADD, ALU.max),
                 *[lambda j=j: scan(brow[:, blk(j):blk(j + 1)], lrow[:, P * j:TP], zrow[:, P * j:TP], 0.0, ADD, ADD)
                   for j in range(NTB)],
                 lambda: scan(brow[:, SCW:SCW + TS], lrow[:, TP:T], zrow[:, 0:TS], 0.0, ADD, ADD))
            for j in range(NTB):
                ch.mark(tt(rrow[:, blk(j):blk(j + 1)], brow[:, blk(j):blk(j + 1)], mrow[:, P * j:TP], SUB))
                ch.mark(tt(arow[:, j, :], ig[:, P * j:P * j + P], brow[:, blk(j):blk(j) + P], SUB))
            ch.mark(tt(rrow[:, SCW:SCW + TS], brow[:, SCW:SCW + TS], mrow[:, TP:T], SUB))
            ch.mark(tt(arow[:, NTB, 0:TS], ig[:, TP:T], brow[:, SCW:SCW + TS], SUB))
            ch.mark(v.tensor_copy(mo[:, 0:1], mrow[:, TP - 1:TP]))
            ch.mark(v.tensor_copy(mo[:, 1:2], mrow[:, T - 1:T]))
            ch.sync()
            v.sem_inc(S("rows_ready"), 1)
            scale_z(1)
            g = GR["acol"]
            group_ready(v, g)
            ch.mark(v.tensor_copy(acol[:, 0:16], bank(g, 0)[:, 0:16]))
            ch.mark(v.tensor_copy(acol[0:TS, 16:20], bank(g, 0)[0:TS, 16:20]))
            ch.sync()
            v.sem_inc(free[g % 2], 1)
            v.sem_inc(S("acol_ready"), 1)
            for x_ in ("cell_q", "cell_k", "cell_v", "cell_xc"):
                v.sem_inc(S(x_), 1)
            SC = float(ML_DH) ** -0.5
            for n, h in enumerate(CELL_ORDER):
                v.wait_ge(S("cell_w"), n + 1)
                if n:
                    group_ready(v, GR["cell", CELL_ORDER[n - 1], "n"])
                    v.wait_ge(S("cell_q"), 16 * n + 1)
                else:
                    v.wait_ge(S("rows_exp"), 1)
                for j in range(NTB):
                    at = blk(j + 1) - 1
                    ch.mark(ts(wcol[:, j:j + 1], wt[:, at:at + 1], SC, None, MUL))
                ch.mark(ts(wcol[0:TS, 4:5], wts[:, TS - 1:TS], SC, None, MUL))
                ch.sync()
                v.sem_inc(S("cell_wcol"), 1)
                g = GR["cell", h, "score"]
                group_ready(v, g)
                for j in range(NTB):
                    seg = wt[:, blk(j):blk(j + 1)]
                    ins = stt(seg, bank(g, j)[:, 0:TP - P * j], SC, seg, MUL, MUL)
                ch.mark(ins, free[g % 2], S("cell_pt"))
                for d in range(ML_T):
                    ts(n0b[:, d, :], ones[:], col("n0", 4 * h + d), None, MUL)
                g = GR["cell", h, "smp"]
                group_ready(v, g)
                ins = tt(qs[:], mq[:, :, TP:T], siB[:].unsqueeze(1).to_broadcast([P, ML_T, TS]), MUL)
                ch.mark(ins, S("cell_qs"))
                stt(wts[:], bank(g, 0)[0:TS, 0:TS], SC, wts[:], MUL, MUL)
                v.tensor_copy(vt5[:], bank(g, 1)[0:TS, :])
                ins = ts(kt5[:], bank(g, 2)[0:TS, :], wcol[0:TS, 4:5], None, MUL)
                ch.mark(ins, free[g % 2], S("cell_smp"))
                if h == 1:
                    add_residual(GR["ml_out", 1, 0], 0)
                v.wait_ge(S("cell_abs"), n + 1)
                step(lambda: tt(tm[:, 1, :], tm[:, 1, :], ss[:], ALU.max))
                step(lambda: v.reciprocal(tm[:, 1, :], tm[:, 1, :]))
                v.wait_ge(S("cell_z"), 16 * (n + 1))
                if n == 0:
                    v.wait_ge(S("late_z"), 1)
                step(lambda: tt(sz[:], sz[:], tm[:, 1, :].unsqueeze(1).to_broadcast([P, ML_T, T]), MUL))
                g = GR["cell", h, "den"]
                ins = tt(sz[:, :, TP:T], sz[:, :, TP:T], bank(g, 2)[:, 0:ML_T * TS].rearrange("p (e t) -> p e t", e=ML_T), MUL)
                ch.mark(ins, free[g % 2])
                if h == 1:
                    add_residual(GR["ml_out", 1, 1], 1)
                g = GR["cell", h, "num"]
                group_ready(v, g)
                for e in range(ML_T):
                    ins = tt(sz[:, e, 0:TP], sz[:, e, 0:TP], bank(g, e), MUL)
                ch.mark(ins, free[g % 2])
                step(lambda: tt(ss[:], sz[:, 0, :], sz[:, 1, :], ADD))
                step(lambda: tt(ss[:], ss[:], sz[:, 2, :], ADD))
                step(lambda: tt(ss[:], ss[:], sz[:, 3, :], ADD))
                v.sem_inc(S("cell_sum"), 1)
                g = GR["cell", h, "kvs"]
                group_ready(v, g)
                for d in range(ML_T):
                    ins = stt(C0[:, d, :], C0[:, d, :], siB[:, TS - 1:TS], bank(g, d), MUL, ADD)
                ch.mark(ins, free[g % 2], S("cell_cs"))
                if h == 1:
                    add_residual(GR["ml_out", 1, 2], 2)
                g = GR["cell", h, "n"]
                group_ready(v, g)
                v.tensor_copy(nout[:, 0, 4 * h:4 * h + 4], bank(g, 0)[:, 0:4])
                ins = stt(nout[:, 1, 4 * h:4 * h + 4], col("n0", 4 * h, 4), siB[:, TS - 1:TS], bank(g, 0)[:, 4:8], MUL, ADD)
                ch.mark(ins, free[g % 2])
                if h == 1:
                    add_residual(GR["ml_out", 1, 3], 3)
                g = GR["cell", h, "mean"]
                group_ready(v, g)
                for b, (t0, t1) in enumerate(((0, HALF), (HALF, T))):
                    ins = tt(sz[:, :, t0:t1], sz[:, :, t0:t1], bank(g, b)[:, 0:HALF].unsqueeze(1).to_broadcast([P, ML_T, HALF]), SUB)
                    ch.mark(ins)
                ch.sync()
                v.sem_inc(free[g % 2], 1)
                v.sem_inc(S("cell_c0"), 1)
                for e in range(ML_T):
                    v.wait_ge(S("csq_ready"), 4 * n + e + 1)
                    if e == 0:
                        ins = v.tensor_copy(ss[:], tm[:, 0, :])
                    else:
                        ins = tt(ss[:], ss[:], tm[:, e % 2, :], ADD)
                    ch.mark(ins, S("csq_used"))
                v.sem_inc(S("cell_sum"), 1)
                rstd_ready()
                if n == 2:
                    group_ready(v, GR["ml_out", 1, 3])
                v.wait_ge(S("cell_xc"), 16 * n + 1)
                for e in range(ML_T):
                    f, o = 4 * h + e, 4 * (h % 2) + e
                    step(lambda: stt(tm[:, 0, :], sz[:, e, :], col("ml_gn", f), rs[:], MUL, MUL))
                    step(lambda: stt(tm[:, 1, :], xc[:, e, :], col("ml_skip", f), tm[:, 0, :], MUL, ADD))
                    step(lambda: v.tensor_copy(xnh[:, o, :], tm[:, 1, :]))
                    step(lambda: tt(xnl[:, o, :], tm[:, 1, :], xnh[:, o, :].bitcast(F32), SUB))
                    v.sem_inc(S("cell_y"), 1)
            v.sem_inc(S("arena_free"), 1)
            residual_and_norm([GR["ml_out", 0, i] for i in range(4)], 4, "cross1")
            attention(1)
            mlp(1)
            rstd_ready()
            for kk in range(DT):
                ch.mark(stt(x[:, kk, :], x[:, kk, :], col("final", kk), rs[:], MUL, MUL))
                if kk % 2 == 1:
                    ch.sync()
                    v.sem_inc(S("y_ready"), 1)


INPUTS = {
    "w": [NSLAB, P, SLAB], "xT": [P, DT, T], "memT": [P, DT, MEM], "par": [P, NPAR], "rope": [P, 2, T],
    "decay": [P, RET_H, TP], "wq64": [P, RET_H, TS], "ident": [P, P], "ret0": [P, RET_H, P],
    "Bre": [P, S5_TILES, 32], "Bim": [P, S5_TILES, 32], "Cre": [P, S5_TILES, 32], "Cim": [P, S5_TILES, 32],
    "ckT": [2, P, DT, MEM], "cv": [2, P, 2, D],
    "gw": [P, 48, 36], "causal": [P, P], "sel": [4, ML_H, P], "C0": [ML_H, P, ML_T, ML_DH],
}
OUTPUTS = {
    "o_y": [P, DT, T], "o_retp": [P, RET_H, P], "o_rets": [P, RET_H, P], "o_s5": [P, 4, S5_TILES],
    "o_mkT": [2, P, DT, MEM], "o_mv": [2, P, 2, D],
    "o_cp": [ML_H, P, ML_T, ML_DH], "o_cs": [ML_H, P, ML_T, ML_DH], "o_n": [P, 2, 16], "o_m": [4, 2],
    "o_conv": [P, 2, 16, 3],
}
SCRATCH = {"t_q": [ML_H, P, ML_T, T], "t_k": [ML_H, P, ML_T, T], "t_v": [ML_H, P, ML_T, T], "t_xc": [ML_H, P, ML_T, T],
           "t_z": [ML_H, P, ML_T, T]}


def tiles(a):
    return np.ascontiguousarray(a.reshape(-1, P, a.shape[-1]).transpose(1, 0, 2))


def pack_weights(i):
    w = np.zeros((NSLAB, P, SLAB), np.float32)

    def slab(m, kg, cg, kts=DT, cols=256):
        b = m[kg * kts * P:(kg + 1) * kts * P, cg * cols:(cg + 1) * cols]
        return b.reshape(kts, P, cols).transpose(1, 0, 2).reshape(P, -1)

    at = {"q": 0, "k": 512, "v": 1024, "g": 1536, "u": 2048}
    for name, n in SLABS.items():
        if name[0] == "rs":
            m = i["rs_w_in"][0][:, at[name[1]]:at[name[1]] + 512]
            w[n] = slab(m, 0, name[2])
        elif name[0] == "mem":
            w[n] = slab(i["x_wk" if name[2] == "k" else "x_wv"][name[1]], 0, name[3])
        elif name == "glu":
            w[n] = slab(i["s5_w_glu"][0], 0, 0, 4, 512)
        elif name[0] == "rs_out":
            w[n] = slab(i["rs_w_out"][0], 0, name[1])
        elif name[0] in ("xq", "xo"):
            w[n] = slab(i["x_w" + name[0][1]][name[1]], 0, name[2])
        elif name[0] == "mlp":
            _, l, a, d, c = name
            w[n] = slab(i["mlp_w_up"][l], 0, 4 * a + c) if d == "up" else slab(i["mlp_w_down"][l], a, c)
        elif name[0] == "ml" and name[2] in ("xm", "z"):
            _, h, part, c = name
            w[n] = slab(i["ml_w_in"][0], 0, (8 if part == "z" else 0) + 2 * h + c)
        elif name[0] == "ml":
            w[n] = slab(i["ml_w" + name[2]][0][name[1]], 0, 0, 4, 512)
        elif name[0] == "ml_out":
            w[n] = slab(i["ml_w_out"][0], name[1], name[2])
    return w


def layout(i):
    i = {k: np.asarray(v) for k, v in i.items()}
    f = np.float32
    par = np.zeros((P, NPAR), f)

    def put(name, a):
        c, n = PCOL[name]
        par[:a.shape[0], c:c + n] = a.reshape(a.shape[0], n)

    vec = lambda a: a.reshape(-1, P).T
    for l in range(2):
        put(f"mix{l}", vec(i["norm_mix"][l]))
        put(f"cross{l}", vec(i["norm_cross"][l]))
        put(f"mlp{l}", vec(i["norm_mlp"][l]))
        put(f"mem{l}", vec(i["norm_mem"][l]))
    put("final", vec(i["norm_final"]))
    put("ret_gn", vec(i["ret_gn"][0]))
    put("s5_d", vec(i["s5_d"][0]))
    put("b_glu", vec(i["s5_b_glu"][0]))
    put("conv_w", i["ml_conv_w"][0].reshape(4, 16, P).transpose(2, 1, 0))
    put("conv_b", vec(i["ml_conv_b"][0]))
    put("ml_gn", vec(i["ml_gn"][0]))
    put("ml_skip", vec(i["ml_skip"][0]))
    put("a_re", i["s5_a_re"][0].reshape(16, P).T)
    put("a_im", i["s5_a_im"][0].reshape(16, P).T)
    put("log_dt", np.repeat(i["s5_log_dt"][0], 64).reshape(16, P).T)
    put("h0_re", i["state_s5_re"][0, 0].reshape(16, P).T)
    put("h0_im", i["state_s5_im"][0, 0].reshape(16, P).T)
    bg = np.zeros((36, 1), f)
    bg[0:4, 0], bg[32:36, 0] = i["ml_b_gates"][0][0:4], i["ml_b_gates"][0][4:8]
    put("b_gates", bg)
    put("m0", i["state_mlstm_m"][0, 0].reshape(4, 1))
    put("n0", i["state_mlstm_n"][0, 0].reshape(16, P).T)
    put("conv_cache", i["cache_mlstm_conv"][0, 0].reshape(3, 16, P).transpose(2, 1, 0))
    pos = np.concatenate([np.arange(TP), PAST + np.arange(TS)]).astype(f)
    inv = f(10000.0) ** (-np.arange(64, dtype=f) / f(64))
    ang = (pos[:, None] * inv[None, :]).astype(f).T
    cos, sin = np.cos(ang).astype(f), np.sin(ang).astype(f)
    rope = np.stack([np.concatenate([cos, cos]), np.concatenate([-sin, sin])], 1)
    lg = np.log1p(-np.exp2(-5.0 - np.arange(4)))
    d = np.arange(TP)[None, :] - np.arange(P)[:, None]
    decay = np.stack([np.where(d >= 0, np.exp(np.maximum(d, 0) * lg[h]) * P ** -0.5, 0) for h in range(4)], 1).astype(f)
    wq64 = np.broadcast_to(np.exp((np.arange(TS) + 1.0)[None, :] * lg[:, None]).astype(f), (P, 4, TS))

    def block_diag(a):
        z = np.zeros((16, 2, 64, 2, 16), f)
        a = a.reshape(16, 2, 64, 16)
        z[:, 0, :, 0], z[:, 1, :, 1] = a[:, 0], a[:, 1]
        return z.reshape(16, P, 32).transpose(1, 0, 2)

    gw = np.zeros((48, P, 36), f)
    g = i["ml_w_gates"][0].reshape(48, P, 8)
    gw[:, :, 0:4], gw[:, :, 32:36] = g[:, :, 0:4], g[:, :, 4:8]
    sel = np.zeros((4, 4, P), f)
    for h in range(4):
        sel[h, h] = 1
    out = {
        "w": pack_weights(i),
        "xT": tiles(np.concatenate([i["x_prompt"][0], i["x_sample"][0]]).T),
        "memT": tiles(i["mem_prompt"][0].T), "par": par, "rope": rope, "decay": decay, "wq64": wq64,
        "ident": np.eye(P, dtype=f), "ret0": i["state_ret"][0, 0].transpose(1, 0, 2),
        "Bre": block_diag(i["s5_b_re"][0]), "Bim": block_diag(i["s5_b_im"][0]),
        "Cre": block_diag(i["s5_c_re"][0].transpose(0, 2, 1)), "Cim": block_diag(i["s5_c_im"][0].transpose(0, 2, 1)),
        "ckT": np.stack([tiles(i["cache_mem_k"][l, 0].reshape(MEM, D).T) for l in range(2)]),
        "cv": np.stack([i["cache_mem_v"][l, 0].reshape(2, P, D).transpose(1, 0, 2) for l in range(2)]),
        "gw": gw.transpose(1, 0, 2), "causal": np.where(np.arange(P)[:, None] <= np.arange(P)[None, :], 0, NEG).astype(f),
        "sel": sel, "C0": i["state_mlstm_c"][0, 0].reshape(4, 4, P, 512).transpose(0, 2, 1, 3),
    }
    return {"in_" + k: np.ascontiguousarray(v) for k, v in out.items()}


def returned(r):
    y = r["o_y"].transpose(1, 0, 2).reshape(D, T).T
    s5 = r["o_s5"].transpose(1, 2, 0).reshape(4, 1, 1, 32, 64)
    ret = [r[n].transpose(1, 0, 2)[None, None] for n in ("o_retp", "o_rets")]
    mk = r["o_mkT"].transpose(0, 2, 1, 3).reshape(2, D, MEM).transpose(0, 2, 1).reshape(2, 1, MEM, 4, 256)
    mv = r["o_mv"].transpose(0, 2, 1, 3).reshape(2, 1, MEM, 4, 256)
    mc = [r[n].transpose(0, 2, 1, 3).reshape(1, 1, 4, 512, 512) for n in ("o_cp", "o_cs")]
    mn = r["o_n"].transpose(1, 2, 0).reshape(2, 1, 1, 4, 512)
    mm = r["o_m"].T.reshape(2, 1, 1, 4)
    cv = r["o_conv"].transpose(1, 3, 2, 0).reshape(2, 1, 1, 3, 2048)
    c = np.ascontiguousarray
    return tuple(c(a) for a in (y[None, :TP], y[None, TP:], ret[0], s5[0], s5[1], mc[0], mn[0], mm[0], cv[0], mk, mv,
                                ret[1], s5[2], s5[3], mc[1], mn[1], mm[1], cv[1]))


def kernel(**inputs):
    import concourse.bacc as bacc
    from concourse.bass_utils import run_bass_kernel_spmd as run

    nc = bacc.Bacc("TRN2", target_bir_lowering=False, num_devices=1)
    A = {}
    for n, sh in INPUTS.items():
        A[n] = nc.dram_tensor("in_" + n, sh, F32, kind="ExternalInput").ap()
    for n, sh in OUTPUTS.items():
        A[n] = nc.dram_tensor(n, sh, F32, kind="ExternalOutput").ap()
    for n, sh in SCRATCH.items():
        A[n] = nc.dram_tensor(n, sh, F32, kind="Internal").ap()
    program(nc, A)
    r = run(nc, [layout(inputs)], core_ids=[0])
    return returned(r.results[0])
```
